# Optimizing a Trainium2 kernel written in Bass

```python
import jax, jax.numpy as jnp
from jax import lax
import numpy as np

D_MODEL = 1024
BATCH = 1
SEQ = 256
DEPTH = 2

MEM_LEN = 256
MIX_WIDTH = D_MODEL
HG_WIDTH = MIX_WIDTH // 2
HG_HEADS = 4
HG_DK = HG_WIDTH // HG_HEADS
HG_DV = HG_WIDTH // HG_HEADS
HG_CHUNK = 64
ATT_WIDTH = MIX_WIDTH - HG_WIDTH
ATT_HEADS = 8
ATT_DH = ATT_WIDTH // ATT_HEADS
DILATED_PATTERNS = ((128, 1), (512, 4), (2048, 16))
ROPE_THETA = 10000.0
X_HEADS = 4
X_DH = D_MODEL // X_HEADS
N_GROUPS = 4
EXPERTS_PER_GROUP = 4
N_EXPERTS = N_GROUPS * EXPERTS_PER_GROUP
TOP_K_IN_GROUP = 2
EXPERT_FF = 512
NORM_EPS = 1e-6
IN_PROJ_WIDTH = 4 * HG_WIDTH + 3 * ATT_WIDTH
IN_SPLITS = (HG_WIDTH, 2 * HG_WIDTH, 3 * HG_WIDTH, 4 * HG_WIDTH,
             4 * HG_WIDTH + ATT_WIDTH, 4 * HG_WIDTH + 2 * ATT_WIDTH)

kernel_name = 'hybrid_hgrn2_dilated_attn_hmoe'

F32 = jnp.float32

def rms_norm(x, g):
    xf = x.astype(F32)
    y = xf * lax.rsqrt(jnp.mean(xf * xf, axis=-1, keepdims=True) + NORM_EPS)
    return (y * g.astype(F32)).astype(x.dtype)

def rope(t, positions):
    dh = t.shape[-1]
    inv = ROPE_THETA ** (-jnp.arange(0, dh, 2, dtype=F32) / dh)
    ang = positions.astype(F32)[:, None, :, None] * inv
    cos, sin = jnp.cos(ang), jnp.sin(ang)
    t1, t2 = jnp.split(t, 2, axis=-1)
    return jnp.concatenate([t1 * cos - t2 * sin, t2 * cos + t1 * sin], axis=-1)

def chunked_gated_recurrence(q, k, v, logf):
    B, H, S, dk = q.shape
    dv = v.shape[-1]
    nc = S // HG_CHUNK

    def chunks(t):
        return t.reshape(B, H, nc, HG_CHUNK, t.shape[-1]).transpose(2, 0, 1, 3, 4)

    causal = jnp.tril(jnp.ones((HG_CHUNK, HG_CHUNK), dtype=bool))

    def step(state, xs):
        qc, kc, vc, gc = xs
        b = jnp.cumsum(gc, axis=-2)
        diff = b[:, :, :, None, :] - b[:, :, None, :, :]
        decay = jnp.exp(jnp.where(causal[:, :, None], diff, -jnp.inf))
        scores = jnp.einsum('bhtk,bhsk,bhtsk->bhts', qc, kc, decay)
        o = (jnp.einsum('bhts,bhsv->bhtv', scores, vc)
             + jnp.einsum('bhtk,bhkv->bhtv', qc * jnp.exp(b), state))
        b_last = b[:, :, -1:, :]
        state = (jnp.exp(b_last)[:, :, 0, :, None] * state
                 + jnp.einsum('bhsk,bhsv->bhkv', kc * jnp.exp(b_last - b), vc))
        return state, o

    state0 = jnp.zeros((B, H, dk, dv), F32)
    _, outs = lax.scan(step, state0, (chunks(q), chunks(k), chunks(v), chunks(logf)))
    return outs.transpose(1, 2, 0, 3, 4).reshape(B, H, S, dv)

def hgrn2_mixer(q, f_logit, i, g, lb, out_gain):
    B, S, _ = q.shape

    def heads(t):
        return t.reshape(B, S, HG_HEADS, -1).transpose(0, 2, 1, 3).astype(F32)

    qh, zf, ih = heads(q), heads(f_logit), heads(i)
    lbh = lb.astype(F32).reshape(HG_HEADS, 1, HG_DK)
    f = lbh + (1.0 - lbh) * jax.nn.sigmoid(zf)
    o = chunked_gated_recurrence(qh, 1.0 - f, ih, jnp.log(f))
    o = o * lax.rsqrt(jnp.mean(o * o, axis=-1, keepdims=True) + NORM_EPS)
    o = o * out_gain.astype(F32).reshape(HG_HEADS, 1, HG_DV)
    o = o.transpose(0, 2, 1, 3).reshape(B, S, HG_WIDTH)
    return (o * jax.nn.silu(g.astype(F32))).astype(q.dtype)

def dilated_branch(q, k, v, dilation, n_back):
    B, H, S, dh = q.shape
    L = S // dilation
    blk = n_back
    nb = -(-L // blk)
    pad = nb * blk - L

    def to_blocks(t):
        t = t.reshape(B, H, L, dilation, dh).transpose(0, 1, 3, 2, 4)
        t = jnp.pad(t, ((0, 0), (0, 0), (0, 0), (0, pad), (0, 0)))
        return t.reshape(B, H, dilation, nb, blk, dh)

    def with_prev(t):
        prev = jnp.pad(t, ((0, 0), (0, 0), (0, 0), (1, 0), (0, 0), (0, 0)))[:, :, :, :-1]
        return jnp.concatenate([prev, t], axis=-2)

    qb = to_blocks(q)
    kk, vv = with_prev(to_blocks(k)), with_prev(to_blocks(v))
    s = jnp.einsum('bhrnqd,bhrnkd->bhrnqk', qb, kk)
    qi = jnp.arange(blk)[:, None]
    kj = jnp.arange(2 * blk)[None, :]
    dist = qi + blk - kj
    band = (dist >= 0) & (dist <= n_back)
    valid = band[None] & ((jnp.arange(nb)[:, None, None] > 0) | (kj[None] >= blk))
    s = jnp.where(valid, s, -jnp.inf)
    m = jnp.max(s, axis=-1)
    p = jnp.exp(s - m[..., None])
    den = jnp.sum(p, axis=-1)
    o = jnp.einsum('bhrnqk,bhrnkd->bhrnqd', p, vv) / den[..., None]

    def from_blocks(t):
        c = t.shape[-1]
        t = t.reshape(B, H, dilation, nb * blk, c)[:, :, :, :L]
        return t.transpose(0, 1, 3, 2, 4).reshape(B, H, S, c)

    return from_blocks(o), from_blocks(m[..., None])[..., 0], from_blocks(den[..., None])[..., 0]

def dilated_attention_mixer(q, k, v, positions):
    B, S, _ = q.shape

    def heads(t):
        return t.reshape(B, S, ATT_HEADS, ATT_DH).transpose(0, 2, 1, 3).astype(F32)

    qh = rope(heads(q), positions) * (ATT_DH ** -0.5)
    kh = rope(heads(k), positions)
    vh = heads(v)
    outs, ms, dens = [], [], []
    for window, dilation in DILATED_PATTERNS:
        o, m, d = dilated_branch(qh, kh, vh, dilation, window // dilation)
        outs.append(o)
        ms.append(m)
        dens.append(d)
    outs, ms, dens = jnp.stack(outs), jnp.stack(ms), jnp.stack(dens)
    wts = dens * jnp.exp(ms - jnp.max(ms, axis=0, keepdims=True))
    wts = wts / jnp.sum(wts, axis=0, keepdims=True)
    o = jnp.sum(wts[..., None] * outs, axis=0)
    return o.transpose(0, 2, 1, 3).reshape(B, S, ATT_WIDTH).astype(q.dtype)

def memory_cross_attention(h, mem_n, wq, wkv, wo):
    B, S, D = h.shape
    q = (h @ wq).reshape(B, S, X_HEADS, X_DH)
    k, v = jnp.split(mem_n @ wkv, 2, axis=-1)
    k = k.reshape(B, MEM_LEN, X_HEADS, X_DH)
    v = v.reshape(B, MEM_LEN, X_HEADS, X_DH)
    s = jnp.einsum('bshd,bmhd->bhsm', q, k).astype(F32) * (X_DH ** -0.5)
    p = jax.nn.softmax(s, axis=-1)
    o = jnp.einsum('bhsm,bmhd->bshd', p, v.astype(F32)).reshape(B, S, D)
    return o.astype(h.dtype) @ wo

def hierarchical_moe(h, w_rg, w_re, w_gate, w_up, w_down):
    B, S, D = h.shape
    t = h.reshape(-1, D)
    g_logits = (t @ w_rg).astype(F32)
    g_prob = jax.nn.softmax(g_logits, axis=-1)
    g_sel = jnp.argmax(g_logits, axis=-1)
    g_onehot = jax.nn.one_hot(g_sel, N_GROUPS, dtype=F32)
    g_w = jnp.sum(g_prob * g_onehot, axis=-1, keepdims=True)
    e_logits = (t @ w_re).astype(F32).reshape(-1, N_GROUPS, EXPERTS_PER_GROUP)
    e_in = jnp.einsum('nge,ng->ne', e_logits, g_onehot)
    top_v, top_i = lax.top_k(e_in, TOP_K_IN_GROUP)
    e_w = jax.nn.softmax(top_v, axis=-1) * g_w
    ids = g_sel[:, None] * EXPERTS_PER_GROUP + top_i
    gates = jnp.einsum('nk,nke->ne', e_w, jax.nn.one_hot(ids, N_EXPERTS, dtype=F32))
    hg = jnp.einsum('nd,edf->nef', t, w_gate)
    hu = jnp.einsum('nd,edf->nef', t, w_up)
    act = (jax.nn.silu(hg.astype(F32)) * hu.astype(F32) * gates[..., None]).astype(t.dtype)
    y = jnp.einsum('nef,efd->nd', act, w_down)
    return y.reshape(B, S, D).astype(h.dtype)

def setup_inputs(seed: int = 0) -> dict:
    key = jax.random.key(seed)
    ks = jax.random.split(key, 24)

    def w(k, shape, fan_in):
        return jax.random.normal(k, shape, F32) * (fan_in ** -0.5)

    def gain(k, shape):
        return 1.0 + 0.02 * jax.random.normal(k, shape, F32)

    return {
        'x': jax.random.normal(ks[0], (BATCH, SEQ, D_MODEL), F32),
        'mem': jax.random.normal(ks[1], (BATCH, MEM_LEN, D_MODEL), F32),
        'positions': (jnp.arange(SEQ, dtype=jnp.int32)[None, :]
                      + jax.random.randint(ks[2], (BATCH, 1), 0, 4096, dtype=jnp.int32)),
        'norm_mix': gain(ks[3], (DEPTH, D_MODEL)),
        'w_in': w(ks[4], (DEPTH, D_MODEL, IN_PROJ_WIDTH), D_MODEL),
        'hg_lower_bounds': 1.0 + 0.1 * jax.random.normal(ks[5], (DEPTH, HG_WIDTH), F32),
        'hg_out_norm': gain(ks[6], (DEPTH, HG_WIDTH)),
        'w_out': w(ks[7], (DEPTH, MIX_WIDTH, D_MODEL), MIX_WIDTH),
        'norm_cross': gain(ks[8], (DEPTH, D_MODEL)),
        'norm_mem': gain(ks[9], (DEPTH, D_MODEL)),
        'wq_x': w(ks[10], (DEPTH, D_MODEL, D_MODEL), D_MODEL),
        'wkv_x': w(ks[11], (DEPTH, D_MODEL, 2 * D_MODEL), D_MODEL),
        'wo_x': w(ks[12], (DEPTH, D_MODEL, D_MODEL), D_MODEL),
        'norm_ffn': gain(ks[13], (DEPTH, D_MODEL)),
        'w_router_group': w(ks[14], (DEPTH, D_MODEL, N_GROUPS), D_MODEL),
        'w_router_expert': w(ks[15], (DEPTH, D_MODEL, N_EXPERTS), D_MODEL),
        'w_gate': w(ks[16], (DEPTH, N_EXPERTS, D_MODEL, EXPERT_FF), D_MODEL),
        'w_up': w(ks[17], (DEPTH, N_EXPERTS, D_MODEL, EXPERT_FF), D_MODEL),
        'w_down': w(ks[18], (DEPTH, N_EXPERTS, EXPERT_FF, D_MODEL), EXPERT_FF),
        'norm_final': gain(ks[19], (D_MODEL,)),
    }

def reference(x, mem, positions, norm_mix, w_in, hg_lower_bounds, hg_out_norm, w_out,
              norm_cross, norm_mem, wq_x, wkv_x, wo_x, norm_ffn, w_router_group,
              w_router_expert, w_gate, w_up, w_down, norm_final):
    lb_sm = jax.nn.softmax(hg_lower_bounds.astype(F32), axis=0)
    lbs = jnp.cumsum(lb_sm, axis=0) - lb_sm[0:1]
    for l in range(DEPTH):
        h = rms_norm(x, norm_mix[l])
        proj = h @ w_in[l]
        hq, hf, hi, hgate, aq, ak, av = jnp.split(proj, IN_SPLITS, axis=-1)
        y_hg = hgrn2_mixer(hq, hf, hi, hgate, lbs[l], hg_out_norm[l])
        y_att = dilated_attention_mixer(aq, ak, av, positions)
        x = x + jnp.concatenate([y_hg, y_att], axis=-1) @ w_out[l]
        x = x + memory_cross_attention(rms_norm(x, norm_cross[l]), rms_norm(mem, norm_mem[l]),
                                       wq_x[l], wkv_x[l], wo_x[l])
        x = x + hierarchical_moe(rms_norm(x, norm_ffn[l]), w_router_group[l], w_router_expert[l],
                                 w_gate[l], w_up[l], w_down[l])
    return rms_norm(x, norm_final)


_drawn_inputs = setup_inputs


def setup_inputs(seed=0):
    import zlib

    import numpy as np

    out = dict(_drawn_inputs(seed))
    spreads = {}
    factors = {'norm_cross': 4.041, 'norm_mem': 3.051, 'norm_final': 2.844}
    for name, (base, spread) in spreads.items():
        noise = np.random.default_rng([zlib.crc32(name.encode()), seed]).standard_normal(out[name].shape)
        drawn = base * np.exp(spread * noise) if base else spread * noise
        out[name] = __import__('jax').numpy.asarray(drawn.astype(out[name].dtype))
    for name, factor in factors.items():
        out[name] = (out[name] * factor).astype(out[name].dtype)
    return out
```

```python
from contextlib import ExitStack

import numpy as np

import concourse.bass as bass
from concourse import mybir

P = 128
ALU = mybir.AluOpType
ACT = mybir.ActivationFunctionType
F32 = mybir.dt.float32
I32 = mybir.dt.int32
AX = mybir.AxisListType.X

D = 1024
C = D // P
T = 256
M = T // P
DEPTH = 2
HG_HEADS = 4
ATT_HEADS = 8
DH = 64
X_HEADS = 4
X_DH = D // X_HEADS
N_GROUPS = 4
N_EXPERTS = 16
FF = 512
W = 512
NEG = -1.0e30
EPS = 1e-6
ROPE_THETA = 10000.0

SLOTS = 6
UNITS = ["hf", "hq", "hi", "aq", "ak", "av", "hg", "k0", "k1", "v0", "v1", "o0", "o1", "q0", "q1", "p0", "p1", "router"]
MIX_ROUNDS = len(UNITS) // SLOTS
PAIRS = N_EXPERTS // 2
ROUNDS = MIX_ROUNDS + PAIRS


def job_list():
    quarters = [(m, c) for m in range(M) for c in range(2)]
    jobs = [(f"t1_{m}{c}", "D") for m, c in quarters]
    for name, who in (("hf", "A"), ("hq", "A"), ("hi", "A"), ("aq", "D"), ("ak", "D"), ("av", "A"), ("hg", "D")):
        jobs += [(f"{name}{m}", who) for m in range(2)]
    jobs += [(f"{name}{m}", "A") for name in ("qT", "kT") for m in range(M)]
    for j in range(8):
        jobs += [(f"kv{j}", "A")] + [(f"lev{j}_{m}", "D") for m in range(M)]
    jobs += [("cross", "D")]
    jobs += [(f"s{k}", "D") for k in range(6)]
    jobs += [(f"hp{m}", "D") for m in range(M)]
    jobs += [(f"et{k}", "D") for k in range(6)]
    jobs += [(f"ap{m}{g}", "D") for m, g in quarters]
    jobs += [(f"t2_{m}{c}", "A") for m, c in quarters]
    jobs += [(f"wo{n}{m}", "D") for n in range(2) for m in range(M)]
    jobs += [(f"t3_{m}{c}", "D") for m, c in quarters]
    jobs += [(f"qx{k}", "A") for k in range(4)]
    jobs += [(f"sx{m}{g}", "A") for m, g in quarters]
    jobs += [(f"pt{m}{c}", "D") for m, c in quarters]
    jobs += [(f"px{m}{g}", "D") for m, g in quarters]
    jobs += [(f"t4_{m}{c}", "A") for m, c in quarters]
    jobs += [(f"ox{n}{m}", "D") for n in range(2) for m in range(M)]
    jobs += [(f"t5_{m}{c}", "D") for m, c in quarters]
    return jobs + [("rt", "A"), ("rl", "D")]


JOBS = job_list()
NAMES = [n for n, _ in JOBS]
NJ = len(JOBS)
EMPTIER = dict(JOBS)
NTH = {n: sum(w == EMPTIER[n] for _, w in JOBS[:i + 1]) for i, (n, _) in enumerate(JOBS)}
EMPTIED = {w: sum(x == w for _, x in JOBS) for w in "AD"}
LAST_USE = {"hf": "hf1", "hq": "hq1", "hi": "hi1", "aq": "aq1", "ak": "ak1", "av": "av1", "hg": "hg1",
            "k0": "kv1", "k1": "kv3", "v0": "kv5", "v1": "kv7", "o0": "wo01", "o1": "wo11",
            "q0": "qx1", "q1": "qx3", "p0": "ox01", "p1": "ox11", "router": "rt"}
SCORES = [(0, (0, 2, 4, 6)), (0, (1, 3, 5, 7)), (1, (0, 2)), (1, (1, 3)), (1, (4, 6)), (1, (5, 7))]

MOE_JOBS = 20
MOE_FREE = {0: 12, 1: 12, 2: 14, 3: 14, 4: 20, 5: 20}

DVE_LINKS = 136
DVE_PAIR_LINKS = 8 + 4
POOL_LINKS = 5


class Chain:

    def __init__(self, eng, sem):
        self.eng, self.sem, self.base, self.n = eng, sem, 0, 0

    def link(self, ins):
        self.n += 1
        ins.then_inc(self.sem, 1)
        self.eng.wait_ge(self.sem, self.base + self.n)

    def enter(self, base):
        self.base, self.n = base, 0


def trunk(nc, x_in, mem_in, pos_in, inv_in, gains_in, lb_in, og_in, w_in, w_out, wq, wkv, wo, w_router,
          w_gate, w_up, w_down, nf_in, out):
    ctx = ExitStack()
    with ctx:
        def sb(name, shape, dt=F32):
            return ctx.enter_context(nc.sbuf_tensor(name, shape, dt))

        def sem(name):
            return ctx.enter_context(nc.semaphore(name))

        ring = sb("ring", [P, SLOTS, 4096])
        x = sb("x", [P, M, D])
        xs = sb("xs", [P, M, D])
        hT = sb("hT", [P, C, T])
        memT = sb("memT", [P, C, T])
        hi = sb("hi", [P, M, W])
        gg = sb("gg", [P, M, W])
        rot = sb("rot", [P, 4 * W])
        vaug = sb("vaug", [P, M, ATT_HEADS, DH + 1])
        work = sb("work", [P, 4, HG_HEADS * T])
        S = sb("S", [P, M, HG_HEADS, P])
        PT = sb("PT", [P, 3, ATT_HEADS, P])
        S01 = PT[:, 2, 0:HG_HEADS, :]
        KT = sb("KT", [P, 8, T])
        Vx = sb("Vx", [P, M, D])
        lev = sb("lev", [P, 8, P])
        bias0 = sb("bias0", [P, P])
        bias10 = sb("bias10", [P, P])
        cnt = sb("cnt", [P, 2, P])
        ident = sb("ident", [P, P])
        gains = sb("gains", [P, DEPTH, 40])
        cur = sb("cur", [P, 40])
        og = sb("og", [P, W])
        cosT = sb("cosT", [P, M, 32])
        sinT = sb("sinT", [P, M, 32])
        sm = sb("sm", [P, 112])
        wsm = sb("wsm", [P, 216])
        early = PT[:, 2, 6:8, :].rearrange("p a t -> p (a t)")
        gates = sb("gates", [P, M, N_EXPERTS])

        Q = work[:, 0, :].rearrange("p (a t) -> p a t", a=HG_HEADS)
        K = work[:, 1, :].rearrange("p (a t) -> p a t", a=HG_HEADS)
        F = work[:, 2, :].rearrange("p (a t) -> p a t", a=HG_HEADS)
        TOT = work[:, 3, :].rearrange("p (a t) -> p a t", a=HG_HEADS)
        E = work[:, :, :].rearrange("p a b -> p (a b)")
        attT = xs[:, :, :].rearrange("p a (g t) -> p (a g) t", t=T)
        QxT = rot[:, :].rearrange("p (n t) -> p n t", t=T)
        Px = work[:, 0:2, :].rearrange("p m (h s) -> p m h s", s=T)
        PTx = PT[:, 0:2, :, :].rearrange("p a (b h) t -> p (a b) h t", h=HG_HEADS)
        ss = sm[:, 0:2]
        rstd = sm[:, 2:4]
        hss = sm[:, 4:12].rearrange("p (m h) -> p m h", m=M)
        hrs = sm[:, 12:20].rearrange("p (m h) -> p m h", m=M)
        nmx = sm[:, 20:36]
        rden = sm[:, 36:52].rearrange("p (m h) -> p m h", m=M)
        xmx = sm[:, 52:60].rearrange("p (m h) -> p m h", m=M)
        xden = sm[:, 60:68].rearrange("p (m h) -> p m h", m=M)
        xrd = sm[:, 68:76].rearrange("p (m h) -> p m h", m=M)
        expo = sm[:, 76:84]
        mss = sm[:, 84:86]
        mrs = sm[:, 86:88]
        msq = sm[:, 88:96]
        posf = sm[:, 96:98]
        sq = rot[:, 0:D]

        banks = [ctx.enter_context(nc.psum_tensor(f"bank{i}", [P, W], F32)) for i in range(8)]

        loaded = [sem(f"loaded{s}") for s in range(SLOTS)]
        x_loaded, mem_loaded, small_loaded = sem("x_loaded"), sem("mem_loaded"), sem("small_loaded")
        og_loaded, nf_loaded = sem("og_loaded"), sem("nf_loaded")
        iota_done, masks_done, tables_done = sem("iota_done"), sem("masks_done"), sem("tables_done")
        zeroed = sem("zeroed")
        ident_done = sem("ident_done")
        mem_sq, mem_rstd, mem_scaled, mem_tr, mem_kept = (sem(n) for n in ("mem_sq", "mem_rstd", "mem_scaled", "mem_tr", "mem_kept"))
        trig_arg = sem("trig_arg")
        lb_exp = sem("lb_exp")
        lb_max = sem("lb_max")
        gains_done = sem("gains_done")
        cur_done = sem("cur_done")
        job_done = sem("job_done")
        empt = {"A": sem("emptied_by_scalar"), "D": sem("emptied_by_vector")}
        sq_done = sem("sq_done")
        rstd_done = sem("rstd_done")
        normed = sem("normed")
        f_done = sem("f_done")
        q_done = sem("q_done")
        k_done = sem("k_done")
        tot_done = sem("tot_done")
        rot_done = sem("rot_done")
        gate_exp = sem("gate_exp")
        memg_done = sem("memg_done")
        max_done = sem("max_done")
        e_done = sem("e_done")
        hsq_done = sem("hsq_done")
        hms_done = sem("hms_done")
        hrs_done = sem("hrs_done")
        y_done = sem("y_done")
        xmax_done = sem("xmax_done")
        lexp_done = sem("lexp_done")
        lmax_done = sem("lmax_done")
        gates_done = sem("gates_done")
        moe_done = sem("moe_done")
        g_exp = sem("g_exp")
        act_done = sem("act_done")
        actT_done = sem("actT_done")
        added = sem("added")
        dve_chain, pool_chain, act_chain = sem("dve_chain"), sem("pool_chain"), sem("act_chain")
        fin_done, out_done = sem("fin_done"), sem("out_done")

        def bank(name):
            return banks[NAMES.index(name) % 8]

        def wait_job(eng, L, name):
            eng.wait_ge(job_done, L * NJ + NAMES.index(name) + 1)

        def wait_emptied(eng, L, name):
            who = EMPTIER[name]
            eng.wait_ge(empt[who], L * EMPTIED[who] + NTH[name])

        def unit_source(L, u):
            name = UNITS[u]
            starts = {"hq": 0, "hf": 512, "hi": 1024, "hg": 1536, "aq": 2048, "ak": 2560, "av": 3072}
            if name in starts:
                t, n0 = w_in, starts[name]
            elif name == "router":
                return w_router[bass.ds(L, 1), :, :].rearrange("l (p c) n -> p (l c) n", c=C), N_GROUPS + N_EXPERTS
            else:
                t, n0 = {"k0": (wkv, 0), "k1": (wkv, 512), "v0": (wkv, 1024), "v1": (wkv, 1536), "o0": (w_out, 0),
                         "o1": (w_out, 512), "q0": (wq, 0), "q1": (wq, 512), "p0": (wo, 0), "p1": (wo, 512)}[name]
            return t[bass.ds(L, 1), :, n0:n0 + W].rearrange("l (p c) n -> p (l c) n", c=C), W

        def unit(name, n=W):
            return ring[:, UNITS.index(name) % SLOTS, 0:C * n].rearrange("p (c n) -> p c n", c=C)

        tots = []
        off = 0
        for j in range(1, 7):
            tots.append(TOT[:, :, off:off + (T >> j)])
            off += T >> j

        actb = work[:, 0, :].rearrange("p (m n) -> p m n", m=M)
        actT = work[:, 1, 0:W].rearrange("p (c t) -> p c t", c=4)
        gexp = work[:, 2, :].rearrange("p (m n) -> p m n", m=M)
        HALF_PI = float(np.pi / 2)

        logits = wsm[:, 0:40].rearrange("p (m n) -> p m n", m=M)
        ngmx = wsm[:, 40:42]
        gsum = wsm[:, 42:44]
        lexp = wsm[:, 44:52].rearrange("p (m n) -> p m n", m=M)
        e2 = wsm[:, 52:54]
        pad8 = wsm[:, 56:72].rearrange("p (m n) -> p m n", m=M)
        top8 = wsm[:, 72:88].rearrange("p (m n) -> p m n", m=M)
        idx8 = wsm[:, 88:104].rearrange("p (m n) -> p m n", m=M)
        oneg = wsm[:, 104:112].rearrange("p (m n) -> p m n", m=M)
        elog = wsm[:, 112:144].rearrange("p (m n) -> p m n", m=M)
        idxf = wsm[:, 144:160].rearrange("p (m n) -> p m n", m=M)
        io16 = wsm[:, 160:176]
        w1 = wsm[:, 176:178]
        w2 = wsm[:, 178:180]
        sc2 = wsm[:, 180:182]
        one1 = wsm[:, 184:216].rearrange("p (m n) -> p m n", m=M)

        block = ctx.enter_context(nc.Block())

        @block.sync
        def _(sp):
            for L in range(DEPTH):
                for u, name in enumerate(UNITS):
                    s = u % SLOTS
                    if u < SLOTS:
                        sp.wait_ge(moe_done, MOE_JOBS * PAIRS * L + MOE_FREE[s])
                    else:
                        wait_job(sp, L, LAST_USE[UNITS[u - SLOTS]])
                    src, n = unit_source(L, u)
                    sp.dma_start(unit(name, n), src).then_inc(loaded[s], 16)
                with sp.Fori(0, PAIRS) as p:
                    for s in range(SLOTS):
                        e = sp.snap(2 * p + N_EXPERTS * L + s % 2)
                        wait_job(sp, L, LAST_USE[UNITS[(MIX_ROUNDS - 1) * SLOTS + s]])
                        sp.wait_ge(moe_done, (MOE_JOBS * PAIRS) * L + MOE_JOBS * p + MOE_FREE[s])
                        w = (w_gate, w_up, w_down)[s // 2]
                        sp.dma_start(ring[:, s, :], w[bass.ds(e, 1), :, :].rearrange("e p n -> p (e n)"))\
                          .then_inc(loaded[s], 16)

        @block.tensor
        def _(pe):
            def wait_unit(L, name):
                u = UNITS.index(name)
                pe.wait_ge(loaded[u % SLOTS], 16 * ROUNDS * L + 16 * (u // SLOTS + 1))

            def open_bank(L, name):
                i = NAMES.index(name)
                if i >= 8:
                    wait_emptied(pe, L, NAMES[i - 8])
                return banks[i % 8]

            def close(ins):
                ins.then_inc(job_done, 1)

            def transposes(L, name, src, rows=P):
                b = open_bank(L, name)
                for k, s in enumerate(src):
                    last = nc.tensor.transpose(b[:, k * P:(k + 1) * P], s, ident[:, :])
                close(last)

            def by_columns(src, m, c2):
                v = src[:, m, :].rearrange("p (k c) -> p c k", c=C)
                return [v[:, 4 * c2 + k, :] for k in range(4)]

            def project(L, name, lhs, m, w):
                b = open_bank(L, name)
                for c in range(C):
                    last = nc.tensor.matmul(b[:, :], lhs[:, c, m * P:(m + 1) * P], w[:, c, :], start=(c == 0), stop=(c == C - 1))
                close(last)

            def project_T(L, name, rhs, w, n2):
                b = open_bank(L, name)
                for k in range(2):
                    for c in range(C):
                        last = nc.tensor.matmul(b[:, k * T:(k + 1) * T], w[:, c, (n2 + k) * P:(n2 + k + 1) * P],
                                                rhs[:, c, :], start=(c == 0), stop=(c == C - 1))
                close(last)

            pe.sem_inc(moe_done, MOE_JOBS)
            pe.wait_ge(ident_done, 2)
            pe.wait_ge(mem_scaled, 2)
            memrow = E[:, 0:M * D].rearrange("p (m d) -> p m d", m=M)
            for m in range(M):
                for c2 in range(2):
                    b = banks[4 + 2 * m + c2]
                    for k, s in enumerate(by_columns(memrow, m, c2)):
                        last = nc.tensor.transpose(b[:, k * P:(k + 1) * P], s, ident[:, :])
                    last.then_inc(mem_tr, 1)
            pe.wait_ge(mem_kept, 4)

            for L in range(DEPTH):
                for m in range(M):
                    pe.wait_ge(normed, 6 * L + m + 1)
                    for c2 in range(2):
                        transposes(L, f"t1_{m}{c2}", by_columns(xs, m, c2))
                wait_emptied(pe, L, "t1_11")
                for name in ("hf", "hq"):
                    wait_unit(L, name)
                    for k in range(2):
                        project_T(L, f"{name}{k}", hT, unit(name), 2 * k)
                for name in ("hi", "aq", "ak", "av", "hg"):
                    wait_unit(L, name)
                    for m in range(M):
                        project(L, f"{name}{m}", hT, m, unit(name))
                for w, name in enumerate(("qT", "kT")):
                    for m in range(M):
                        pe.wait_ge(rot_done, 4 * L + 2 * w + m + 1)
                        r = rot[:, (2 * w + m) * W:(2 * w + m + 1) * W]
                        transposes(L, f"{name}{m}", [r[:, k * P:(k + 1) * P] for k in range(4)])
                pe.wait_ge(memg_done, L + 1)
                for j in range(8):
                    if j < 4:
                        wait_unit(L, f"k{j // 2}")
                        project_T(L, f"kv{j}", hT, unit(f"k{j // 2}"), 2 * (j % 2))
                    else:
                        wait_unit(L, f"v{(j - 4) // 2}")
                        project(L, f"kv{j}", hT, j % 2, unit(f"v{(j - 4) // 2}"))
                    if j == 0:
                        pe.wait_ge(f_done, 2 * L + 2)
                        wait_emptied(pe, L, "hq1")
                    for m in range(M):
                        if j >= 1:
                            pe.wait_ge(q_done, 16 * L + 2 * (j - 1) + m + 1)
                        if j >= 2:
                            pe.wait_ge(k_done, 14 * L + 2 * (j - 2) + m + 1)
                        b = open_bank(L, f"lev{j}_{m}")
                        for a in range(HG_HEADS):
                            last = nc.tensor.matmul(b[:, a * P:(a + 1) * P], K[:, a, m * P:(m + 1) * P],
                                                    Q[:, a, m * P:(m + 1) * P], start=True, stop=True)
                        close(last)
                pe.wait_ge(q_done, 16 * L + 16)
                pe.wait_ge(k_done, 14 * L + 14)
                b = open_bank(L, "cross")
                for a in range(HG_HEADS):
                    last = nc.tensor.matmul(b[:, a * P:(a + 1) * P], K[:, a, 0:P], Q[:, a, P:T], start=True, stop=True)
                close(last)
                wait_emptied(pe, L, "kT1")
                for k, (m, heads) in enumerate(SCORES):
                    n = (m + 1) * P
                    b = open_bank(L, f"s{k}")
                    for i, h in enumerate(heads):
                        r = 64 * (h % 2)
                        last = nc.tensor.matmul(b[:, i * n:(i + 1) * n], attT[r:r + 64, h // 2, m * P:(m + 1) * P],
                                                attT[r:r + 64, 4 + h // 2, 0:n], start=True, stop=True)
                    close(last)
                wait_emptied(pe, L, "cross")
                wait_emptied(pe, L, "hi1")
                for m in range(M):
                    b = open_bank(L, f"hp{m}")
                    for a in range(HG_HEADS):
                        o = b[:, a * P:(a + 1) * P]
                        last = nc.tensor.matmul(o, S[:, m, a, :], hi[:, m, a * P:(a + 1) * P], start=True, stop=(m == 0))
                        if m:
                            last = nc.tensor.matmul(o, S01[:, a, :], hi[:, 0, a * P:(a + 1) * P], start=False, stop=True)
                    close(last)
                for k in range(6):
                    if k == 0:
                        pe.wait_ge(e_done, 6 * L + 2)
                    if k == 2:
                        pe.wait_ge(e_done, 6 * L + 6)
                    if k < 2:
                        src = [E[:, (4 * k + i) * P:(4 * k + i + 1) * P] for i in range(4)]
                    else:
                        jb, h0 = (k - 2) // 2, 4 * (k % 2)
                        src = [E[:, D + (h0 + i) * T + jb * P:D + (h0 + i) * T + (jb + 1) * P] for i in range(4)]
                    transposes(L, f"et{k}", src)
                wait_emptied(pe, L, "av1")
                for m in range(M):
                    for g in range(2):
                        wait_emptied(pe, L, f"et{g}" if m == 0 else f"et{4 + g}")
                        b = open_bank(L, f"ap{m}{g}")
                        for i in range(4):
                            h = 4 * g + i
                            o = b[:, i * P:i * P + DH + 1]
                            last = nc.tensor.matmul(o, PT[:, 2 * m, h, :], vaug[:, m, h, :], start=True, stop=(m == 0))
                            if m:
                                last = nc.tensor.matmul(o, PT[:, 1, h, :], vaug[:, 0, h, :], start=False, stop=True)
                        close(last)
                for m in range(M):
                    pe.wait_ge(y_done, 4 * L + 2 + m + 1)
                    for c2 in range(2):
                        transposes(L, f"t2_{m}{c2}", by_columns(xs, m, c2))
                wait_emptied(pe, L, "t2_11")
                for n in range(2):
                    wait_unit(L, f"o{n}")
                    for m in range(M):
                        project(L, f"wo{n}{m}", hT, m, unit(f"o{n}"))
                for m in range(M):
                    pe.wait_ge(normed, 6 * L + 2 + m + 1)
                    for c2 in range(2):
                        transposes(L, f"t3_{m}{c2}", by_columns(xs, m, c2))
                wait_emptied(pe, L, "t3_11")
                for k in range(4):
                    wait_unit(L, f"q{k // 2}")
                    project_T(L, f"qx{k}", hT, unit(f"q{k // 2}"), 2 * (k % 2))
                wait_emptied(pe, L, "qx3")
                for m in range(M):
                    for g in range(2):
                        b = open_bank(L, f"sx{m}{g}")
                        for i in range(2):
                            h = 2 * g + i
                            for k in range(2):
                                last = nc.tensor.matmul(b[:, i * T:(i + 1) * T], QxT[:, 2 * h + k, m * P:(m + 1) * P],
                                                        KT[:, 2 * h + k, :], start=(k == 0), stop=(k == 1))
                        close(last)
                for m in range(M):
                    wait_emptied(pe, L, f"sx{m}1")
                    for jb in range(2):
                        transposes(L, f"pt{m}{jb}", [Px[:, m, h, jb * P:(jb + 1) * P] for h in range(X_HEADS)])
                for m in range(M):
                    wait_emptied(pe, L, f"pt{m}1")
                    for g in range(2):
                        b = open_bank(L, f"px{m}{g}")
                        for i in range(2):
                            h = 2 * g + i
                            for jb in range(2):
                                last = nc.tensor.matmul(b[:, i * T:(i + 1) * T], PTx[:, 2 * m + jb, h, :],
                                                        Vx[:, jb, h * T:(h + 1) * T], start=(jb == 0), stop=(jb == 1))
                        close(last)
                for m in range(M):
                    wait_emptied(pe, L, f"px{m}1")
                    for c2 in range(2):
                        transposes(L, f"t4_{m}{c2}", by_columns(xs, m, c2))
                wait_emptied(pe, L, "t4_11")
                for n in range(2):
                    wait_unit(L, f"p{n}")
                    for m in range(M):
                        project(L, f"ox{n}{m}", hT, m, unit(f"p{n}"))
                for m in range(M):
                    pe.wait_ge(normed, 6 * L + 4 + m + 1)
                    for c2 in range(2):
                        transposes(L, f"t5_{m}{c2}", by_columns(xs, m, c2))
                wait_emptied(pe, L, "t5_11")
                NR = N_GROUPS + N_EXPERTS
                wait_unit(L, "router")
                b = open_bank(L, "rt")
                for c in range(C):
                    last = nc.tensor.matmul(b[0:NR, 0:T], unit("router", NR)[:, c, :], hT[:, c, :], start=(c == 0), stop=(c == C - 1))
                close(last)
                wait_emptied(pe, L, "rt")
                b = open_bank(L, "rl")
                for m in range(M):
                    last = nc.tensor.transpose(b[:, m * NR:(m + 1) * NR], early[0:NR, m * P:(m + 1) * P], ident[0:NR, 0:NR])
                close(last)
                pe.wait_ge(gates_done, L + 1)

                def fill(p, s):
                    pe.wait_ge(loaded[s], 16 * ROUNDS * L + 16 * p + 16 * (MIX_ROUNDS + 1))

                def pair(p):
                    n4 = 4 * PAIRS * L + 4 * p + 4
                    for b2 in range(2):
                        for s in (b2, 2 + b2):
                            fill(p, s)
                            w = ring[:, s, :].rearrange("p (c n) -> p c n", c=C)
                            for m in range(M):
                                if s < 2:
                                    pe.wait_ge(act_done, n4 + 2 * b2)
                                for c in range(C):
                                    last = nc.tensor.matmul(banks[(0 if s < 2 else 2) + m][:, :], hT[:, c, m * P:(m + 1) * P],
                                                            w[:, c, :], start=(c == 0), stop=(c == C - 1))
                                last.then_inc(moe_done, 1)
                        for m in range(M):
                            pe.wait_ge(act_done, n4 + 2 * b2 + m + 1)
                            pe.wait_ge(actT_done, n4 + 2 * b2 + m)
                            av = actb[:, m, :].rearrange("p (k c) -> p c k", c=4)
                            for k in range(4):
                                last = nc.tensor.transpose(banks[4][:, k * P:(k + 1) * P], av[:, k, :], ident[:, :])
                            last.then_inc(moe_done, 1)
                            pe.wait_ge(actT_done, n4 + 2 * b2 + m + 1)
                            if m == 0:
                                fill(p, 4 + b2)
                            w = ring[:, 4 + b2, :].rearrange("p (c n) -> p c n", c=4)
                            for n in range(2):
                                pe.wait_ge(added, 2 * n4 + 4 * b2 + 2 * m)
                                for c in range(4):
                                    last = nc.tensor.matmul(banks[5 + n][:, :], actT[:, c, :], w[:, c, n * W:(n + 1) * W],
                                                            start=(c == 0), stop=(c == 3))
                                last.then_inc(moe_done, 1)

                with pe.Fori(0, PAIRS) as p:
                    pair(p)

        @block.scalar
        def _(act):
            act.sem_inc(actT_done, 4)
            act.sem_inc(g_exp, 4)
            act.dma_start(x[:, :, :], x_in.rearrange("(m p) d -> p m d", p=P)).then_inc(x_loaded, 16)
            act.dma_start(E[:, 0:M * D].rearrange("p (m d) -> p m d", m=M), mem_in.rearrange("(m p) d -> p m d", p=P))\
               .then_inc(mem_loaded, 16)
            with nc.allow_non_contiguous_dma(reason="small vectors, once"):
                for l in range(DEPTH):
                    act.dma_start(gains[:, l, 0:32].rearrange("p (g c) -> p g c", g=4),
                                  gains_in[:, l, :].rearrange("g (p c) -> p g c", c=C)).then_inc(small_loaded, 16)
                    act.dma_start(gains[:, l, 32:36], lb_in[l, :].rearrange("(h p) -> p h", p=P)).then_inc(small_loaded, 16)
                act.dma_start(early[:, 0:M].bitcast(I32), pos_in.rearrange("(m p) -> p m", p=P)).then_inc(small_loaded, 16)
                act.dma_start(early[:, 64:96], inv_in.partition_broadcast(P)).then_inc(small_loaded, 16)
            act.wait_ge(mem_loaded, 16)
            act.wait_ge(zeroed, 1)
            for m in range(M):
                nc.scalar.activation(sq, E[:, m * D:(m + 1) * D], ACT.Square, accum_out=mss[:, m:m + 1]).then_inc(mem_sq, 1)
                act.wait_ge(mem_sq, m + 1)
            act.wait_ge(lb_max, 1)
            nc.scalar.activation(gains[:, :, 36:40], gains[:, :, 36:40], ACT.Exp).then_inc(lb_exp, 1)
            act.wait_ge(trig_arg, 1)
            nc.scalar.activation(cosT[:, :, :], cosT[:, :, :], ACT.Sin)
            nc.scalar.activation(sinT[:, :, :], sinT[:, :, :], ACT.Sin).then_inc(tables_done, 1)

            def squares(count):
                for m in range(M):
                    nc.scalar.activation(sq, x[:, m, :], ACT.Square, accum_out=ss[:, m:m + 1]).then_inc(sq_done, 1)
                    act.wait_ge(sq_done, count + m + 1)

            act.wait_ge(x_loaded, 16)
            for L in range(DEPTH):
                act.wait_ge(added, 8 * PAIRS * L + 8)
                act.wait_ge(y_done, 4 * L)
                with nc.allow_non_contiguous_dma(reason="one row to all partitions"):
                    act.dma_start(og[:, :], og_in[bass.ds(L, 1), :].rearrange("l n -> (l n)").partition_broadcast(P)).then_inc(og_loaded, 16)
                squares(6 * L)

                def empty(name, dst, func=ACT.Copy, scale=1.0, view=None):
                    wait_job(act, L, name)
                    src = bank(name)[:, :] if view is None else view
                    nc.scalar.activation(dst, src, func, scale=scale).then_inc(empt["A"], 1)

                def halves(name):
                    return bank(name)[:, :].rearrange("p (a t) -> p a t", a=2)

                for k in range(2):
                    empty(f"hf{k}", F[:, 2 * k:2 * k + 2, :], ACT.Exp, -1.0, halves(f"hf{k}"))
                for k in range(2):
                    empty(f"hq{k}", Q[:, 2 * k:2 * k + 2, :], view=halves(f"hq{k}"))
                for m in range(M):
                    empty(f"hi{m}", hi[:, m, :])
                for m in range(M):
                    empty(f"av{m}", vaug[:, m, :, 0:DH], view=bank(f"av{m}")[:, :].rearrange("p (h d) -> p h d", d=DH))
                for m in range(M):
                    wait_job(act, L, f"hg{m}")
                    nc.scalar.activation(gg[:, m, :], bank(f"hg{m}")[:, :], ACT.Exp, scale=-1.0).then_inc(gate_exp, 1)
                for w, name in enumerate(("qT", "kT")):
                    for m in range(M):
                        empty(f"{name}{m}", attT[:, 4 * w:4 * w + 4, m * P:(m + 1) * P], scale=(DH ** -0.5 if w == 0 else 1.0),
                              view=bank(f"{name}{m}")[:, :].rearrange("p (g t) -> p g t", t=P))
                for j in range(8):
                    if j < 4:
                        empty(f"kv{j}", KT[:, 2 * j:2 * j + 2, :], view=halves(f"kv{j}"))
                    else:
                        empty(f"kv{j}", Vx[:, j % 2, ((j - 4) // 2) * W:((j - 4) // 2 + 1) * W])
                at = 0
                for k, (m, heads) in enumerate(SCORES):
                    act.wait_ge(max_done, 6 * L + k + 1)
                    n = (m + 1) * P
                    for h in heads:
                        e = E[:, m * D + h * n:m * D + (h + 1) * n]
                        last = nc.scalar.activation(e, e, ACT.Exp, bias=nmx[:, at:at + 1])
                        at += 1
                    last.then_inc(e_done, 1)
                for m in range(M):
                    wait_job(act, L, f"hp{m}")
                    nc.scalar.activation(rot[:, m * W:(m + 1) * W], bank(f"hp{m}")[:, :], ACT.Square).then_inc(hsq_done, 1)

                def rows_T(t):
                    for m in range(M):
                        for c2 in range(2):
                            empty(f"{t}_{m}{c2}", hT[:, 4 * c2:4 * c2 + 4, m * P:(m + 1) * P],
                                  view=bank(f"{t}_{m}{c2}")[:, :].rearrange("p (c t) -> p c t", c=4))

                wait_job(act, L, "kv7")
                rows_T("t2")
                wait_emptied(act, L, "wo11")
                squares(6 * L + 2)
                act.wait_ge(hms_done, 2 * L + 2)
                for k in range(4):
                    empty(f"qx{k}", QxT[:, 2 * k:2 * k + 2, :], view=halves(f"qx{k}"))
                for m in range(M):
                    for g in range(2):
                        act.wait_ge(xmax_done, 4 * L + 2 * m + g + 1)
                        for i in range(2):
                            h = 2 * g + i
                            last = nc.scalar.activation(Px[:, m, h, :], bank(f"sx{m}{g}")[:, i * T:(i + 1) * T], ACT.Exp,
                                                        bias=xmx[:, m, h:h + 1], scale=X_DH ** -0.5, accum_out=xden[:, m, h:h + 1])
                        last.then_inc(empt["A"], 1)
                rows_T("t4")
                wait_emptied(act, L, "ox11")
                squares(6 * L + 4)
                empty("rt", early[0:20, 0:T], view=bank("rt")[0:20, 0:T])
                act.wait_ge(lmax_done, 2 * L + 1)
                for m in range(M):
                    last = nc.scalar.activation(lexp[:, m, :], logits[:, m, 0:N_GROUPS], ACT.Exp, bias=ngmx[:, m:m + 1],
                                                accum_out=gsum[:, m:m + 1])
                last.then_inc(lexp_done, 1)
                act.wait_ge(lmax_done, 2 * L + 2)
                nc.scalar.activation(e2[:, :], e2[:, :], ACT.Exp).then_inc(lexp_done, 1)

                with act.Fori(0, PAIRS) as p:
                    n4 = 4 * PAIRS * L + 4 * p + 4
                    moe = MOE_JOBS * PAIRS * L + MOE_JOBS * p + MOE_JOBS
                    for b2 in range(2):
                        for m in range(M):
                            act.wait_ge(moe_done, moe + 10 * b2 + m + 1)
                            act.wait_ge(act_done, n4 + 2 * b2)
                            nc.scalar.activation(gexp[:, m, :], banks[m][:, :], ACT.Exp, scale=-1.0).then_inc(g_exp, 1)
                        for m in range(M):
                            act.wait_ge(moe_done, moe + 10 * b2 + 4 + 3 * m + 1)
                            nc.scalar.activation(actT[:, :, :], banks[4][:, :].rearrange("p (c t) -> p c t", c=4), ACT.Copy)\
                              .then_inc(actT_done, 1)

            act.wait_ge(added, 8 * PAIRS * DEPTH + 8)
            act.wait_ge(y_done, 4 * DEPTH)
            with nc.allow_non_contiguous_dma(reason="one row to all partitions"):
                act.dma_start(Vx[:, 0, :], nf_in.partition_broadcast(P)).then_inc(nf_loaded, 16)
            squares(6 * DEPTH)
            for m in range(M):
                act.wait_ge(fin_done, m + 1)
                act.dma_start(out[m * P:(m + 1) * P, :], xs[:, m, :]).then_inc(out_done, 16)
            act.wait_ge(out_done, 16 * M)

        @block.gpsimd
        def _(pool):
            chain = Chain(pool, pool_chain)
            link = chain.link
            nc.gpsimd.memset(sm[:, :], 0.0).then_inc(zeroed, 1)
            pool.wait_ge(zeroed, 1)
            nc.gpsimd.iota(PT[:, 0, 0, :].bitcast(I32), pattern=[[1, P]], base=P, channel_multiplier=-1)
            nc.gpsimd.iota(PT[:, 1, 0, :].bitcast(I32), pattern=[[1, P]], base=0, channel_multiplier=0)
            nc.gpsimd.iota(PT[:, 1, 1, :].bitcast(I32), pattern=[[0, P]], base=0, channel_multiplier=1).then_inc(iota_done, 1)
            nc.gpsimd.iota(io16, pattern=[[1, N_EXPERTS]], base=0, channel_multiplier=0, allow_small_or_imprecise_dtypes=True)\
              .then_inc(iota_done, 1)
            link(nc.gpsimd.memset(expo, -0.5))
            nc.gpsimd.memset(ident[:, :], 0.0).then_inc(ident_done, 1)
            pool.wait_ge(ident_done, 1)
            nc.gpsimd.affine_select(out=ident[:, :], in_=ident[:, :], compare_op=ALU.not_equal, fill=1.0, base=0,
                                    pattern=[[-1, P]], channel_multiplier=1).then_inc(ident_done, 1)
            nc.gpsimd.memset(S[:, :, :, :], 0.0)
            nc.gpsimd.memset(pad8[:, :, :], NEG)
            nc.gpsimd.memset(vaug[:, :, :, :], 1.0).then_inc(zeroed, 1)

            def root(dst, src, n, width):
                link(nc.gpsimd.tensor_scalar(dst, src, 1.0 / n, EPS, ALU.mult, ALU.add))
                return nc.gpsimd.tensor_tensor(dst, dst, expo[:, 0:width], ALU.pow)

            pool.wait_ge(mem_sq, 2)
            root(mrs, mss, D, 2).then_inc(mem_rstd, 1)

            first = chain.n
            for L in range(DEPTH):
                chain.enter(first + POOL_LINKS * L)
                pool.wait_ge(gains_done, 1)
                pool.wait_ge(gates_done, L)
                nc.gpsimd.tensor_copy(cur[:, :], gains[:, bass.ds(L, 1), :].rearrange("p l n -> p (l n)")).then_inc(cur_done, 1)

                def norm(k):
                    pool.wait_ge(sq_done, 6 * L + 2 * k + 2)
                    root(rstd, ss, D, 2).then_inc(rstd_done, 1)

                norm(0)
                tot_n = 0
                pool.wait_ge(f_done, 2 * L + 2)
                for prev, cu in zip([F] + tots, tots):
                    pv = prev.rearrange("p a (b u) -> p a b u", u=2)
                    nc.gpsimd.tensor_tensor(cu, pv[:, :, :, 0], pv[:, :, :, 1], ALU.mult).then_inc(tot_done, 1)
                    tot_n += 1
                    pool.wait_ge(tot_done, 6 * L + tot_n)
                wait_job(pool, L, "hg1")
                pool.wait_ge(mem_kept, 4)
                pool.wait_ge(cur_done, L + 1)
                nc.gpsimd.tensor_tensor(hT[:, :, :], memT[:, :, :], cur[:, 16:24].unsqueeze(2).to_broadcast([P, C, T]), ALU.mult)\
                  .then_inc(memg_done, 1)
                for j in range(7):
                    h = 1 << j
                    tj = [F] + tots
                    for m in range(M):
                        kv = K[:, :, m * P:(m + 1) * P].rearrange("p a (b u i) -> p a b u i", u=2, i=h)[:, :, :, 0, :]
                        tv = tj[j][:, :, m * (P // h):(m + 1) * (P // h)].rearrange("p a (b u) -> p a b u", u=2)[:, :, :, 1]
                        wait_job(pool, L, f"lev{j + 1}_{m}")
                        nc.gpsimd.tensor_tensor(kv, kv, tv.unsqueeze(3).to_broadcast([P, HG_HEADS, P // (2 * h), h]), ALU.mult)\
                          .then_inc(k_done, 1)
                        pool.wait_ge(k_done, 14 * L + 2 * j + m + 1)
                for m in range(M):
                    pool.wait_ge(hms_done, 2 * L + m + 1)
                    root(hrs[:, m, :], hss[:, m, :], P, HG_HEADS).then_inc(hrs_done, 1)
                norm(1)
                norm(2)
                assert chain.n == POOL_LINKS, f"POOL_LINKS = {chain.n}"
            pool.wait_ge(sq_done, 6 * DEPTH + 2)
            chain.enter(first + POOL_LINKS * DEPTH)
            root(rstd, ss, D, 2).then_inc(rstd_done, 1)

        @block.vector
        def _(dve):
            chain = Chain(dve, dve_chain)
            link = chain.link
            V = nc.vector
            dve.sem_inc(act_done, 4)
            dve.sem_inc(added, 8)
            dve.wait_ge(iota_done, 2)
            dve.wait_ge(zeroed, 2)
            dif, fi, pi = (PT[:, 0, 0, :].bitcast(I32), PT[:, 1, 0, :].bitcast(I32), PT[:, 1, 1, :].bitcast(I32))
            tmp = PT[:, 2, 0, :].bitcast(I32)
            ge, le, m4, m16 = (PT[:, 2, k, :] for k in range(1, 5))
            V.tensor_scalar(ge, dif, float(P), None, ALU.is_ge)
            V.tensor_scalar(le, dif, float(P), None, ALU.is_le)
            link(V.tensor_scalar(tmp, dif, 3, None, ALU.bitwise_and))
            link(V.tensor_scalar(m4, tmp, 0.0, None, ALU.is_equal))
            link(V.tensor_scalar(tmp, dif, 15, None, ALU.bitwise_and))
            link(V.tensor_scalar(m16, tmp, 0.0, None, ALU.is_equal))
            V.tensor_scalar(bias0[:, :], le, 1.0, -NEG, ALU.subtract, ALU.mult)
            link(V.tensor_tensor(bias10[:, :], ge, m4, ALU.max))
            link(V.tensor_scalar(bias10[:, :], bias10[:, :], 1.0, -NEG, ALU.subtract, ALU.mult))
            link(V.tensor_tensor(m4, m4, m16, ALU.add))
            link(V.tensor_tensor(cnt[:, 1, :], le, m4, ALU.add))
            link(V.tensor_scalar(m4, m4, 1.0, None, ALU.add))
            link(V.tensor_tensor(cnt[:, 0, :], ge, m4, ALU.mult))
            link(V.tensor_tensor(fi, fi, pi, ALU.bitwise_xor))
            V.tensor_scalar(lev[:, 0, :], dif, float(P), None, ALU.is_equal)
            for j in range(7):
                link(V.tensor_scalar(tmp, fi, j, None, ALU.logical_shift_right))
                link(V.tensor_scalar(lev[:, j + 1, :], tmp, 1.0, None, ALU.is_equal))
                link(V.tensor_tensor(lev[:, j + 1, :], lev[:, j + 1, :], ge, ALU.mult))
            dve.wait_ge(mem_rstd, 1)
            dve.wait_ge(mem_loaded, 16)
            for m in range(M):
                V.tensor_scalar(E[:, m * D:(m + 1) * D], E[:, m * D:(m + 1) * D], mrs[:, m:m + 1], None, ALU.mult).then_inc(mem_scaled, 1)
            dve.wait_ge(small_loaded, 96)
            lb = [gains[:, l, 32:36] for l in range(DEPTH)]
            ex = [gains[:, l, 36:40] for l in range(DEPTH)]
            mx, tot = early[:, 100:104], early[:, 104:108]
            link(V.tensor_tensor(mx, lb[0], lb[1], ALU.max))
            V.tensor_tensor(ex[0], lb[0], mx, ALU.subtract)
            V.tensor_tensor(ex[1], lb[1], mx, ALU.subtract).then_inc(lb_max, 1)
            link(V.tensor_copy(posf, early[:, 0:M].bitcast(I32)))
            for m in range(M):
                last = V.tensor_scalar(sinT[:, m, :], early[:, 64:96], posf[:, m:m + 1], None, ALU.mult)
            link(last)
            ang = sinT[:, :, :].rearrange("p m k -> p (m k)")
            red = cosT[:, :, :].rearrange("p m k -> p (m k)")
            turns = early[:, 128:192]
            MAGIC = 1.5 * 2.0 ** 23
            two_pi = 2.0 * np.pi
            c1 = 6.28125
            c2 = float(np.float32(np.round((two_pi - c1) * 2.0 ** 20) / 2.0 ** 20))
            c3 = float(two_pi - c1 - c2)
            for table, shift in ((red, 0.25), (ang, 0.0)):
                link(V.tensor_scalar(turns, ang, 1.0 / two_pi, shift, ALU.mult, ALU.add))
                link(V.tensor_scalar(turns, turns, MAGIC, None, ALU.add))
                link(V.tensor_scalar(turns, turns, MAGIC, None, ALU.subtract))
                link(V.scalar_tensor_tensor(table, turns, -c1, ang, ALU.mult, ALU.add))
                link(V.scalar_tensor_tensor(table, turns, -c2, table, ALU.mult, ALU.add))
                link(V.scalar_tensor_tensor(table, turns, -c3, table, ALU.mult, ALU.add))
                if shift:
                    link(V.tensor_scalar(table, table, HALF_PI, None, ALU.add))
                link(V.tensor_scalar(table, table, 3.1415925, -3.1415925, ALU.min, ALU.max))
            V.tensor_copy(sm[:, 106:107], sm[:, 107:108]).then_inc(trig_arg, 1)
            dve.wait_ge(lb_exp, 1)
            link(V.tensor_tensor(tot, ex[0], ex[1], ALU.add))
            link(V.reciprocal(tot, tot))
            V.tensor_tensor(ex[0], ex[0], tot, ALU.mult)
            link(V.tensor_tensor(ex[1], ex[1], tot, ALU.mult))
            link(V.tensor_tensor(lb[1], ex[0], ex[1], ALU.add))
            V.tensor_tensor(lb[0], ex[0], ex[0], ALU.subtract)
            link(V.tensor_tensor(lb[1], lb[1], ex[0], ALU.subtract))
            for l in range(DEPTH):
                last = V.tensor_scalar(ex[l], lb[l], -1.0, 1.0, ALU.mult, ALU.add)
            last.then_inc(gains_done, 1)
            for m in range(M):
                for c2 in range(2):
                    dve.wait_ge(mem_tr, 2 * m + c2 + 1)
                    V.tensor_copy(memT[:, 4 * c2:4 * c2 + 4, m * P:(m + 1) * P],
                                  banks[4 + 2 * m + c2][:, :].rearrange("p (c t) -> p c t", c=4)).then_inc(mem_kept, 1)
            dve.wait_ge(tables_done, 1)

            def scale_rows(L, k):
                dve.wait_ge(rstd_done, 3 * L + k + 1)
                for m in range(M):
                    V.tensor_scalar(xs[:, m, :], x[:, m, :], rstd[:, m:m + 1], None, ALU.mult).then_inc(normed, 1)

            first = chain.n
            for L in range(DEPTH):
                chain.enter(first + DVE_LINKS * L)

                def emptied(ins):
                    ins.then_inc(empt["D"], 1)

                def rows_T(t, g0):
                    for m in range(M):
                        for c2 in range(2):
                            wait_job(dve, L, f"{t}_{m}{c2}")
                            emptied(V.tensor_tensor(hT[:, 4 * c2:4 * c2 + 4, m * P:(m + 1) * P],
                                                    bank(f"{t}_{m}{c2}")[:, :].rearrange("p (c t) -> p c t", c=4),
                                                    cur[:, g0 + 4 * c2:g0 + 4 * c2 + 4].unsqueeze(2).to_broadcast([P, 4, P]), ALU.mult))

                scale_rows(L, 0)
                dve.wait_ge(cur_done, L + 1)
                rows_T("t1", 0)
                Fall = F[:, :, :].rearrange("p a t -> p (a t)")
                wait_emptied(dve, L, "hf1")
                link(V.tensor_scalar(Fall, Fall, 1.0, None, ALU.add))
                link(V.reciprocal(Fall, Fall))
                for a in range(HG_HEADS):
                    last = V.tensor_scalar(F[:, a, :], F[:, a, :], cur[:, 36 + a:37 + a], cur[:, 32 + a:33 + a], ALU.mult, ALU.add)
                last.then_inc(f_done, 1)
                dve.wait_ge(f_done, 2 * L + 1)
                V.tensor_scalar(K[:, :, :].rearrange("p a t -> p (a t)"), Fall, -1.0, 1.0, ALU.mult, ALU.add).then_inc(f_done, 1)
                for w, name in enumerate(("aq", "ak")):
                    for m in range(M):
                        wait_job(dve, L, f"{name}{m}")
                        t = bank(f"{name}{m}")[:, :].rearrange("p (h u i) -> p h u i", u=2, i=32)
                        r = rot[:, (2 * w + m) * W:(2 * w + m + 1) * W].rearrange("p (h u i) -> p h u i", u=2, i=32)
                        b = PT[:, 0, 0:4, :].rearrange("p a (h u i) -> p (a h) u i", u=2, i=32)
                        cs = cosT[:, m, :].unsqueeze(1).unsqueeze(1).to_broadcast([P, ATT_HEADS, 2, 32])
                        sn = sinT[:, m, :].unsqueeze(1).unsqueeze(1).to_broadcast([P, ATT_HEADS, 2, 32])
                        V.tensor_tensor(r, t, cs, ALU.mult)
                        link(V.tensor_tensor(b, t, sn, ALU.mult))
                        V.tensor_tensor(r[:, :, 0, :], r[:, :, 0, :], b[:, :, 1, :], ALU.subtract)
                        link(V.tensor_tensor(r[:, :, 1, :], r[:, :, 1, :], b[:, :, 0, :], ALU.add))
                        V.tensor_copy(sm[:, 100:101], sm[:, 101:102]).then_inc(rot_done, 1)
                        emptied(V.tensor_copy(sm[:, 102:103], sm[:, 103:104]))
                dve.wait_ge(og_loaded, 16 * L + 16)
                for m in range(M):
                    dve.wait_ge(gate_exp, 2 * L + m + 1)
                    g = gg[:, m, :]
                    link(V.tensor_scalar(g, g, 1.0, None, ALU.add))
                    link(V.reciprocal(g, g))
                    link(V.tensor_tensor(g, bank(f"hg{m}")[:, :], g, ALU.mult))
                    emptied(V.tensor_tensor(g, g, og[:, :], ALU.mult))
                dve.wait_ge(tot_done, 6 * L + 6)
                tj = [F] + tots
                for j in range(8):
                    for m in range(M):
                        wait_job(dve, L, f"lev{j}_{m}")
                        emptied(V.copy_predicated(S[:, m, :, :], lev[:, j, :].bitcast(I32).unsqueeze(1).to_broadcast([P, HG_HEADS, P]),
                                                  bank(f"lev{j}_{m}")[:, :].rearrange("p (a t) -> p a t", t=P)))
                        Qm = Q[:, :, m * P:(m + 1) * P]
                        if j == 0:
                            V.tensor_tensor(Qm, Qm, F[:, :, m * P:(m + 1) * P], ALU.mult).then_inc(q_done, 1)
                        else:
                            h = 1 << (j - 1)
                            qv = Qm.rearrange("p a (b u i) -> p a b u i", u=2, i=h)[:, :, :, 1, :]
                            tv = tj[j - 1][:, :, m * (P // h):(m + 1) * (P // h)].rearrange("p a (b u) -> p a b u", u=2)[:, :, :, 0]
                            V.tensor_tensor(qv, qv, tv.unsqueeze(3).to_broadcast([P, HG_HEADS, P // (2 * h), h]), ALU.mult)\
                             .then_inc(q_done, 1)
                        dve.wait_ge(q_done, 16 * L + 2 * j + m + 1)
                wait_job(dve, L, "cross")
                emptied(V.tensor_copy(S01[:, :, :], bank("cross")[:, :].rearrange("p (a t) -> p a t", t=P)))
                at = 0
                dve.wait_ge(k_done, 14 * L + 14)
                for k, (m, heads) in enumerate(SCORES):
                    wait_job(dve, L, f"s{k}")
                    n, nh, h0 = (m + 1) * P, len(heads), heads[0]
                    eh = E[:, m * D:m * D + ATT_HEADS * n].rearrange("p (g u n) -> p g u n", u=2, n=n)
                    e = eh[:, h0 // 2:h0 // 2 + nh, h0 % 2, :]
                    src = bank(f"s{k}")[:, :].rearrange("p (g n) -> p g n", n=n)
                    if m:
                        V.tensor_tensor(e[:, :, 0:P], src[:, :, 0:P], bias10[:, :].unsqueeze(1).to_broadcast([P, nh, P]), ALU.add)
                    last = V.tensor_tensor(e[:, :, n - P:n], src[:, :, n - P:n], bias0[:, :].unsqueeze(1).to_broadcast([P, nh, P]), ALU.add)
                    emptied(last)
                    wait_emptied(dve, L, f"s{k}")
                    V.tensor_reduce(nmx[:, at:at + nh], e, AX, ALU.max, negate=True).then_inc(max_done, 1)
                    at += nh
                for m in range(M):
                    dve.wait_ge(hsq_done, 2 * L + m + 1)
                    V.tensor_reduce(hss[:, m, :], rot[:, m * W:(m + 1) * W].rearrange("p (h v) -> p h v", v=P), AX, ALU.add).then_inc(hms_done, 1)
                wait_job(dve, L, "s5")
                for m in range(M):
                    y = xs[:, m, 0:W]
                    emptied(V.tensor_tensor(y, bank(f"hp{m}")[:, :], gg[:, m, :], ALU.mult))
                    wait_emptied(dve, L, f"hp{m}")
                    dve.wait_ge(hrs_done, 2 * L + m + 1)
                    yh = y.rearrange("p (h v) -> p h v", v=P)
                    V.tensor_tensor(yh, yh, hrs[:, m, :].unsqueeze(2).to_broadcast([P, HG_HEADS, P]), ALU.mult).then_inc(y_done, 1)
                for k in range(6):
                    wait_job(dve, L, f"et{k}")
                    blk = 0 if k < 2 else 1 + (k - 2) // 2
                    c = cnt[:, 1 if blk == 1 else 0, :]
                    emptied(V.tensor_tensor(PT[:, blk, 4 * (k % 2):4 * (k % 2) + 4, :], bank(f"et{k}")[:, :].rearrange("p (h t) -> p h t", t=P),
                                            c.unsqueeze(1).to_broadcast([P, 4, P]), ALU.mult))
                for m in range(M):
                    for g in range(2):
                        wait_job(dve, L, f"ap{m}{g}")
                        o = bank(f"ap{m}{g}")[:, :].rearrange("p (h n) -> p h n", n=P)
                        rd = rden[:, m, 4 * g:4 * g + 4]
                        link(V.reciprocal(rd.unsqueeze(2), o[:, :, DH:DH + 1]))
                        y = xs[:, m, W + g * 256:W + (g + 1) * 256].rearrange("p (h d) -> p h d", d=DH)
                        emptied(V.tensor_tensor(y, o[:, :, 0:DH], rd.unsqueeze(2).to_broadcast([P, 4, DH]), ALU.mult))
                    wait_emptied(dve, L, f"ap{m}1")
                    V.tensor_copy(sm[:, 104:105], sm[:, 105:106]).then_inc(y_done, 1)

                def add_rows(t):
                    for n in range(2):
                        for m in range(M):
                            wait_job(dve, L, f"{t}{n}{m}")
                            xv = x[:, m, n * W:(n + 1) * W]
                            emptied(V.tensor_tensor(xv, bank(f"{t}{n}{m}")[:, :], xv, ALU.add))
                    wait_emptied(dve, L, f"{t}11")

                add_rows("wo")
                scale_rows(L, 1)
                rows_T("t3", 8)
                for m in range(M):
                    for g in range(2):
                        wait_job(dve, L, f"sx{m}{g}")
                        mv = xmx[:, m, 2 * g:2 * g + 2]
                        link(V.tensor_reduce(mv, bank(f"sx{m}{g}")[:, :].rearrange("p (h s) -> p h s", s=T), AX, ALU.max, negate=True))
                        V.tensor_scalar(mv, mv, X_DH ** -0.5, None, ALU.mult).then_inc(xmax_done, 1)
                for m in range(M):
                    for jb in range(2):
                        wait_job(dve, L, f"pt{m}{jb}")
                        emptied(V.tensor_copy(PTx[:, 2 * m + jb, :, :], bank(f"pt{m}{jb}")[:, :].rearrange("p (h t) -> p h t", t=P)))
                wait_emptied(dve, L, "sx11")
                link(V.reciprocal(xrd[:, :, :], xden[:, :, :]))
                for m in range(M):
                    for g in range(2):
                        wait_job(dve, L, f"px{m}{g}")
                        y = xs[:, m, g * W:(g + 1) * W].rearrange("p (h d) -> p h d", d=T)
                        emptied(V.tensor_tensor(y, bank(f"px{m}{g}")[:, :].rearrange("p (h d) -> p h d", d=T),
                                                xrd[:, m, 2 * g:2 * g + 2].unsqueeze(2).to_broadcast([P, 2, T]), ALU.mult))
                add_rows("ox")
                scale_rows(L, 2)
                rows_T("t5", 24)
                wait_job(dve, L, "rl")
                emptied(V.tensor_copy(logits[:, :, :], bank("rl")[:, 0:40].rearrange("p (m n) -> p m n", m=M)))
                wait_emptied(dve, L, "rl")
                link(V.tensor_copy(pad8[:, :, 0:N_GROUPS], logits[:, :, 0:N_GROUPS]))
                for m in range(M):
                    last = V.max(top8[:, m, :], pad8[:, m, :])
                link(last)
                V.tensor_scalar(ngmx.unsqueeze(2), top8[:, :, 0:1], -1.0, None, ALU.mult).then_inc(lmax_done, 1)
                for m in range(M):
                    last = V.max_index(idx8[:, m, :].bitcast(mybir.dt.uint32), top8[:, m, :], pad8[:, m, :])
                link(last)
                link(V.tensor_copy(idxf[:, :, :], idx8[:, :, :].bitcast(mybir.dt.uint32)))
                for m in range(M):
                    last = V.tensor_scalar(oneg[:, m, :], io16[:, 0:N_GROUPS], idxf[:, m, 0:1], None, ALU.is_equal)
                link(last)
                link(V.tensor_scalar(oneg[:, :, :], oneg[:, :, :], 1.0, -NEG, ALU.subtract, ALU.mult))
                for m in range(M):
                    last = V.tensor_tensor(elog[:, m, :].rearrange("p (g e) -> p g e", e=4),
                                           logits[:, m, N_GROUPS:].rearrange("p (g e) -> p g e", e=4),
                                           oneg[:, m, :].unsqueeze(2).to_broadcast([P, N_GROUPS, 4]), ALU.add)
                link(last)
                for m in range(M):
                    last = V.max(top8[:, m, :], elog[:, m, :])
                link(last)
                dve.wait_ge(lexp_done, 2 * L + 1)
                V.tensor_tensor(e2.unsqueeze(2), top8[:, :, 1:2], top8[:, :, 0:1], ALU.subtract).then_inc(lmax_done, 1)
                for m in range(M):
                    last = V.max_index(idx8[:, m, :].bitcast(mybir.dt.uint32), top8[:, m, :], elog[:, m, :])
                link(last)
                link(V.tensor_copy(idxf[:, :, :], idx8[:, :, :].bitcast(mybir.dt.uint32)))
                dve.wait_ge(lexp_done, 2 * L + 2)
                link(V.tensor_scalar(sc2, e2, 1.0, None, ALU.add))
                link(V.tensor_tensor(sc2, sc2, gsum, ALU.mult))
                link(V.reciprocal(w1, sc2))
                link(V.tensor_tensor(w2, w1, e2, ALU.mult))
                for m in range(M):
                    V.tensor_scalar(gates[:, m, :], io16, idxf[:, m, 0:1], w1[:, m:m + 1], ALU.is_equal, ALU.mult)
                    last = V.tensor_scalar(one1[:, m, :], io16, idxf[:, m, 1:2], w2[:, m:m + 1], ALU.is_equal, ALU.mult)
                link(last)
                V.tensor_tensor(gates[:, :, :], gates[:, :, :], one1[:, :, :], ALU.add).then_inc(gates_done, 1)
                dve.wait_ge(gates_done, L + 1)
                mixed = chain.n
                with dve.Fori(0, PAIRS) as p:
                    chain.enter(first + mixed + DVE_LINKS * L + DVE_PAIR_LINKS * p)
                    n4 = 4 * PAIRS * L + 4 * p + 4
                    moe = MOE_JOBS * PAIRS * L + MOE_JOBS * p + MOE_JOBS
                    for b2 in range(2):
                        for m in range(M):
                            dve.wait_ge(g_exp, n4 + 2 * b2 + m + 1)
                            g = gexp[:, m, :]
                            link(V.tensor_scalar(g, g, 1.0, None, ALU.add))
                            link(V.reciprocal(g, g))
                            link(V.tensor_tensor(g, banks[m][:, :], g, ALU.mult))
                            dve.wait_ge(moe_done, moe + 10 * b2 + 2 + m + 1)
                            V.tensor_tensor(actb[:, m, :], banks[2 + m][:, :], g, ALU.mult).then_inc(act_done, 1)
                        for m in range(M):
                            for n in range(2):
                                dve.wait_ge(moe_done, moe + 10 * b2 + 4 + 3 * m + 1 + n + 1)
                                xv = x[:, m, n * W:(n + 1) * W]
                                gate = gates[:, m, bass.ds(2 * p + b2, 1)]
                                V.scalar_tensor_tensor(xv, banks[5 + n][:, :], gate, xv, ALU.mult, ALU.add).then_inc(added, 1)
                    assert chain.n == DVE_PAIR_LINKS, f"DVE_PAIR_LINKS = {chain.n}"
                assert mixed + DVE_PAIR_LINKS * PAIRS == DVE_LINKS, f"DVE_LINKS = {mixed + DVE_PAIR_LINKS * PAIRS}"
            chain.enter(first + DVE_LINKS * DEPTH)
            dve.wait_ge(added, 8 * PAIRS * DEPTH + 8)
            dve.wait_ge(rstd_done, 3 * DEPTH + 1)
            dve.wait_ge(nf_loaded, 16)
            for m in range(M):
                V.scalar_tensor_tensor(xs[:, m, :], x[:, m, :], rstd[:, m:m + 1], Vx[:, 0, :], ALU.mult, ALU.mult).then_inc(fin_done, 1)


_INS = ["x", "mem", "positions", "inv", "gains", "hg_lower_bounds", "hg_out_norm", "w_in", "w_out", "wq_x", "wkv_x", "wo_x",
        "w_router", "w_gate", "w_up", "w_down", "norm_final"]


def kernel(**inputs):
    import numpy as _np
    import concourse.bacc as _bacc
    from concourse import mybir as _mybir
    from concourse.bass_utils import run_bass_kernel_spmd as _run

    a = {k: _np.ascontiguousarray(v) for k, v in inputs.items()}
    a["x"], a["mem"], a["positions"] = a["x"].reshape(T, D), a["mem"].reshape(T, D), a["positions"].reshape(T)
    a["inv"] = _np.power(_np.float32(ROPE_THETA), -_np.arange(0, DH, 2, dtype=_np.float32) / _np.float32(DH)).astype(_np.float32)
    a["gains"] = _np.stack([a.pop("norm_mix"), a.pop("norm_cross"), a.pop("norm_mem"), a.pop("norm_ffn")])
    a["w_router"] = _np.concatenate([a.pop("w_router_group"), a.pop("w_router_expert")], axis=2)
    for name in ("w_gate", "w_up", "w_down"):
        a[name] = a[name].reshape(DEPTH * N_EXPERTS, P, D * FF // P)
    nc = _bacc.Bacc("TRN2", target_bir_lowering=False, num_devices=1)
    arrays = {f"in_{n}": a[n] for n in _INS}
    args = [nc.dram_tensor(f"in_{n}", a[n].shape, _mybir.dt.from_np(a[n].dtype), kind="ExternalInput").ap() for n in _INS]
    out = nc.dram_tensor("out", (T, D), F32, kind="ExternalOutput").ap()
    trunk(nc, *args, out)
    r = _run(nc, [arrays], core_ids=[0])
    return r.results[0]["out"].reshape(1, T, D)
```

```python
from contextlib import ExitStack

import numpy as np

import concourse.bass as bass
from concourse import mybir

P = 128
ALU = mybir.AluOpType
ACT = mybir.ActivationFunctionType
F32 = mybir.dt.float32
I32 = mybir.dt.int32
BF16 = mybir.dt.bfloat16
AX = mybir.AxisListType.X

D = 1024
C = D // P
T = 256
M = T // P
DEPTH = 2
HG_HEADS = 4
ATT_HEADS = 8
DH = 64
X_HEADS = 4
X_DH = D // X_HEADS
N_GROUPS = 4
N_EXPERTS = 16
FF = 512
W = 512
NEG = -1.0e30
EPS = 1e-6
ROPE_THETA = 10000.0

SLOTS = 6
UNITS = ["hf", "hq", "hi", "aq", "ak", "av", "hg", "k0", "k1", "v0", "v1", "o0", "o1", "q0", "q1", "p0", "p1", "router"]
MIX_ROUNDS = len(UNITS) // SLOTS
PAIRS = N_EXPERTS // 2
ROUNDS = MIX_ROUNDS + PAIRS


def job_list():
    quarters = [(m, c) for m in range(M) for c in range(2)]
    jobs = [(f"t1_{m}{c}", "D") for m, c in quarters]
    for name, who in (("hf", "A"), ("hq", "A"), ("hi", "A"), ("aq", "D"), ("ak", "D"), ("av", "A"), ("hg", "D")):
        jobs += [(f"{name}{m}", who) for m in range(2)]
    jobs += [(f"{name}{m}", "A") for name in ("qT", "kT") for m in range(M)]
    for j in range(8):
        jobs += [(f"kv{j}", "A")] + [(f"lev{j}_{m}", "D") for m in range(M)]
    jobs += [("cross", "D")]
    jobs += [(f"s{k}", "D") for k in range(6)]
    jobs += [(f"hp{m}", "D") for m in range(M)]
    jobs += [(f"et{k}", "D") for k in range(6)]
    jobs += [(f"ap{m}{g}", "D") for m, g in quarters]
    jobs += [(f"t2_{m}{c}", "A") for m, c in quarters]
    jobs += [(f"wo{n}{m}", "D") for n in range(2) for m in range(M)]
    jobs += [(f"t3_{m}{c}", "D") for m, c in quarters]
    jobs += [(f"qx{k}", "A") for k in range(4)]
    jobs += [(f"sx{m}{g}", "A") for m, g in quarters]
    jobs += [(f"pt{m}{c}", "D") for m, c in quarters]
    jobs += [(f"px{m}{g}", "D") for m, g in quarters]
    jobs += [(f"t4_{m}{c}", "A") for m, c in quarters]
    jobs += [(f"ox{n}{m}", "D") for n in range(2) for m in range(M)]
    jobs += [(f"t5_{m}{c}", "D") for m, c in quarters]
    return jobs + [("rt", "A"), ("rl", "D"), ("rank", "D")]


JOBS = job_list()
NAMES = [n for n, _ in JOBS]
NJ = len(JOBS)
EMPTIER = dict(JOBS)
NTH = {n: sum(w == EMPTIER[n] for _, w in JOBS[:i + 1]) for i, (n, _) in enumerate(JOBS)}
EMPTIED = {w: sum(x == w for _, x in JOBS) for w in "AD"}
LAST_USE = {"hf": "hf1", "hq": "hq1", "hi": "hi1", "aq": "aq1", "ak": "ak1", "av": "av1", "hg": "hg1",
            "k0": "kv1", "k1": "kv3", "v0": "kv5", "v1": "kv7", "o0": "wo01", "o1": "wo11",
            "q0": "qx1", "q1": "qx3", "p0": "ox01", "p1": "ox11", "router": "rt"}
SCORES = [(0, (0, 2, 4, 6)), (0, (1, 3, 5, 7)), (1, (0, 2)), (1, (1, 3)), (1, (4, 6)), (1, (5, 7))]

CAP = 64
ROUTED_JOBS = 7
DENSE_JOBS = 20

DENSE_LINKS = 12
ROUTED_LINKS = 3


class Chain:

    def __init__(self, eng, sem, base=0):
        self.eng, self.sem, self.base, self.n = eng, sem, base, 0

    def link(self, ins):
        self.n += 1
        ins.then_inc(self.sem, 1)
        self.eng.wait_ge(self.sem, self.base + self.n)


def trunk(nc, x_in, mem_in, pos_in, inv_in, gains_in, lb_in, og_in, w_in, w_out, wq, wkv, wo, w_router,
          w_gate, w_up, w_down, nf_in, rows_to, rows_from, out):
    ctx = ExitStack()
    with ctx:
        def sb(name, shape, dt=F32):
            return ctx.enter_context(nc.sbuf_tensor(name, shape, dt))

        def sem(name):
            return ctx.enter_context(nc.semaphore(name))

        ring = sb("ring", [P, SLOTS, 4096])
        x = sb("x", [P, M, D])
        xs = sb("xs", [P, M, D])
        hT = sb("hT", [P, C, T])
        memT = sb("memT", [P, C, T])
        hi = sb("hi", [P, M, W])
        gg = sb("gg", [P, M, W])
        rot = sb("rot", [P, 4 * W])
        vaug = sb("vaug", [P, M, ATT_HEADS, DH + 1])
        work = sb("work", [P, 4, HG_HEADS * T])
        S = sb("S", [P, M, HG_HEADS, P])
        PT = sb("PT", [P, 3, ATT_HEADS, P])
        S01 = PT[:, 2, 0:HG_HEADS, :]
        KT = sb("KT", [P, 8, T])
        Vx = sb("Vx", [P, M, D])
        lev = sb("lev", [P, 8, P])
        bias0 = sb("bias0", [P, P])
        bias10 = sb("bias10", [P, P])
        cnt = sb("cnt", [P, 2, P])
        ident = sb("ident", [P, P])
        gains = sb("gains", [P, DEPTH, 40])
        cur = sb("cur", [P, 40])
        og = sb("og", [P, W])
        cosT = sb("cosT", [P, M, 32])
        sinT = sb("sinT", [P, M, 32])
        sm = sb("sm", [P, 112])
        wsm = sb("wsm", [P, 242])
        early = PT[:, 2, 6:8, :].rearrange("p a t -> p (a t)")
        gates = sb("gates", [P, M, N_EXPERTS])
        before = sb("before", [P, P], BF16)
        ones = sb("ones", [P, P], BF16)
        chosen = sb("chosen", [P, M, N_EXPERTS], BF16)

        Q = work[:, 0, :].rearrange("p (a t) -> p a t", a=HG_HEADS)
        K = work[:, 1, :].rearrange("p (a t) -> p a t", a=HG_HEADS)
        F = work[:, 2, :].rearrange("p (a t) -> p a t", a=HG_HEADS)
        TOT = work[:, 3, :].rearrange("p (a t) -> p a t", a=HG_HEADS)
        E = work[:, :, :].rearrange("p a b -> p (a b)")
        attT = xs[:, :, :].rearrange("p a (g t) -> p (a g) t", t=T)
        QxT = rot[:, :].rearrange("p (n t) -> p n t", t=T)
        Px = work[:, 0:2, :].rearrange("p m (h s) -> p m h s", s=T)
        PTx = PT[:, 0:2, :, :].rearrange("p a (b h) t -> p (a b) h t", h=HG_HEADS)
        ss = sm[:, 0:2]
        rstd = sm[:, 2:4]
        hss = sm[:, 4:12].rearrange("p (m h) -> p m h", m=M)
        hrs = sm[:, 12:20].rearrange("p (m h) -> p m h", m=M)
        nmx = sm[:, 20:36]
        rden = sm[:, 36:52].rearrange("p (m h) -> p m h", m=M)
        xmx = sm[:, 52:60].rearrange("p (m h) -> p m h", m=M)
        xden = sm[:, 60:68].rearrange("p (m h) -> p m h", m=M)
        xrd = sm[:, 68:76].rearrange("p (m h) -> p m h", m=M)
        expo = sm[:, 76:84]
        mss = sm[:, 84:86]
        mrs = sm[:, 86:88]
        msq = sm[:, 88:96]
        posf = sm[:, 96:98]
        sq = rot[:, 0:D]

        banks = [ctx.enter_context(nc.psum_tensor(f"bank{i}", [P, W], F32)) for i in range(8)]

        loaded = [sem(f"loaded{s}") for s in range(SLOTS)]
        x_loaded, mem_loaded, small_loaded = sem("x_loaded"), sem("mem_loaded"), sem("small_loaded")
        og_loaded, nf_loaded = sem("og_loaded"), sem("nf_loaded")
        iota_done, masks_done, tables_done = sem("iota_done"), sem("masks_done"), sem("tables_done")
        zeroed = sem("zeroed")
        ident_done = sem("ident_done")
        mem_sq, mem_rstd, mem_scaled, mem_tr, mem_kept = (sem(n) for n in ("mem_sq", "mem_rstd", "mem_scaled", "mem_tr", "mem_kept"))
        trig_arg = sem("trig_arg")
        lb_exp = sem("lb_exp")
        lb_max = sem("lb_max")
        gains_done = sem("gains_done")
        cur_done = sem("cur_done")
        job_done = sem("job_done")
        empt = {"A": sem("emptied_by_scalar"), "D": sem("emptied_by_vector")}
        sq_done = sem("sq_done")
        rstd_done = sem("rstd_done")
        normed = sem("normed")
        f_done = sem("f_done")
        q_done = sem("q_done")
        k_done = sem("k_done")
        tot_done = sem("tot_done")
        rot_done = sem("rot_done")
        gate_exp = sem("gate_exp")
        memg_done = sem("memg_done")
        max_done = sem("max_done")
        e_done = sem("e_done")
        hsq_done = sem("hsq_done")
        hms_done = sem("hms_done")
        hrs_done = sem("hrs_done")
        y_done = sem("y_done")
        xmax_done = sem("xmax_done")
        lexp_done = sem("lexp_done")
        lmax_done = sem("lmax_done")
        chosen_done = sem("chosen_done")
        flag_done = sem("flag_done")
        slots_read = sem("slots_read")
        x_done = sem("x_done")
        rows_zeroed = sem("rows_zeroed")

        def per_layer(name):
            return [sem(f"{name}{l}") for l in range(DEPTH)]

        d_jobs = per_layer("d_jobs")
        d_gexp = per_layer("d_gexp")
        d_act = per_layer("d_act")
        d_actT = per_layer("d_actT")
        d_added = per_layer("d_added")
        d_chain = per_layer("d_chain")
        r_sent = per_layer("r_sent")
        r_rows = per_layer("r_rows")
        r_jobs = per_layer("r_jobs")
        r_rowsT = per_layer("r_rowsT")
        r_gexp = per_layer("r_gexp")
        r_act = per_layer("r_act")
        r_actT = per_layer("r_actT")
        r_kept = per_layer("r_kept")
        r_stored = per_layer("r_stored")
        r_back = per_layer("r_back")
        r_chain = per_layer("r_chain")
        dve_chain, pool_chain, act_chain = sem("dve_chain"), sem("pool_chain"), sem("act_chain")
        fin_done, out_done = sem("fin_done"), sem("out_done")

        def bank(name):
            return banks[NAMES.index(name) % 8]

        def wait_job(eng, L, name):
            eng.wait_ge(job_done, L * NJ + NAMES.index(name) + 1)

        def wait_emptied(eng, L, name):
            who = EMPTIER[name]
            eng.wait_ge(empt[who], L * EMPTIED[who] + NTH[name])

        def unit_source(L, u):
            name = UNITS[u]
            starts = {"hq": 0, "hf": 512, "hi": 1024, "hg": 1536, "aq": 2048, "ak": 2560, "av": 3072}
            if name in starts:
                t, n0 = w_in, starts[name]
            elif name == "router":
                return w_router[bass.ds(L, 1), :, :].rearrange("l (p c) n -> p (l c) n", c=C), N_GROUPS + N_EXPERTS
            else:
                t, n0 = {"k0": (wkv, 0), "k1": (wkv, 512), "v0": (wkv, 1024), "v1": (wkv, 1536), "o0": (w_out, 0),
                         "o1": (w_out, 512), "q0": (wq, 0), "q1": (wq, 512), "p0": (wo, 0), "p1": (wo, 512)}[name]
            return t[bass.ds(L, 1), :, n0:n0 + W].rearrange("l (p c) n -> p (l c) n", c=C), W

        def unit(name, n=W):
            return ring[:, UNITS.index(name) % SLOTS, 0:C * n].rearrange("p (c n) -> p c n", c=C)

        tots = []
        off = 0
        for j in range(1, 7):
            tots.append(TOT[:, :, off:off + (T >> j)])
            off += T >> j

        actb = work[:, 0, :].rearrange("p (m n) -> p m n", m=M)
        actT = work[:, 1, 0:W].rearrange("p (c t) -> p c t", c=4)
        gexp = work[:, 2, :].rearrange("p (m n) -> p m n", m=M)
        HALF_PI = float(np.pi / 2)

        logits = wsm[:, 0:40].rearrange("p (m n) -> p m n", m=M)
        ngmx = wsm[:, 40:42]
        gsum = wsm[:, 42:44]
        lexp = wsm[:, 44:52].rearrange("p (m n) -> p m n", m=M)
        e2 = wsm[:, 52:54]
        pad8 = wsm[:, 56:72].rearrange("p (m n) -> p m n", m=M)
        top8 = wsm[:, 72:88].rearrange("p (m n) -> p m n", m=M)
        idx8 = wsm[:, 88:104].rearrange("p (m n) -> p m n", m=M)
        oneg = wsm[:, 104:112].rearrange("p (m n) -> p m n", m=M)
        elog = wsm[:, 112:144].rearrange("p (m n) -> p m n", m=M)
        idxf = wsm[:, 144:160].rearrange("p (m n) -> p m n", m=M)
        io16 = wsm[:, 160:176]
        slotf = wsm[:, 216:220].rearrange("p (m k) -> p m k", m=M)
        slots = wsm[:, 220:224].bitcast(I32).rearrange("p (m k) -> p m k", m=M)
        base16 = wsm[:, 224:240]
        mostf = wsm[:, 240:241]
        most = wsm[:, 241:242].bitcast(I32)
        one2 = PT[:, 1, 0, 0:64].rearrange("p (m k n) -> p m k n", m=M, k=2)
        pick = PT[:, 1, 0, 64:128].rearrange("p (m k n) -> p m k n", m=M, k=2)
        rank = PT[:, 1, 1, 0:32].rearrange("p (m n) -> p m n", m=M)
        rows = KT[:, 0:4, :].rearrange("p a t -> p (a t)")
        rowsT = hT[:, :, 0:P]
        ract, ractT, rexp = work[:, 0, 0:W], work[:, 1, 0:W].rearrange("p (c t) -> p c t", c=4), work[:, 2, 0:W]
        yrows = Vx[:, 0, :]
        back = work[:, :, :].rearrange("p (m k) n -> p m k n", m=M)
        w1 = wsm[:, 176:178]
        w2 = wsm[:, 178:180]
        sc2 = wsm[:, 180:182]
        one1 = wsm[:, 184:216].rearrange("p (m n) -> p m n", m=M)

        def either_way(eng, L, routed, dense, routed_first=None, routed_last=None, dense_first=None, dense_last=None):
            eng.wait_ge(flag_done, L + 1)
            fullest = eng.value_load(most[0:1, 0:1], min_val=0, max_val=T)
            with eng.If(fullest <= CAP):
                if routed_first:
                    routed_first()
                with eng.Fori(0, PAIRS) as p:
                    routed(p)
                if routed_last:
                    routed_last()
            with eng.Else():
                if dense_first:
                    dense_first()
                with eng.Fori(0, PAIRS) as p:
                    dense(p)
                if dense_last:
                    dense_last()

        block = ctx.enter_context(nc.Block())

        @block.sync
        def _(sp):
            for L in range(DEPTH):
                for u, name in enumerate(UNITS):
                    s = u % SLOTS
                    if u < SLOTS:
                        if L:
                            sp.wait_ge(slots_read, 3 * PAIRS * L + s // 2 + 1)
                    else:
                        wait_job(sp, L, LAST_USE[UNITS[u - SLOTS]])
                    src, n = unit_source(L, u)
                    sp.dma_start(unit(name, n), src).then_inc(loaded[s], 16)
                with sp.Fori(0, PAIRS) as p:
                    for s in range(SLOTS):
                        e = sp.snap(2 * p + N_EXPERTS * L + s % 2)
                        wait_job(sp, L, LAST_USE[UNITS[(MIX_ROUNDS - 1) * SLOTS + s]])
                        sp.wait_ge(slots_read, 3 * PAIRS * L + s // 2 + 1 + 3 * p)
                        w = (w_gate, w_up, w_down)[s // 2]
                        sp.dma_start(ring[:, s, :], w[bass.ds(e, 1), :, :].rearrange("e p n -> p (e n)"))\
                          .then_inc(loaded[s], 16)

        @block.tensor
        def _(pe):
            def wait_unit(L, name):
                u = UNITS.index(name)
                pe.wait_ge(loaded[u % SLOTS], 16 * ROUNDS * L + 16 * (u // SLOTS + 1))

            def open_bank(L, name):
                i = NAMES.index(name)
                if i >= 8:
                    wait_emptied(pe, L, NAMES[i - 8])
                return banks[i % 8]

            def close(ins):
                ins.then_inc(job_done, 1)

            def transposes(L, name, src, rows=P):
                b = open_bank(L, name)
                for k, s in enumerate(src):
                    last = nc.tensor.transpose(b[:, k * P:(k + 1) * P], s, ident[:, :])
                close(last)

            def by_columns(src, m, c2):
                v = src[:, m, :].rearrange("p (k c) -> p c k", c=C)
                return [v[:, 4 * c2 + k, :] for k in range(4)]

            def project(L, name, lhs, m, w):
                b = open_bank(L, name)
                for c in range(C):
                    last = nc.tensor.matmul(b[:, :], lhs[:, c, m * P:(m + 1) * P], w[:, c, :], start=(c == 0), stop=(c == C - 1))
                close(last)

            def project_T(L, name, rhs, w, n2):
                b = open_bank(L, name)
                for k in range(2):
                    for c in range(C):
                        last = nc.tensor.matmul(b[:, k * T:(k + 1) * T], w[:, c, (n2 + k) * P:(n2 + k + 1) * P],
                                                rhs[:, c, :], start=(c == 0), stop=(c == C - 1))
                close(last)

            pe.wait_ge(ident_done, 2)
            pe.wait_ge(mem_scaled, 2)
            memrow = E[:, 0:M * D].rearrange("p (m d) -> p m d", m=M)
            for m in range(M):
                for c2 in range(2):
                    b = banks[4 + 2 * m + c2]
                    for k, s in enumerate(by_columns(memrow, m, c2)):
                        last = nc.tensor.transpose(b[:, k * P:(k + 1) * P], s, ident[:, :])
                    last.then_inc(mem_tr, 1)
            pe.wait_ge(mem_kept, 4)

            for L in range(DEPTH):
                for m in range(M):
                    pe.wait_ge(normed, 6 * L + m + 1)
                    for c2 in range(2):
                        transposes(L, f"t1_{m}{c2}", by_columns(xs, m, c2))
                wait_emptied(pe, L, "t1_11")
                for name in ("hf", "hq"):
                    wait_unit(L, name)
                    for k in range(2):
                        project_T(L, f"{name}{k}", hT, unit(name), 2 * k)
                for name in ("hi", "aq", "ak", "av", "hg"):
                    wait_unit(L, name)
                    for m in range(M):
                        project(L, f"{name}{m}", hT, m, unit(name))
                for w, name in enumerate(("qT", "kT")):
                    for m in range(M):
                        pe.wait_ge(rot_done, 4 * L + 2 * w + m + 1)
                        r = rot[:, (2 * w + m) * W:(2 * w + m + 1) * W]
                        transposes(L, f"{name}{m}", [r[:, k * P:(k + 1) * P] for k in range(4)])
                pe.wait_ge(memg_done, L + 1)
                for j in range(8):
                    if j < 4:
                        wait_unit(L, f"k{j // 2}")
                        project_T(L, f"kv{j}", hT, unit(f"k{j // 2}"), 2 * (j % 2))
                    else:
                        wait_unit(L, f"v{(j - 4) // 2}")
                        project(L, f"kv{j}", hT, j % 2, unit(f"v{(j - 4) // 2}"))
                    if j == 0:
                        pe.wait_ge(f_done, 2 * L + 2)
                        wait_emptied(pe, L, "hq1")
                    for m in range(M):
                        if j >= 1:
                            pe.wait_ge(q_done, 16 * L + 2 * (j - 1) + m + 1)
                        if j >= 2:
                            pe.wait_ge(k_done, 14 * L + 2 * (j - 2) + m + 1)
                        b = open_bank(L, f"lev{j}_{m}")
                        for a in range(HG_HEADS):
                            last = nc.tensor.matmul(b[:, a * P:(a + 1) * P], K[:, a, m * P:(m + 1) * P],
                                                    Q[:, a, m * P:(m + 1) * P], start=True, stop=True)
                        close(last)
                pe.wait_ge(q_done, 16 * L + 16)
                pe.wait_ge(k_done, 14 * L + 14)
                b = open_bank(L, "cross")
                for a in range(HG_HEADS):
                    last = nc.tensor.matmul(b[:, a * P:(a + 1) * P], K[:, a, 0:P], Q[:, a, P:T], start=True, stop=True)
                close(last)
                wait_emptied(pe, L, "kT1")
                for k, (m, heads) in enumerate(SCORES):
                    n = (m + 1) * P
                    b = open_bank(L, f"s{k}")
                    for i, h in enumerate(heads):
                        r = 64 * (h % 2)
                        last = nc.tensor.matmul(b[:, i * n:(i + 1) * n], attT[r:r + 64, h // 2, m * P:(m + 1) * P],
                                                attT[r:r + 64, 4 + h // 2, 0:n], start=True, stop=True)
                    close(last)
                wait_emptied(pe, L, "cross")
                wait_emptied(pe, L, "hi1")
                for m in range(M):
                    b = open_bank(L, f"hp{m}")
                    for a in range(HG_HEADS):
                        o = b[:, a * P:(a + 1) * P]
                        last = nc.tensor.matmul(o, S[:, m, a, :], hi[:, m, a * P:(a + 1) * P], start=True, stop=(m == 0))
                        if m:
                            last = nc.tensor.matmul(o, S01[:, a, :], hi[:, 0, a * P:(a + 1) * P], start=False, stop=True)
                    close(last)
                for k in range(6):
                    if k == 0:
                        pe.wait_ge(e_done, 6 * L + 2)
                    if k == 2:
                        pe.wait_ge(e_done, 6 * L + 6)
                    if k < 2:
                        src = [E[:, (4 * k + i) * P:(4 * k + i + 1) * P] for i in range(4)]
                    else:
                        jb, h0 = (k - 2) // 2, 4 * (k % 2)
                        src = [E[:, D + (h0 + i) * T + jb * P:D + (h0 + i) * T + (jb + 1) * P] for i in range(4)]
                    transposes(L, f"et{k}", src)
                wait_emptied(pe, L, "av1")
                for m in range(M):
                    for g in range(2):
                        wait_emptied(pe, L, f"et{g}" if m == 0 else f"et{4 + g}")
                        b = open_bank(L, f"ap{m}{g}")
                        for i in range(4):
                            h = 4 * g + i
                            o = b[:, i * P:i * P + DH + 1]
                            last = nc.tensor.matmul(o, PT[:, 2 * m, h, :], vaug[:, m, h, :], start=True, stop=(m == 0))
                            if m:
                                last = nc.tensor.matmul(o, PT[:, 1, h, :], vaug[:, 0, h, :], start=False, stop=True)
                        close(last)
                for m in range(M):
                    pe.wait_ge(y_done, 4 * L + 2 + m + 1)
                    for c2 in range(2):
                        transposes(L, f"t2_{m}{c2}", by_columns(xs, m, c2))
                wait_emptied(pe, L, "t2_11")
                for n in range(2):
                    wait_unit(L, f"o{n}")
                    for m in range(M):
                        project(L, f"wo{n}{m}", hT, m, unit(f"o{n}"))
                for m in range(M):
                    pe.wait_ge(normed, 6 * L + 2 + m + 1)
                    for c2 in range(2):
                        transposes(L, f"t3_{m}{c2}", by_columns(xs, m, c2))
                wait_emptied(pe, L, "t3_11")
                for k in range(4):
                    wait_unit(L, f"q{k // 2}")
                    project_T(L, f"qx{k}", hT, unit(f"q{k // 2}"), 2 * (k % 2))
                wait_emptied(pe, L, "qx3")
                for m in range(M):
                    for g in range(2):
                        b = open_bank(L, f"sx{m}{g}")
                        for i in range(2):
                            h = 2 * g + i
                            for k in range(2):
                                last = nc.tensor.matmul(b[:, i * T:(i + 1) * T], QxT[:, 2 * h + k, m * P:(m + 1) * P],
                                                        KT[:, 2 * h + k, :], start=(k == 0), stop=(k == 1))
                        close(last)
                for m in range(M):
                    wait_emptied(pe, L, f"sx{m}1")
                    for jb in range(2):
                        transposes(L, f"pt{m}{jb}", [Px[:, m, h, jb * P:(jb + 1) * P] for h in range(X_HEADS)])
                for m in range(M):
                    wait_emptied(pe, L, f"pt{m}1")
                    for g in range(2):
                        b = open_bank(L, f"px{m}{g}")
                        for i in range(2):
                            h = 2 * g + i
                            for jb in range(2):
                                last = nc.tensor.matmul(b[:, i * T:(i + 1) * T], PTx[:, 2 * m + jb, h, :],
                                                        Vx[:, jb, h * T:(h + 1) * T], start=(jb == 0), stop=(jb == 1))
                        close(last)
                for m in range(M):
                    wait_emptied(pe, L, f"px{m}1")
                    for c2 in range(2):
                        transposes(L, f"t4_{m}{c2}", by_columns(xs, m, c2))
                wait_emptied(pe, L, "t4_11")
                for n in range(2):
                    wait_unit(L, f"p{n}")
                    for m in range(M):
                        project(L, f"ox{n}{m}", hT, m, unit(f"p{n}"))
                for m in range(M):
                    pe.wait_ge(normed, 6 * L + 4 + m + 1)
                    for c2 in range(2):
                        transposes(L, f"t5_{m}{c2}", by_columns(xs, m, c2))
                wait_emptied(pe, L, "t5_11")
                NR = N_GROUPS + N_EXPERTS
                wait_unit(L, "router")
                b = open_bank(L, "rt")
                for c in range(C):
                    last = nc.tensor.matmul(b[0:NR, 0:T], unit("router", NR)[:, c, :], hT[:, c, :], start=(c == 0), stop=(c == C - 1))
                close(last)
                wait_emptied(pe, L, "rt")
                b = open_bank(L, "rl")
                for m in range(M):
                    last = nc.tensor.transpose(b[:, m * NR:(m + 1) * NR], early[0:NR, m * P:(m + 1) * P], ident[0:NR, 0:NR])
                close(last)
                pe.wait_ge(chosen_done, L + 1)
                b = open_bank(L, "rank")
                NE = N_EXPERTS
                nc.tensor.matmul(b[:, 0:NE], before[:, :], chosen[:, 0, :], start=True, stop=True)
                nc.tensor.matmul(b[:, NE:2 * NE], before[:, :], chosen[:, 1, :], start=True, stop=False)
                nc.tensor.matmul(b[:, NE:2 * NE], ones[:, :], chosen[:, 0, :], start=False, stop=True)
                nc.tensor.matmul(b[:, 2 * NE:3 * NE], ones[:, :], chosen[:, 0, :], start=True, stop=False)
                close(nc.tensor.matmul(b[:, 2 * NE:3 * NE], ones[:, :], chosen[:, 1, :], start=False, stop=True))

                def fill(p, s):
                    pe.wait_ge(loaded[s], 16 * ROUNDS * L + 16 * p + 16 * (MIX_ROUNDS + 1))

                def routed(p):
                    def job(last):
                        last.then_inc(r_jobs[L], 1)

                    pe.wait_ge(r_rows[L], 16 * p + 16)
                    rv = rows.rearrange("p (k c) -> p c k", c=C)
                    for c2 in range(2):
                        for k in range(4):
                            last = nc.tensor.transpose(banks[c2][:, k * P:(k + 1) * P], rv[:, 4 * c2 + k, :], ident[:, :])
                        job(last)
                    pe.wait_ge(r_rowsT[L], 2 * p + 2)
                    for g in range(2):
                        for b2 in range(2):
                            fill(p, 2 * g + b2)
                        for c in range(C):
                            for b2 in range(2):
                                w = ring[:, 2 * g + b2, c * W:(c + 1) * W]
                                last = nc.tensor.matmul(banks[2 + g][b2 * CAP:(b2 + 1) * CAP, :], rowsT[:, c, b2 * CAP:(b2 + 1) * CAP],
                                                        w, start=(c == 0), stop=(c == C - 1))
                        job(last)
                    pe.wait_ge(r_act[L], p + 1)
                    av = ract.rearrange("p (k c) -> p c k", c=4)
                    for k in range(4):
                        last = nc.tensor.transpose(banks[4][:, k * P:(k + 1) * P], av[:, k, :], ident[:, :])
                    job(last)
                    pe.wait_ge(r_actT[L], p + 1)
                    for b2 in range(2):
                        fill(p, 4 + b2)
                    pe.wait_ge(r_kept[L], 2 * p + 2)
                    for n in range(2):
                        for c in range(4):
                            for b2 in range(2):
                                w = ring[:, 4 + b2, c * D + n * W:c * D + (n + 1) * W]
                                last = nc.tensor.matmul(banks[5 + n][b2 * CAP:(b2 + 1) * CAP, :], ractT[:, c, b2 * CAP:(b2 + 1) * CAP],
                                                        w, start=(c == 0), stop=(c == 3))
                        job(last)

                def dense(p):
                    n4 = 4 * p + 4
                    for b2 in range(2):
                        for s in (b2, 2 + b2):
                            fill(p, s)
                            w = ring[:, s, :].rearrange("p (c n) -> p c n", c=C)
                            for m in range(M):
                                if s < 2:
                                    pe.wait_ge(d_act[L], n4 + 2 * b2)
                                for c in range(C):
                                    last = nc.tensor.matmul(banks[(0 if s < 2 else 2) + m][:, :], hT[:, c, m * P:(m + 1) * P],
                                                            w[:, c, :], start=(c == 0), stop=(c == C - 1))
                                last.then_inc(d_jobs[L], 1)
                        for m in range(M):
                            pe.wait_ge(d_act[L], n4 + 2 * b2 + m + 1)
                            pe.wait_ge(d_actT[L], n4 + 2 * b2 + m)
                            av = actb[:, m, :].rearrange("p (k c) -> p c k", c=4)
                            for k in range(4):
                                last = nc.tensor.transpose(banks[4][:, k * P:(k + 1) * P], av[:, k, :], ident[:, :])
                            last.then_inc(d_jobs[L], 1)
                            pe.wait_ge(d_actT[L], n4 + 2 * b2 + m + 1)
                            if m == 0:
                                fill(p, 4 + b2)
                            w = ring[:, 4 + b2, :].rearrange("p (c n) -> p c n", c=4)
                            for n in range(2):
                                pe.wait_ge(d_added[L], 2 * n4 + 4 * b2 + 2 * m)
                                for c in range(4):
                                    last = nc.tensor.matmul(banks[5 + n][:, :], actT[:, c, :], w[:, c, n * W:(n + 1) * W],
                                                            start=(c == 0), stop=(c == 3))
                                last.then_inc(d_jobs[L], 1)

                either_way(pe, L, routed, dense)

        @block.scalar
        def _(act):
            for l in range(DEPTH):
                act.sem_inc(d_actT[l], 4)
                act.sem_inc(r_kept[l], 2)
                act.sem_inc(r_stored[l], 16)
            act.dma_start(x[:, :, :], x_in.rearrange("(m p) d -> p m d", p=P)).then_inc(x_loaded, 16)
            act.dma_start(E[:, 0:M * D].rearrange("p (m d) -> p m d", m=M), mem_in.rearrange("(m p) d -> p m d", p=P))\
               .then_inc(mem_loaded, 16)
            with nc.allow_non_contiguous_dma(reason="small vectors, once"):
                for l in range(DEPTH):
                    act.dma_start(gains[:, l, 0:32].rearrange("p (g c) -> p g c", g=4),
                                  gains_in[:, l, :].rearrange("g (p c) -> p g c", c=C)).then_inc(small_loaded, 16)
                    act.dma_start(gains[:, l, 32:36], lb_in[l, :].rearrange("(h p) -> p h", p=P)).then_inc(small_loaded, 16)
                act.dma_start(early[:, 0:M].bitcast(I32), pos_in.rearrange("(m p) -> p m", p=P)).then_inc(small_loaded, 16)
                act.dma_start(early[:, 64:96], inv_in.partition_broadcast(P)).then_inc(small_loaded, 16)
            act.wait_ge(mem_loaded, 16)
            act.wait_ge(zeroed, 1)
            for m in range(M):
                nc.scalar.activation(sq, E[:, m * D:(m + 1) * D], ACT.Square, accum_out=mss[:, m:m + 1]).then_inc(mem_sq, 1)
                act.wait_ge(mem_sq, m + 1)
            act.wait_ge(lb_max, 1)
            nc.scalar.activation(gains[:, :, 36:40], gains[:, :, 36:40], ACT.Exp).then_inc(lb_exp, 1)
            act.wait_ge(trig_arg, 1)
            nc.scalar.activation(cosT[:, :, :], cosT[:, :, :], ACT.Sin)
            nc.scalar.activation(sinT[:, :, :], sinT[:, :, :], ACT.Sin).then_inc(tables_done, 1)

            def squares(count):
                for m in range(M):
                    nc.scalar.activation(sq, x[:, m, :], ACT.Square, accum_out=ss[:, m:m + 1]).then_inc(sq_done, 1)
                    act.wait_ge(sq_done, count + m + 1)

            act.wait_ge(x_loaded, 16)
            for L in range(DEPTH):
                act.wait_ge(x_done, L)
                act.wait_ge(y_done, 4 * L)
                with nc.allow_non_contiguous_dma(reason="one row to all partitions"):
                    act.dma_start(og[:, :], og_in[bass.ds(L, 1), :].rearrange("l n -> (l n)").partition_broadcast(P)).then_inc(og_loaded, 16)
                squares(6 * L)

                def empty(name, dst, func=ACT.Copy, scale=1.0, view=None):
                    wait_job(act, L, name)
                    src = bank(name)[:, :] if view is None else view
                    nc.scalar.activation(dst, src, func, scale=scale).then_inc(empt["A"], 1)

                def halves(name):
                    return bank(name)[:, :].rearrange("p (a t) -> p a t", a=2)

                for k in range(2):
                    empty(f"hf{k}", F[:, 2 * k:2 * k + 2, :], ACT.Exp, -1.0, halves(f"hf{k}"))
                if L == 0:
                    act.wait_ge(zeroed, 2)
                    for p in range(PAIRS + 1):
                        act.dma_start(rows_to[p * P:(p + 1) * P, :], S[:, :, :, :].rearrange("p m a t -> p (m a t)")).then_inc(rows_zeroed, 16)
                for k in range(2):
                    empty(f"hq{k}", Q[:, 2 * k:2 * k + 2, :], view=halves(f"hq{k}"))
                for m in range(M):
                    empty(f"hi{m}", hi[:, m, :])
                for m in range(M):
                    empty(f"av{m}", vaug[:, m, :, 0:DH], view=bank(f"av{m}")[:, :].rearrange("p (h d) -> p h d", d=DH))
                for m in range(M):
                    wait_job(act, L, f"hg{m}")
                    nc.scalar.activation(gg[:, m, :], bank(f"hg{m}")[:, :], ACT.Exp, scale=-1.0).then_inc(gate_exp, 1)
                for w, name in enumerate(("qT", "kT")):
                    for m in range(M):
                        empty(f"{name}{m}", attT[:, 4 * w:4 * w + 4, m * P:(m + 1) * P], scale=(DH ** -0.5 if w == 0 else 1.0),
                              view=bank(f"{name}{m}")[:, :].rearrange("p (g t) -> p g t", t=P))
                for j in range(8):
                    if j < 4:
                        empty(f"kv{j}", KT[:, 2 * j:2 * j + 2, :], view=halves(f"kv{j}"))
                    else:
                        empty(f"kv{j}", Vx[:, j % 2, ((j - 4) // 2) * W:((j - 4) // 2 + 1) * W])
                at = 0
                for k, (m, heads) in enumerate(SCORES):
                    act.wait_ge(max_done, 6 * L + k + 1)
                    n = (m + 1) * P
                    for h in heads:
                        e = E[:, m * D + h * n:m * D + (h + 1) * n]
                        last = nc.scalar.activation(e, e, ACT.Exp, bias=nmx[:, at:at + 1])
                        at += 1
                    last.then_inc(e_done, 1)
                for m in range(M):
                    wait_job(act, L, f"hp{m}")
                    nc.scalar.activation(rot[:, m * W:(m + 1) * W], bank(f"hp{m}")[:, :], ACT.Square).then_inc(hsq_done, 1)

                def rows_T(t):
                    for m in range(M):
                        for c2 in range(2):
                            empty(f"{t}_{m}{c2}", hT[:, 4 * c2:4 * c2 + 4, m * P:(m + 1) * P],
                                  view=bank(f"{t}_{m}{c2}")[:, :].rearrange("p (c t) -> p c t", c=4))

                wait_job(act, L, "kv7")
                rows_T("t2")
                wait_emptied(act, L, "wo11")
                squares(6 * L + 2)
                act.wait_ge(hms_done, 2 * L + 2)
                for k in range(4):
                    empty(f"qx{k}", QxT[:, 2 * k:2 * k + 2, :], view=halves(f"qx{k}"))
                for m in range(M):
                    for g in range(2):
                        act.wait_ge(xmax_done, 4 * L + 2 * m + g + 1)
                        for i in range(2):
                            h = 2 * g + i
                            last = nc.scalar.activation(Px[:, m, h, :], bank(f"sx{m}{g}")[:, i * T:(i + 1) * T], ACT.Exp,
                                                        bias=xmx[:, m, h:h + 1], scale=X_DH ** -0.5, accum_out=xden[:, m, h:h + 1])
                        last.then_inc(empt["A"], 1)
                rows_T("t4")
                wait_emptied(act, L, "ox11")
                squares(6 * L + 4)
                empty("rt", early[0:20, 0:T], view=bank("rt")[0:20, 0:T])
                act.wait_ge(lmax_done, 2 * L + 1)
                for m in range(M):
                    last = nc.scalar.activation(lexp[:, m, :], logits[:, m, 0:N_GROUPS], ACT.Exp, bias=ngmx[:, m:m + 1],
                                                accum_out=gsum[:, m:m + 1])
                last.then_inc(lexp_done, 1)
                act.wait_ge(lmax_done, 2 * L + 2)
                nc.scalar.activation(e2[:, :], e2[:, :], ACT.Exp).then_inc(lexp_done, 1)

                def load_rows(p):
                    act.dma_start(rows, rows_to[bass.ds(p * P, P), :]).then_inc(r_rows[L], 16)

                def routed(p):
                    jobs = ROUTED_JOBS * p
                    following = act.snap(p + 1)
                    act.wait_ge(r_jobs[L], jobs + 2)
                    load_rows(following)
                    act.wait_ge(r_jobs[L], jobs + 3)
                    nc.scalar.activation(rexp, banks[2][:, :], ACT.Exp, scale=-1.0).then_inc(r_gexp[L], 1)
                    act.wait_ge(r_jobs[L], jobs + 5)
                    nc.scalar.activation(ractT, banks[4][:, :].rearrange("p (c t) -> p c t", c=4), ACT.Copy).then_inc(r_actT[L], 1)
                    act.wait_ge(r_stored[L], 16 * p + 16)
                    for n in range(2):
                        act.wait_ge(r_jobs[L], jobs + 6 + n)
                        nc.scalar.activation(yrows[:, n * W:(n + 1) * W], banks[5 + n][:, :], ACT.Copy).then_inc(r_kept[L], 1)
                    act.wait_ge(r_kept[L], 2 * p + 4)
                    act.dma_start(rows_from[bass.ds(p * P, P), :], yrows).then_inc(r_stored[L], 16)

                def dense(p):
                    n4 = 4 * p + 4
                    for b2 in range(2):
                        for m in range(M):
                            act.wait_ge(d_jobs[L], DENSE_JOBS * p + 10 * b2 + m + 1)
                            act.wait_ge(d_act[L], n4 + 2 * b2)
                            nc.scalar.activation(gexp[:, m, :], banks[m][:, :], ACT.Exp, scale=-1.0).then_inc(d_gexp[L], 1)
                        for m in range(M):
                            act.wait_ge(d_jobs[L], DENSE_JOBS * p + 10 * b2 + 4 + 3 * m + 1)
                            nc.scalar.activation(actT[:, :, :], banks[4][:, :].rearrange("p (c t) -> p c t", c=4), ACT.Copy)\
                              .then_inc(d_actT[L], 1)

                def first_rows():
                    act.wait_ge(r_sent[L], 64)
                    load_rows(0)

                def last_rows():
                    act.wait_ge(r_rows[L], 16 * PAIRS + 16)

                either_way(act, L, routed, dense, first_rows, last_rows)

            act.wait_ge(x_done, DEPTH)
            act.wait_ge(y_done, 4 * DEPTH)
            with nc.allow_non_contiguous_dma(reason="one row to all partitions"):
                act.dma_start(Vx[:, 0, :], nf_in.partition_broadcast(P)).then_inc(nf_loaded, 16)
            squares(6 * DEPTH)
            for m in range(M):
                act.wait_ge(fin_done, m + 1)
                act.dma_start(out[m * P:(m + 1) * P, :], xs[:, m, :]).then_inc(out_done, 16)
            act.wait_ge(out_done, 16 * M)

        @block.gpsimd
        def _(pool):
            chain = Chain(pool, pool_chain)
            link = chain.link
            nc.gpsimd.memset(sm[:, :], 0.0).then_inc(zeroed, 1)
            pool.wait_ge(zeroed, 1)
            nc.gpsimd.iota(PT[:, 0, 0, :].bitcast(I32), pattern=[[1, P]], base=P, channel_multiplier=-1)
            nc.gpsimd.iota(PT[:, 1, 0, :].bitcast(I32), pattern=[[1, P]], base=0, channel_multiplier=0)
            nc.gpsimd.iota(PT[:, 1, 1, :].bitcast(I32), pattern=[[0, P]], base=0, channel_multiplier=1).then_inc(iota_done, 1)
            nc.gpsimd.iota(io16, pattern=[[1, N_EXPERTS]], base=0, channel_multiplier=0, allow_small_or_imprecise_dtypes=True)\
              .then_inc(iota_done, 1)
            link(nc.gpsimd.memset(expo, -0.5))
            nc.gpsimd.memset(ident[:, :], 0.0).then_inc(ident_done, 1)
            pool.wait_ge(ident_done, 1)
            nc.gpsimd.affine_select(out=ident[:, :], in_=ident[:, :], compare_op=ALU.not_equal, fill=1.0, base=0,
                                    pattern=[[-1, P]], channel_multiplier=1).then_inc(ident_done, 1)
            nc.gpsimd.memset(S[:, :, :, :], 0.0)
            nc.gpsimd.memset(pad8[:, :, :], NEG)
            nc.gpsimd.memset(vaug[:, :, :, :], 1.0).then_inc(zeroed, 1)

            def root(dst, src, n, width):
                link(nc.gpsimd.tensor_scalar(dst, src, 1.0 / n, EPS, ALU.mult, ALU.add))
                return nc.gpsimd.tensor_tensor(dst, dst, expo[:, 0:width], ALU.pow)

            pool.wait_ge(mem_sq, 2)
            root(mrs, mss, D, 2).then_inc(mem_rstd, 1)

            for L in range(DEPTH):
                pool.wait_ge(gains_done, 1)
                pool.wait_ge(x_done, L)
                nc.gpsimd.tensor_copy(cur[:, :], gains[:, bass.ds(L, 1), :].rearrange("p l n -> p (l n)")).then_inc(cur_done, 1)

                def norm(k):
                    pool.wait_ge(sq_done, 6 * L + 2 * k + 2)
                    root(rstd, ss, D, 2).then_inc(rstd_done, 1)

                norm(0)
                tot_n = 0
                pool.wait_ge(f_done, 2 * L + 2)
                for prev, cu in zip([F] + tots, tots):
                    pv = prev.rearrange("p a (b u) -> p a b u", u=2)
                    nc.gpsimd.tensor_tensor(cu, pv[:, :, :, 0], pv[:, :, :, 1], ALU.mult).then_inc(tot_done, 1)
                    tot_n += 1
                    pool.wait_ge(tot_done, 6 * L + tot_n)
                wait_job(pool, L, "hg1")
                pool.wait_ge(mem_kept, 4)
                pool.wait_ge(cur_done, L + 1)
                nc.gpsimd.tensor_tensor(hT[:, :, :], memT[:, :, :], cur[:, 16:24].unsqueeze(2).to_broadcast([P, C, T]), ALU.mult)\
                  .then_inc(memg_done, 1)
                for j in range(7):
                    h = 1 << j
                    tj = [F] + tots
                    for m in range(M):
                        kv = K[:, :, m * P:(m + 1) * P].rearrange("p a (b u i) -> p a b u i", u=2, i=h)[:, :, :, 0, :]
                        tv = tj[j][:, :, m * (P // h):(m + 1) * (P // h)].rearrange("p a (b u) -> p a b u", u=2)[:, :, :, 1]
                        wait_job(pool, L, f"lev{j + 1}_{m}")
                        nc.gpsimd.tensor_tensor(kv, kv, tv.unsqueeze(3).to_broadcast([P, HG_HEADS, P // (2 * h), h]), ALU.mult)\
                          .then_inc(k_done, 1)
                        pool.wait_ge(k_done, 14 * L + 2 * j + m + 1)
                for m in range(M):
                    pool.wait_ge(hms_done, 2 * L + m + 1)
                    root(hrs[:, m, :], hss[:, m, :], P, HG_HEADS).then_inc(hrs_done, 1)
                norm(1)
                norm(2)

                def send_rows():
                    pool.wait_ge(rows_zeroed, 16 * (PAIRS + 1))
                    for m in range(M):
                        for k in range(2):
                            pool.indirect_dma_start(rows_to[:, :], bass.IndirectOffsetOnAxis(ap=slots[:, m, k:k + 1], axis=0),
                                                    xs[:, m, :], None).then_inc(r_sent[L], 16)

                def fetch_rows():
                    pool.wait_ge(r_stored[L], 16 * PAIRS + 16)
                    for m in range(M):
                        for k in range(2):
                            pool.indirect_dma_start(back[:, m, k, :], None, rows_from[:, :],
                                                    bass.IndirectOffsetOnAxis(ap=slots[:, m, k:k + 1], axis=0)).then_inc(r_back[L], 16)

                pool.wait_ge(flag_done, L + 1)
                fullest = pool.value_load(most[0:1, 0:1], min_val=0, max_val=T)
                with pool.If(fullest <= CAP):
                    send_rows()
                    fetch_rows()
                with pool.Else():
                    pool.wait_ge(x_done, L)
            pool.wait_ge(sq_done, 6 * DEPTH + 2)
            root(rstd, ss, D, 2).then_inc(rstd_done, 1)

        @block.vector
        def _(dve):
            chain = Chain(dve, dve_chain)
            link = chain.link
            V = nc.vector
            for l in range(DEPTH):
                dve.sem_inc(d_act[l], 4)
                dve.sem_inc(d_added[l], 8)
            dve.sem_inc(slots_read, 3)
            dve.wait_ge(iota_done, 2)
            dve.wait_ge(zeroed, 2)
            dif, fi, pi = (PT[:, 0, 0, :].bitcast(I32), PT[:, 1, 0, :].bitcast(I32), PT[:, 1, 1, :].bitcast(I32))
            tmp = PT[:, 2, 0, :].bitcast(I32)
            ge, le, m4, m16 = (PT[:, 2, k, :] for k in range(1, 5))
            V.tensor_scalar(ge, dif, float(P), None, ALU.is_ge)
            V.tensor_scalar(le, dif, float(P), None, ALU.is_le)
            link(V.tensor_scalar(tmp, dif, 3, None, ALU.bitwise_and))
            link(V.tensor_scalar(m4, tmp, 0.0, None, ALU.is_equal))
            link(V.tensor_scalar(tmp, dif, 15, None, ALU.bitwise_and))
            link(V.tensor_scalar(m16, tmp, 0.0, None, ALU.is_equal))
            V.tensor_scalar(before[:, :], dif, float(P), None, ALU.is_gt)
            V.memset(ones[:, :], 1.0)
            V.tensor_scalar(base16, io16, float(CAP), None, ALU.mult)
            V.tensor_scalar(bias0[:, :], le, 1.0, -NEG, ALU.subtract, ALU.mult)
            link(V.tensor_tensor(bias10[:, :], ge, m4, ALU.max))
            link(V.tensor_scalar(bias10[:, :], bias10[:, :], 1.0, -NEG, ALU.subtract, ALU.mult))
            link(V.tensor_tensor(m4, m4, m16, ALU.add))
            link(V.tensor_tensor(cnt[:, 1, :], le, m4, ALU.add))
            link(V.tensor_scalar(m4, m4, 1.0, None, ALU.add))
            link(V.tensor_tensor(cnt[:, 0, :], ge, m4, ALU.mult))
            link(V.tensor_tensor(fi, fi, pi, ALU.bitwise_xor))
            V.tensor_scalar(lev[:, 0, :], dif, float(P), None, ALU.is_equal)
            for j in range(7):
                link(V.tensor_scalar(tmp, fi, j, None, ALU.logical_shift_right))
                link(V.tensor_scalar(lev[:, j + 1, :], tmp, 1.0, None, ALU.is_equal))
                link(V.tensor_tensor(lev[:, j + 1, :], lev[:, j + 1, :], ge, ALU.mult))
            dve.wait_ge(mem_rstd, 1)
            dve.wait_ge(mem_loaded, 16)
            for m in range(M):
                V.tensor_scalar(E[:, m * D:(m + 1) * D], E[:, m * D:(m + 1) * D], mrs[:, m:m + 1], None, ALU.mult).then_inc(mem_scaled, 1)
            dve.wait_ge(small_loaded, 96)
            lb = [gains[:, l, 32:36] for l in range(DEPTH)]
            ex = [gains[:, l, 36:40] for l in range(DEPTH)]
            mx, tot = early[:, 100:104], early[:, 104:108]
            link(V.tensor_tensor(mx, lb[0], lb[1], ALU.max))
            V.tensor_tensor(ex[0], lb[0], mx, ALU.subtract)
            V.tensor_tensor(ex[1], lb[1], mx, ALU.subtract).then_inc(lb_max, 1)
            link(V.tensor_copy(posf, early[:, 0:M].bitcast(I32)))
            for m in range(M):
                last = V.tensor_scalar(sinT[:, m, :], early[:, 64:96], posf[:, m:m + 1], None, ALU.mult)
            link(last)
            ang = sinT[:, :, :].rearrange("p m k -> p (m k)")
            red = cosT[:, :, :].rearrange("p m k -> p (m k)")
            turns = early[:, 128:192]
            MAGIC = 1.5 * 2.0 ** 23
            two_pi = 2.0 * np.pi
            c1 = 6.28125
            c2 = float(np.float32(np.round((two_pi - c1) * 2.0 ** 20) / 2.0 ** 20))
            c3 = float(two_pi - c1 - c2)
            for table, shift in ((red, 0.25), (ang, 0.0)):
                link(V.tensor_scalar(turns, ang, 1.0 / two_pi, shift, ALU.mult, ALU.add))
                link(V.tensor_scalar(turns, turns, MAGIC, None, ALU.add))
                link(V.tensor_scalar(turns, turns, MAGIC, None, ALU.subtract))
                link(V.scalar_tensor_tensor(table, turns, -c1, ang, ALU.mult, ALU.add))
                link(V.scalar_tensor_tensor(table, turns, -c2, table, ALU.mult, ALU.add))
                link(V.scalar_tensor_tensor(table, turns, -c3, table, ALU.mult, ALU.add))
                if shift:
                    link(V.tensor_scalar(table, table, HALF_PI, None, ALU.add))
                link(V.tensor_scalar(table, table, 3.1415925, -3.1415925, ALU.min, ALU.max))
            V.tensor_copy(sm[:, 106:107], sm[:, 107:108]).then_inc(trig_arg, 1)
            dve.wait_ge(lb_exp, 1)
            link(V.tensor_tensor(tot, ex[0], ex[1], ALU.add))
            link(V.reciprocal(tot, tot))
            V.tensor_tensor(ex[0], ex[0], tot, ALU.mult)
            link(V.tensor_tensor(ex[1], ex[1], tot, ALU.mult))
            link(V.tensor_tensor(lb[1], ex[0], ex[1], ALU.add))
            V.tensor_tensor(lb[0], ex[0], ex[0], ALU.subtract)
            link(V.tensor_tensor(lb[1], lb[1], ex[0], ALU.subtract))
            for l in range(DEPTH):
                last = V.tensor_scalar(ex[l], lb[l], -1.0, 1.0, ALU.mult, ALU.add)
            last.then_inc(gains_done, 1)
            for m in range(M):
                for c2 in range(2):
                    dve.wait_ge(mem_tr, 2 * m + c2 + 1)
                    V.tensor_copy(memT[:, 4 * c2:4 * c2 + 4, m * P:(m + 1) * P],
                                  banks[4 + 2 * m + c2][:, :].rearrange("p (c t) -> p c t", c=4)).then_inc(mem_kept, 1)
            dve.wait_ge(tables_done, 1)

            def scale_rows(L, k):
                dve.wait_ge(rstd_done, 3 * L + k + 1)
                for m in range(M):
                    V.tensor_scalar(xs[:, m, :], x[:, m, :], rstd[:, m:m + 1], None, ALU.mult).then_inc(normed, 1)

            for L in range(DEPTH):

                def emptied(ins):
                    ins.then_inc(empt["D"], 1)

                def rows_T(t, g0):
                    for m in range(M):
                        for c2 in range(2):
                            wait_job(dve, L, f"{t}_{m}{c2}")
                            emptied(V.tensor_tensor(hT[:, 4 * c2:4 * c2 + 4, m * P:(m + 1) * P],
                                                    bank(f"{t}_{m}{c2}")[:, :].rearrange("p (c t) -> p c t", c=4),
                                                    cur[:, g0 + 4 * c2:g0 + 4 * c2 + 4].unsqueeze(2).to_broadcast([P, 4, P]), ALU.mult))

                scale_rows(L, 0)
                dve.wait_ge(cur_done, L + 1)
                rows_T("t1", 0)
                Fall = F[:, :, :].rearrange("p a t -> p (a t)")
                wait_emptied(dve, L, "hf1")
                link(V.tensor_scalar(Fall, Fall, 1.0, None, ALU.add))
                link(V.reciprocal(Fall, Fall))
                for a in range(HG_HEADS):
                    last = V.tensor_scalar(F[:, a, :], F[:, a, :], cur[:, 36 + a:37 + a], cur[:, 32 + a:33 + a], ALU.mult, ALU.add)
                last.then_inc(f_done, 1)
                dve.wait_ge(f_done, 2 * L + 1)
                V.tensor_scalar(K[:, :, :].rearrange("p a t -> p (a t)"), Fall, -1.0, 1.0, ALU.mult, ALU.add).then_inc(f_done, 1)
                for w, name in enumerate(("aq", "ak")):
                    for m in range(M):
                        wait_job(dve, L, f"{name}{m}")
                        t = bank(f"{name}{m}")[:, :].rearrange("p (h u i) -> p h u i", u=2, i=32)
                        r = rot[:, (2 * w + m) * W:(2 * w + m + 1) * W].rearrange("p (h u i) -> p h u i", u=2, i=32)
                        b = PT[:, 0, 0:4, :].rearrange("p a (h u i) -> p (a h) u i", u=2, i=32)
                        cs = cosT[:, m, :].unsqueeze(1).unsqueeze(1).to_broadcast([P, ATT_HEADS, 2, 32])
                        sn = sinT[:, m, :].unsqueeze(1).unsqueeze(1).to_broadcast([P, ATT_HEADS, 2, 32])
                        V.tensor_tensor(r, t, cs, ALU.mult)
                        link(V.tensor_tensor(b, t, sn, ALU.mult))
                        V.tensor_tensor(r[:, :, 0, :], r[:, :, 0, :], b[:, :, 1, :], ALU.subtract)
                        link(V.tensor_tensor(r[:, :, 1, :], r[:, :, 1, :], b[:, :, 0, :], ALU.add))
                        V.tensor_copy(sm[:, 100:101], sm[:, 101:102]).then_inc(rot_done, 1)
                        emptied(V.tensor_copy(sm[:, 102:103], sm[:, 103:104]))
                dve.wait_ge(og_loaded, 16 * L + 16)
                for m in range(M):
                    dve.wait_ge(gate_exp, 2 * L + m + 1)
                    g = gg[:, m, :]
                    link(V.tensor_scalar(g, g, 1.0, None, ALU.add))
                    link(V.reciprocal(g, g))
                    link(V.tensor_tensor(g, bank(f"hg{m}")[:, :], g, ALU.mult))
                    emptied(V.tensor_tensor(g, g, og[:, :], ALU.mult))
                dve.wait_ge(tot_done, 6 * L + 6)
                dve.wait_ge(rows_zeroed, 16 * (PAIRS + 1))
                tj = [F] + tots
                for j in range(8):
                    for m in range(M):
                        wait_job(dve, L, f"lev{j}_{m}")
                        emptied(V.copy_predicated(S[:, m, :, :], lev[:, j, :].bitcast(I32).unsqueeze(1).to_broadcast([P, HG_HEADS, P]),
                                                  bank(f"lev{j}_{m}")[:, :].rearrange("p (a t) -> p a t", t=P)))
                        Qm = Q[:, :, m * P:(m + 1) * P]
                        if j == 0:
                            V.tensor_tensor(Qm, Qm, F[:, :, m * P:(m + 1) * P], ALU.mult).then_inc(q_done, 1)
                        else:
                            h = 1 << (j - 1)
                            qv = Qm.rearrange("p a (b u i) -> p a b u i", u=2, i=h)[:, :, :, 1, :]
                            tv = tj[j - 1][:, :, m * (P // h):(m + 1) * (P // h)].rearrange("p a (b u) -> p a b u", u=2)[:, :, :, 0]
                            V.tensor_tensor(qv, qv, tv.unsqueeze(3).to_broadcast([P, HG_HEADS, P // (2 * h), h]), ALU.mult)\
                             .then_inc(q_done, 1)
                        dve.wait_ge(q_done, 16 * L + 2 * j + m + 1)
                wait_job(dve, L, "cross")
                emptied(V.tensor_copy(S01[:, :, :], bank("cross")[:, :].rearrange("p (a t) -> p a t", t=P)))
                at = 0
                dve.wait_ge(k_done, 14 * L + 14)
                for k, (m, heads) in enumerate(SCORES):
                    wait_job(dve, L, f"s{k}")
                    n, nh, h0 = (m + 1) * P, len(heads), heads[0]
                    eh = E[:, m * D:m * D + ATT_HEADS * n].rearrange("p (g u n) -> p g u n", u=2, n=n)
                    e = eh[:, h0 // 2:h0 // 2 + nh, h0 % 2, :]
                    src = bank(f"s{k}")[:, :].rearrange("p (g n) -> p g n", n=n)
                    if m:
                        V.tensor_tensor(e[:, :, 0:P], src[:, :, 0:P], bias10[:, :].unsqueeze(1).to_broadcast([P, nh, P]), ALU.add)
                    last = V.tensor_tensor(e[:, :, n - P:n], src[:, :, n - P:n], bias0[:, :].unsqueeze(1).to_broadcast([P, nh, P]), ALU.add)
                    emptied(last)
                    wait_emptied(dve, L, f"s{k}")
                    V.tensor_reduce(nmx[:, at:at + nh], e, AX, ALU.max, negate=True).then_inc(max_done, 1)
                    at += nh
                for m in range(M):
                    dve.wait_ge(hsq_done, 2 * L + m + 1)
                    V.tensor_reduce(hss[:, m, :], rot[:, m * W:(m + 1) * W].rearrange("p (h v) -> p h v", v=P), AX, ALU.add).then_inc(hms_done, 1)
                wait_job(dve, L, "s5")
                for m in range(M):
                    y = xs[:, m, 0:W]
                    emptied(V.tensor_tensor(y, bank(f"hp{m}")[:, :], gg[:, m, :], ALU.mult))
                    wait_emptied(dve, L, f"hp{m}")
                    dve.wait_ge(hrs_done, 2 * L + m + 1)
                    yh = y.rearrange("p (h v) -> p h v", v=P)
                    V.tensor_tensor(yh, yh, hrs[:, m, :].unsqueeze(2).to_broadcast([P, HG_HEADS, P]), ALU.mult).then_inc(y_done, 1)
                for k in range(6):
                    wait_job(dve, L, f"et{k}")
                    blk = 0 if k < 2 else 1 + (k - 2) // 2
                    c = cnt[:, 1 if blk == 1 else 0, :]
                    emptied(V.tensor_tensor(PT[:, blk, 4 * (k % 2):4 * (k % 2) + 4, :], bank(f"et{k}")[:, :].rearrange("p (h t) -> p h t", t=P),
                                            c.unsqueeze(1).to_broadcast([P, 4, P]), ALU.mult))
                for m in range(M):
                    for g in range(2):
                        wait_job(dve, L, f"ap{m}{g}")
                        o = bank(f"ap{m}{g}")[:, :].rearrange("p (h n) -> p h n", n=P)
                        rd = rden[:, m, 4 * g:4 * g + 4]
                        link(V.reciprocal(rd.unsqueeze(2), o[:, :, DH:DH + 1]))
                        y = xs[:, m, W + g * 256:W + (g + 1) * 256].rearrange("p (h d) -> p h d", d=DH)
                        emptied(V.tensor_tensor(y, o[:, :, 0:DH], rd.unsqueeze(2).to_broadcast([P, 4, DH]), ALU.mult))
                    wait_emptied(dve, L, f"ap{m}1")
                    V.tensor_copy(sm[:, 104:105], sm[:, 105:106]).then_inc(y_done, 1)

                def add_rows(t):
                    for n in range(2):
                        for m in range(M):
                            wait_job(dve, L, f"{t}{n}{m}")
                            xv = x[:, m, n * W:(n + 1) * W]
                            emptied(V.tensor_tensor(xv, bank(f"{t}{n}{m}")[:, :], xv, ALU.add))
                    wait_emptied(dve, L, f"{t}11")

                add_rows("wo")
                scale_rows(L, 1)
                rows_T("t3", 8)
                for m in range(M):
                    for g in range(2):
                        wait_job(dve, L, f"sx{m}{g}")
                        mv = xmx[:, m, 2 * g:2 * g + 2]
                        link(V.tensor_reduce(mv, bank(f"sx{m}{g}")[:, :].rearrange("p (h s) -> p h s", s=T), AX, ALU.max, negate=True))
                        V.tensor_scalar(mv, mv, X_DH ** -0.5, None, ALU.mult).then_inc(xmax_done, 1)
                for m in range(M):
                    for jb in range(2):
                        wait_job(dve, L, f"pt{m}{jb}")
                        emptied(V.tensor_copy(PTx[:, 2 * m + jb, :, :], bank(f"pt{m}{jb}")[:, :].rearrange("p (h t) -> p h t", t=P)))
                wait_emptied(dve, L, "sx11")
                link(V.reciprocal(xrd[:, :, :], xden[:, :, :]))
                for m in range(M):
                    for g in range(2):
                        wait_job(dve, L, f"px{m}{g}")
                        y = xs[:, m, g * W:(g + 1) * W].rearrange("p (h d) -> p h d", d=T)
                        emptied(V.tensor_tensor(y, bank(f"px{m}{g}")[:, :].rearrange("p (h d) -> p h d", d=T),
                                                xrd[:, m, 2 * g:2 * g + 2].unsqueeze(2).to_broadcast([P, 2, T]), ALU.mult))
                add_rows("ox")
                scale_rows(L, 2)
                rows_T("t5", 24)
                wait_job(dve, L, "rl")
                emptied(V.tensor_copy(logits[:, :, :], bank("rl")[:, 0:40].rearrange("p (m n) -> p m n", m=M)))
                wait_emptied(dve, L, "rl")
                link(V.tensor_copy(pad8[:, :, 0:N_GROUPS], logits[:, :, 0:N_GROUPS]))
                for m in range(M):
                    last = V.max(top8[:, m, :], pad8[:, m, :])
                link(last)
                V.tensor_scalar(ngmx.unsqueeze(2), top8[:, :, 0:1], -1.0, None, ALU.mult).then_inc(lmax_done, 1)
                for m in range(M):
                    last = V.max_index(idx8[:, m, :].bitcast(mybir.dt.uint32), top8[:, m, :], pad8[:, m, :])
                link(last)
                link(V.tensor_copy(idxf[:, :, :], idx8[:, :, :].bitcast(mybir.dt.uint32)))
                for m in range(M):
                    last = V.tensor_scalar(oneg[:, m, :], io16[:, 0:N_GROUPS], idxf[:, m, 0:1], None, ALU.is_equal)
                link(last)
                link(V.tensor_scalar(oneg[:, :, :], oneg[:, :, :], 1.0, -NEG, ALU.subtract, ALU.mult))
                for m in range(M):
                    last = V.tensor_tensor(elog[:, m, :].rearrange("p (g e) -> p g e", e=4),
                                           logits[:, m, N_GROUPS:].rearrange("p (g e) -> p g e", e=4),
                                           oneg[:, m, :].unsqueeze(2).to_broadcast([P, N_GROUPS, 4]), ALU.add)
                link(last)
                for m in range(M):
                    last = V.max(top8[:, m, :], elog[:, m, :])
                link(last)
                dve.wait_ge(lexp_done, 2 * L + 1)
                V.tensor_tensor(e2.unsqueeze(2), top8[:, :, 1:2], top8[:, :, 0:1], ALU.subtract).then_inc(lmax_done, 1)
                for m in range(M):
                    last = V.max_index(idx8[:, m, :].bitcast(mybir.dt.uint32), top8[:, m, :], elog[:, m, :])
                link(last)
                link(V.tensor_copy(idxf[:, :, :], idx8[:, :, :].bitcast(mybir.dt.uint32)))
                dve.wait_ge(lexp_done, 2 * L + 2)
                link(V.tensor_scalar(sc2, e2, 1.0, None, ALU.add))
                link(V.tensor_tensor(sc2, sc2, gsum, ALU.mult))
                link(V.reciprocal(w1, sc2))
                link(V.tensor_tensor(w2, w1, e2, ALU.mult))
                for m in range(M):
                    for k in range(2):
                        last = V.tensor_scalar(one2[:, m, k, :], io16, idxf[:, m, k:k + 1], None, ALU.is_equal)
                link(last)
                V.tensor_tensor(chosen[:, :, :], one2[:, :, 0, :], one2[:, :, 1, :], ALU.add).then_inc(chosen_done, 1)
                wait_job(dve, L, "rank")
                bk = bank("rank")
                V.tensor_reduce(mostf, bk[:, 2 * N_EXPERTS:3 * N_EXPERTS], AX, ALU.max)
                last = V.tensor_tensor(rank[:, :, :], bk[:, 0:2 * N_EXPERTS].rearrange("p (m n) -> p m n", m=M),
                                       base16.unsqueeze(1).to_broadcast([P, M, N_EXPERTS]), ALU.add)
                emptied(last)
                wait_emptied(dve, L, "rank")
                V.tensor_copy(most, mostf)
                for k in range(2):
                    last = V.tensor_tensor(pick[:, :, k, :], one2[:, :, k, :], rank[:, :, :], ALU.mult)
                link(last)
                link(V.tensor_reduce(slotf[:, :, :], pick[:, :, :, :], AX, ALU.add))
                V.tensor_copy(slots[:, :, :], slotf[:, :, :]).then_inc(flag_done, 1)

                def taken(semaphore, value):
                    dve.wait_ge(semaphore, value)
                    dve.sem_inc(slots_read, 1)

                def routed(p):
                    inner = Chain(dve, r_chain[L], ROUTED_LINKS * p)
                    jobs = ROUTED_JOBS * p
                    for c2 in range(2):
                        dve.wait_ge(r_jobs[L], jobs + c2 + 1)
                        V.tensor_tensor(rowsT[:, 4 * c2:4 * c2 + 4, :], banks[c2][:, :].rearrange("p (c t) -> p c t", c=4),
                                        cur[:, 24 + 4 * c2:28 + 4 * c2].unsqueeze(2).to_broadcast([P, 4, P]), ALU.mult).then_inc(r_rowsT[L], 1)
                    taken(r_jobs[L], jobs + 3)
                    dve.wait_ge(r_gexp[L], p + 1)
                    inner.link(V.tensor_scalar(rexp, rexp, 1.0, None, ALU.add))
                    inner.link(V.reciprocal(rexp, rexp))
                    inner.link(V.tensor_tensor(rexp, banks[2][:, :], rexp, ALU.mult))
                    taken(r_jobs[L], jobs + 4)
                    V.tensor_tensor(ract, banks[3][:, :], rexp, ALU.mult).then_inc(r_act[L], 1)
                    taken(r_jobs[L], jobs + 7)
                    assert inner.n == ROUTED_LINKS

                def combine():
                    done = Chain(dve, r_chain[L], ROUTED_LINKS * PAIRS)
                    dve.wait_ge(r_back[L], 64)
                    for k, wk in enumerate((w1, w2)):
                        for m in range(M):
                            last = V.scalar_tensor_tensor(x[:, m, :], back[:, m, k, :], wk[:, m:m + 1], x[:, m, :], ALU.mult, ALU.add)
                        done.link(last)

                def gates_of_all():
                    start = Chain(dve, d_chain[L])
                    for m in range(M):
                        V.tensor_scalar(gates[:, m, :], one2[:, m, 0, :], w1[:, m:m + 1], None, ALU.mult)
                        last = V.tensor_scalar(one1[:, m, :], one2[:, m, 1, :], w2[:, m:m + 1], None, ALU.mult)
                    start.link(last)
                    start.link(V.tensor_tensor(gates[:, :, :], gates[:, :, :], one1[:, :, :], ALU.add))

                def dense(p):
                    inner = Chain(dve, d_chain[L], DENSE_LINKS * p + 2)
                    jobs = DENSE_JOBS * p
                    for b2 in range(2):
                        for m in range(M):
                            dve.wait_ge(d_gexp[L], 4 * p + 2 * b2 + m + 1)
                            g = gexp[:, m, :]
                            inner.link(V.tensor_scalar(g, g, 1.0, None, ALU.add))
                            inner.link(V.reciprocal(g, g))
                            inner.link(V.tensor_tensor(g, banks[m][:, :], g, ALU.mult))
                            dve.wait_ge(d_jobs[L], jobs + 10 * b2 + 2 + m + 1)
                            V.tensor_tensor(actb[:, m, :], banks[2 + m][:, :], g, ALU.mult).then_inc(d_act[L], 1)
                        for m in range(M):
                            for n in range(2):
                                dve.wait_ge(d_jobs[L], jobs + 10 * b2 + 4 + 3 * m + 1 + n + 1)
                                xv = x[:, m, n * W:(n + 1) * W]
                                gate = gates[:, m, bass.ds(2 * p + b2, 1)]
                                V.scalar_tensor_tensor(xv, banks[5 + n][:, :], gate, xv, ALU.mult, ALU.add).then_inc(d_added[L], 1)
                    for done in (12, 14, 20):
                        taken(d_jobs[L], jobs + done)
                    assert inner.n == DENSE_LINKS

                def all_added():
                    dve.wait_ge(d_added[L], 8 * PAIRS + 8)

                dve.wait_ge(flag_done, L + 1)
                either_way(dve, L, routed, dense, None, combine, gates_of_all, all_added)
                dve.sem_inc(x_done, 1)
            dve.wait_ge(rstd_done, 3 * DEPTH + 1)
            dve.wait_ge(nf_loaded, 16)
            for m in range(M):
                V.scalar_tensor_tensor(xs[:, m, :], x[:, m, :], rstd[:, m:m + 1], Vx[:, 0, :], ALU.mult, ALU.mult).then_inc(fin_done, 1)


_INS = ["x", "mem", "positions", "inv", "gains", "hg_lower_bounds", "hg_out_norm", "w_in", "w_out", "wq_x", "wkv_x", "wo_x",
        "w_router", "w_gate", "w_up", "w_down", "norm_final"]


def kernel(**inputs):
    import numpy as _np
    import concourse.bacc as _bacc
    from concourse import mybir as _mybir
    from concourse.bass_utils import run_bass_kernel_spmd as _run

    a = {k: _np.ascontiguousarray(v) for k, v in inputs.items()}
    a["x"], a["mem"], a["positions"] = a["x"].reshape(T, D), a["mem"].reshape(T, D), a["positions"].reshape(T)
    a["inv"] = _np.power(_np.float32(ROPE_THETA), -_np.arange(0, DH, 2, dtype=_np.float32) / _np.float32(DH)).astype(_np.float32)
    a["gains"] = _np.stack([a.pop("norm_mix"), a.pop("norm_cross"), a.pop("norm_mem"), a.pop("norm_ffn")])
    a["w_router"] = _np.concatenate([a.pop("w_router_group"), a.pop("w_router_expert")], axis=2)
    for name in ("w_gate", "w_up", "w_down"):
        a[name] = a[name].reshape(DEPTH * N_EXPERTS, P, D * FF // P)
    nc = _bacc.Bacc("TRN2", target_bir_lowering=False, num_devices=1)
    arrays = {f"in_{n}": a[n] for n in _INS}
    args = [nc.dram_tensor(f"in_{n}", a[n].shape, _mybir.dt.from_np(a[n].dtype), kind="ExternalInput").ap() for n in _INS]
    rows = [nc.dram_tensor(n, (P * k, D), F32, kind="Internal").ap() for n, k in (("rows_to", PAIRS + 1), ("rows_from", PAIRS))]
    out = nc.dram_tensor("out", (T, D), F32, kind="ExternalOutput").ap()
    trunk(nc, *args, *rows, out)
    r = _run(nc, [arrays], core_ids=[0])
    return r.results[0]["out"].reshape(1, T, D)
```

```python
from contextlib import ExitStack

import numpy as np

import concourse.bass as bass
from concourse import mybir

P = 128
ALU = mybir.AluOpType
ACT = mybir.ActivationFunctionType
F32 = mybir.dt.float32
I32 = mybir.dt.int32
BF16 = mybir.dt.bfloat16
AX = mybir.AxisListType.X

D = 1024
C = D // P
T = 256
M = T // P
DEPTH = 2
HG_HEADS = 4
ATT_HEADS = 8
DH = 64
X_HEADS = 4
X_DH = D // X_HEADS
N_GROUPS = 4
N_EXPERTS = 16
FF = 512
W = 512
NEG = -1.0e30
EPS = 1e-6
ROPE_THETA = 10000.0

SLOTS = 6
UNITS = ["k0", "k1", "v0", "v1", "hf", "hq", "hi", "aq", "ak", "av", "hg", "o0", "o1", "q0", "q1", "p0", "p1", "router"]
MIX_ROUNDS = len(UNITS) // SLOTS
PAIRS = N_EXPERTS // 2
ROUNDS = MIX_ROUNDS + PAIRS


BETWEEN = [("hi1", "A"), ("aq0", "D"), ("aq1", "D"), ("ak0", "D"), ("ak1", "D"), ("av0", "A"), ("av1", "A"), ("hg0", "D")]


def job_list():
    quarters = [(m, c) for m in range(M) for c in range(2)]
    jobs = [(f"kv{j}", "A") for j in range(8)]
    jobs += [(f"t1_{m}{c}", "D") for m, c in quarters]
    jobs += [(f"{name}{k}", "A") for name in ("hf", "hq") for k in range(2)]
    jobs += [("hi0", "A")]
    for j, (name, who) in enumerate(BETWEEN):
        jobs += [(name, who)] + [(f"lev{j}_{m}", "D") for m in range(M)]
    jobs += [("hg1", "D")] + [(f"{name}{m}", "A") for name in ("qT", "kT") for m in range(M)]
    jobs += [("cross", "D")]
    jobs += [(f"s{k}", "D") for k in range(6)]
    jobs += [(f"hp{m}", "D") for m in range(M)]
    jobs += [(f"et{k}", "D") for k in range(6)]
    jobs += [(f"ap{m}{g}", "D") for m, g in quarters]
    jobs += [(f"t2_{m}{c}", "A") for m, c in quarters]
    jobs += [(f"wo{n}{m}", "D") for m in range(M) for n in range(2)]
    jobs += [(f"t3_{m}{c}", "D") for m, c in quarters]
    jobs += [(f"qx{k}", "A") for k in range(4)]
    jobs += [(f"sx{m}{g}", "A") for m, g in quarters]
    jobs += [(f"pt{m}{c}", "D") for m, c in quarters]
    jobs += [(f"px{m}{g}", "D") for m, g in quarters]
    jobs += [(f"t4_{m}{c}", "A") for m, c in quarters]
    jobs += [(f"ox{n}{m}", "D") for m in range(M) for n in range(2)]
    jobs += [(f"t5_{m}{c}", "D") for m, c in quarters]
    return jobs + [("rt", "A"), ("rl", "D"), ("rank", "D")]


JOBS = job_list()
NAMES = [n for n, _ in JOBS]
NJ = len(JOBS)
EMPTIER = dict(JOBS)
NTH = {n: sum(w == EMPTIER[n] for _, w in JOBS[:i + 1]) for i, (n, _) in enumerate(JOBS)}
EMPTIED = {w: sum(x == w for _, x in JOBS) for w in "AD"}
LAST_USE = {"hf": "hf1", "hq": "hq1", "hi": "hi1", "aq": "aq1", "ak": "ak1", "av": "av1", "hg": "hg1",
            "k0": "kv1", "k1": "kv3", "v0": "kv5", "v1": "kv7", "o0": "wo01", "o1": "wo11",
            "q0": "qx1", "q1": "qx3", "p0": "ox01", "p1": "ox11", "router": "rt"}
SCORES = [(0, (0, 2, 4, 6)), (0, (1, 3, 5, 7)), (1, (0, 2)), (1, (1, 3)), (1, (4, 6)), (1, (5, 7))]

KV_EARLY = 4
OUT_BANK = ((4, 7), (5, 6))
CAP = 64
ROUTED_JOBS = 12
DENSE_JOBS = 20

DENSE_LINKS = 12
ROUTED_LINKS = 5


class Chain:

    def __init__(self, eng, sem, base=0):
        self.eng, self.sem, self.base, self.n = eng, sem, base, 0

    def link(self, ins):
        self.n += 1
        ins.then_inc(self.sem, 1)
        self.eng.wait_ge(self.sem, self.base + self.n)


def trunk(nc, x_in, mem_in, pos_in, inv_in, gains_in, og_in, w_in, w_out, wq, wkv, wo, w_router,
          w_gate, w_up, w_down, nf_in, out):
    ctx = ExitStack()
    with ctx:
        def sb(name, shape, dt=F32):
            return ctx.enter_context(nc.sbuf_tensor(name, shape, dt))

        def sem(name):
            return ctx.enter_context(nc.semaphore(name))

        ring = sb("ring", [P, SLOTS, 4096])
        x = sb("x", [P, M, D])
        xs = sb("xs", [P, M, D])
        hT = sb("hT", [P, C, T])
        memT = sb("memT", [P, C, T])
        hi = sb("hi", [P, M, W])
        gg = sb("gg", [P, M, W])
        rot = sb("rot", [P, 4 * W])
        vaug = sb("vaug", [P, M, ATT_HEADS, DH + 1])
        work = sb("work", [P, 4, HG_HEADS * T])
        S = sb("S", [P, M, HG_HEADS, P])
        PT = sb("PT", [P, 3, ATT_HEADS, P])
        S01 = PT[:, 2, 0:HG_HEADS, :]
        KT = sb("KT", [P, 8, T])
        Vx = sb("Vx", [P, M, D])
        lev = sb("lev", [P, 8, P])
        bias0 = sb("bias0", [P, P])
        bias10 = sb("bias10", [P, P])
        cnt = sb("cnt", [P, 2, P])
        ident = sb("ident", [P, P])
        columns = sb("columns", [P, P], BF16)
        gains = sb("gains", [P, DEPTH, 40])
        og = sb("og", [P, W])
        cosT = sb("cosT", [P, M, 32])
        sinT = sb("sinT", [P, M, 32])
        sm = sb("sm", [P, 112])
        wsm = sb("wsm", [P, 242])
        early = PT[:, 2, 6:8, :].rearrange("p a t -> p (a t)")
        gates = sb("gates", [P, M, N_EXPERTS])
        before = sb("before", [P, P], BF16)
        ones = sb("ones", [P, P], BF16)
        chosen = sb("chosen", [P, M, N_EXPERTS], BF16)

        Q = work[:, 0, :].rearrange("p (a t) -> p a t", a=HG_HEADS)
        K = work[:, 1, :].rearrange("p (a t) -> p a t", a=HG_HEADS)
        F = work[:, 2, :].rearrange("p (a t) -> p a t", a=HG_HEADS)
        TOT = work[:, 3, :].rearrange("p (a t) -> p a t", a=HG_HEADS)
        E = work[:, :, :].rearrange("p a b -> p (a b)")
        attT = xs[:, :, :].rearrange("p a (g t) -> p (a g) t", t=T)
        QxT = rot[:, :].rearrange("p (n t) -> p n t", t=T)
        Px = work[:, 0:2, :].rearrange("p m (h s) -> p m h s", s=T)
        PTx = PT[:, 0:2, :, :].rearrange("p a (b h) t -> p (a b) h t", h=HG_HEADS)
        ss = sm[:, 0:2]
        rstd = sm[:, 2:4]
        hss = sm[:, 4:12].rearrange("p (m h) -> p m h", m=M)
        hrs = sm[:, 12:20].rearrange("p (m h) -> p m h", m=M)
        nmx = sm[:, 20:36]
        rden = sm[:, 36:52].rearrange("p (m h) -> p m h", m=M)
        xmx = sm[:, 52:60].rearrange("p (m h) -> p m h", m=M)
        xden = sm[:, 60:68].rearrange("p (m h) -> p m h", m=M)
        xrd = sm[:, 68:76].rearrange("p (m h) -> p m h", m=M)
        expo = sm[:, 76:84]
        mss = sm[:, 84:86]
        mrs = sm[:, 86:88]
        posf = sm[:, 96:98]
        sq = rot[:, 0:D]

        banks = [ctx.enter_context(nc.psum_tensor(f"bank{i}", [P, W], F32)) for i in range(8)]

        loaded = [sem(f"loaded{s}") for s in range(SLOTS)]
        x_loaded, small_loaded = sem("x_loaded"), sem("small_loaded")
        mem_loaded = [sem(f"mem_loaded{m}") for m in range(M)]
        mem_gained = sem("mem_gained")
        og_loaded, nf_loaded = sem("og_loaded"), sem("nf_loaded")
        iota_done, tables_done = sem("iota_done"), sem("tables_done")
        zeroed = sem("zeroed")
        ident_done = sem("ident_done")
        mem_sq, mem_rstd, mem_scaled, mem_tr, mem_kept = (sem(n) for n in ("mem_sq", "mem_rstd", "mem_scaled", "mem_tr", "mem_kept"))
        trig_arg = sem("trig_arg")
        lb_exp = sem("lb_exp")
        lb_max = sem("lb_max")
        gains_done = sem("gains_done")
        job_done = sem("job_done")
        empt = {"A": sem("emptied_by_scalar"), "D": sem("emptied_by_vector")}
        sq_done = sem("sq_done")
        rstd_done = sem("rstd_done")
        normed = sem("normed")
        f_done = sem("f_done")
        q_done = sem("q_done")
        k_done = sem("k_done")
        tot_done = sem("tot_done")
        rot_done = sem("rot_done")
        gate_exp = sem("gate_exp")
        memg_done = sem("memg_done")
        max_done = sem("max_done")
        e_done = sem("e_done")
        hsq_done = sem("hsq_done")
        hms_done = sem("hms_done")
        hrs_done = sem("hrs_done")
        y_done = sem("y_done")
        xmax_done = sem("xmax_done")
        lexp_done = sem("lexp_done")
        lmax_done = sem("lmax_done")
        chosen_done = sem("chosen_done")
        flag_done = sem("flag_done")
        slots_read = sem("slots_read")
        x_done = sem("x_done")
        def per_layer(name):
            return [sem(f"{name}{l}") for l in range(DEPTH)]

        d_jobs = per_layer("d_jobs")
        d_gexp = per_layer("d_gexp")
        d_act = per_layer("d_act")
        d_actT = per_layer("d_actT")
        d_added = per_layer("d_added")
        d_chain = per_layer("d_chain")
        r_jobs = per_layer("r_jobs")
        r_hot = per_layer("r_hot")
        r_rowsT = per_layer("r_rowsT")
        r_gexp = per_layer("r_gexp")
        r_act = per_layer("r_act")
        r_evac = per_layer("r_evac")
        r_added = per_layer("r_added")
        r_chain = per_layer("r_chain")
        dve_chain, pool_chain = sem("dve_chain"), sem("pool_chain")
        fin_done, out_done = sem("fin_done"), sem("out_done")

        def bank(name):
            return banks[NAMES.index(name) % 8]

        def wait_job(eng, L, name):
            eng.wait_ge(job_done, L * NJ + NAMES.index(name) + 1)

        def wait_emptied(eng, L, name):
            who = EMPTIER[name]
            eng.wait_ge(empt[who], L * EMPTIED[who] + NTH[name])

        def unit_source(L, u):
            name = UNITS[u]
            starts = {"hq": 0, "hf": 512, "hi": 1024, "hg": 1536, "aq": 2048, "ak": 2560, "av": 3072}
            if name in starts:
                t, n0 = w_in, starts[name]
            elif name == "router":
                return w_router[bass.ds(L, 1), :, :].rearrange("l (p c) n -> p (l c) n", c=C), N_GROUPS + N_EXPERTS
            else:
                t, n0 = {"k0": (wkv, 0), "k1": (wkv, 512), "v0": (wkv, 1024), "v1": (wkv, 1536), "o0": (w_out, 0),
                         "o1": (w_out, 512), "q0": (wq, 0), "q1": (wq, 512), "p0": (wo, 0), "p1": (wo, 512)}[name]
            return t[bass.ds(L, 1), :, n0:n0 + W].rearrange("l (p c) n -> p (l c) n", c=C), W

        def unit(name, n=W):
            return ring[:, UNITS.index(name) % SLOTS, 0:C * n].rearrange("p (c n) -> p c n", c=C)

        tots = []
        off = 0
        for j in range(1, 7):
            tots.append(TOT[:, :, off:off + (T >> j)])
            off += T >> j

        actb = work[:, 0, :].rearrange("p (m n) -> p m n", m=M)
        actT = work[:, 1, 0:W].rearrange("p (c t) -> p c t", c=4)
        gexp = work[:, 2, :].rearrange("p (m n) -> p m n", m=M)
        HALF_PI = float(np.pi / 2)

        logits = wsm[:, 0:40].rearrange("p (m n) -> p m n", m=M)
        ngmx = wsm[:, 40:42]
        gsum = wsm[:, 42:44]
        lexp = wsm[:, 44:52].rearrange("p (m n) -> p m n", m=M)
        e2 = wsm[:, 52:54]
        pad8 = wsm[:, 56:72].rearrange("p (m n) -> p m n", m=M)
        top8 = wsm[:, 72:88].rearrange("p (m n) -> p m n", m=M)
        idx8 = wsm[:, 88:104].rearrange("p (m n) -> p m n", m=M)
        oneg = wsm[:, 104:112].rearrange("p (m n) -> p m n", m=M)
        elog = wsm[:, 112:144].rearrange("p (m n) -> p m n", m=M)
        idxf = wsm[:, 144:160].rearrange("p (m n) -> p m n", m=M)
        io16 = wsm[:, 160:176]
        slotf = wsm[:, 216:220].rearrange("p (m k) -> p m k", m=M)
        base16 = wsm[:, 224:240]
        mostf = wsm[:, 240:241]
        most = wsm[:, 241:242].bitcast(I32)
        one2 = PT[:, 1, 0, 0:64].rearrange("p (m k n) -> p m k n", m=M, k=2)
        pick = PT[:, 1, 0, 64:128].rearrange("p (m k n) -> p m k n", m=M, k=2)
        rank = PT[:, 1, 1, 0:32].rearrange("p (m n) -> p m n", m=M)
        rowsT = hT[:, :, 0:P]
        ract, ractT, rexp = work[:, 0, 0:W], work[:, 1, 0:W].rearrange("p (c t) -> p c t", c=4), work[:, 2, 0:W]
        yrows = Vx[:, 0, :]
        hot = PT[:, 0, 0:2, :]
        gated = PT[:, 0, 2:4, :]
        gatedT = PT[:, 0, 4:6, :]
        hot1 = PT[:, 0, 6:8, :]
        w1 = wsm[:, 176:178]
        w2 = wsm[:, 178:180]
        sc2 = wsm[:, 180:182]
        one1 = wsm[:, 184:216].rearrange("p (m n) -> p m n", m=M)

        def either_way(eng, L, routed, dense, routed_first=None, routed_last=None, dense_first=None, dense_last=None):
            eng.wait_ge(flag_done, L + 1)
            fullest = eng.value_load(most[0:1, 0:1], min_val=0, max_val=T)
            with eng.If(fullest <= CAP):
                if routed_first:
                    routed_first()
                with eng.Fori(0, PAIRS) as p:
                    routed(p)
                if routed_last:
                    routed_last()
            with eng.Else():
                if dense_first:
                    dense_first()
                with eng.Fori(0, PAIRS) as p:
                    dense(p)
                if dense_last:
                    dense_last()

        block = ctx.enter_context(nc.Block())

        @block.sync
        def _(sp):
            for m in range(M):
                sp.dma_start(E[:, m * D:(m + 1) * D], mem_in[m * P:(m + 1) * P, :]).then_inc(mem_loaded[m], 16)
            sp.dma_start(gains[:, :, 0:36], gains_in).then_inc(small_loaded, 16)
            for L in range(DEPTH):
                for u, name in enumerate(UNITS):
                    if L == 0 and u == 1:
                        with nc.allow_non_contiguous_dma(reason="small vectors, once"):
                            sp.dma_start(early[:, 0:M].bitcast(I32), pos_in.rearrange("(m p) -> p m", p=P)).then_inc(small_loaded, 16)
                            sp.dma_start(early[:, 64:96], inv_in.partition_broadcast(P)).then_inc(small_loaded, 16)
                        sp.dma_start(x[:, :, :], x_in.rearrange("(m p) d -> p m d", p=P)).then_inc(x_loaded, 16)
                    s = u % SLOTS
                    if u < SLOTS:
                        if L:
                            sp.wait_ge(slots_read, 3 * PAIRS * L + s // 2 + 1)
                    else:
                        wait_job(sp, L, LAST_USE[UNITS[u - SLOTS]])
                    src, n = unit_source(L, u)
                    sp.dma_start(unit(name, n), src).then_inc(loaded[s], 16)
                with sp.Fori(0, PAIRS) as p:
                    for s in range(SLOTS):
                        e = sp.snap(2 * p + N_EXPERTS * L + s % 2)
                        wait_job(sp, L, LAST_USE[UNITS[(MIX_ROUNDS - 1) * SLOTS + s]])
                        sp.wait_ge(slots_read, 3 * PAIRS * L + s // 2 + 1 + 3 * p)
                        w = (w_gate, w_up, w_down)[s // 2]
                        sp.dma_start(ring[:, s, :], w[bass.ds(e, 1), :, :].rearrange("e p n -> p (e n)"))\
                          .then_inc(loaded[s], 16)

        @block.tensor
        def _(pe):
            def wait_unit(L, name):
                u = UNITS.index(name)
                pe.wait_ge(loaded[u % SLOTS], 16 * ROUNDS * L + 16 * (u // SLOTS + 1))

            def open_bank(L, name):
                i = NAMES.index(name)
                if i >= 8:
                    wait_emptied(pe, L, NAMES[i - 8])
                return banks[i % 8]

            def close(ins):
                ins.then_inc(job_done, 1)

            def transposes(L, name, src, rows=P):
                b = open_bank(L, name)
                for k, s in enumerate(src):
                    last = nc.tensor.transpose(b[:, k * P:(k + 1) * P], s, ident[:, :])
                close(last)

            def by_columns(src, m, c2):
                v = src[:, m, :].rearrange("p (k c) -> p c k", c=C)
                return [v[:, 4 * c2 + k, :] for k in range(4)]

            def project(L, name, lhs, m, w):
                b = open_bank(L, name)
                for c in range(C):
                    last = nc.tensor.matmul(b[:, :], lhs[:, c, m * P:(m + 1) * P], w[:, c, :], start=(c == 0), stop=(c == C - 1))
                close(last)

            def project_T(L, name, rhs, w, n2):
                b = open_bank(L, name)
                for k in range(2):
                    for c in range(C):
                        last = nc.tensor.matmul(b[:, k * T:(k + 1) * T], w[:, c, (n2 + k) * P:(n2 + k + 1) * P],
                                                rhs[:, c, :], start=(c == 0), stop=(c == C - 1))
                close(last)

            pe.wait_ge(ident_done, 2)
            memrow = E[:, 0:M * D].rearrange("p (m d) -> p m d", m=M)
            for m in range(M):
                pe.wait_ge(mem_scaled, m + 1)
                for c2 in range(2):
                    b = banks[4 + 2 * m + c2]
                    for k, s in enumerate(by_columns(memrow, m, c2)):
                        last = nc.tensor.transpose(b[:, k * P:(k + 1) * P], s, ident[:, :])
                    last.then_inc(mem_tr, 1)
            pe.wait_ge(mem_gained, 4)

            for L in range(DEPTH):
                if L:
                    pe.wait_ge(memg_done, L)
                for j in range(8):
                    if j < 4:
                        wait_unit(L, f"k{j // 2}")
                        project_T(L, f"kv{j}", hT, unit(f"k{j // 2}"), 2 * (j % 2))
                    else:
                        if j == 4 and L == 0:
                            pe.wait_ge(mem_kept, 4)
                        wait_unit(L, f"v{(j - 4) // 2}")
                        project(L, f"kv{j}", hT, j % 2, unit(f"v{(j - 4) // 2}"))
                for m in range(M):
                    pe.wait_ge(normed, 6 * L + m + 1)
                    for c2 in range(2):
                        transposes(L, f"t1_{m}{c2}", by_columns(xs, m, c2))
                wait_emptied(pe, L, "t1_11")
                for name in ("hf", "hq"):
                    wait_unit(L, name)
                    for k in range(2):
                        project_T(L, f"{name}{k}", hT, unit(name), 2 * k)

                def rows_by(name):
                    wait_unit(L, name[:2])
                    project(L, name, hT, int(name[2]), unit(name[:2]))

                rows_by("hi0")
                for j, (name, _) in enumerate(BETWEEN):
                    rows_by(name)
                    if j == 0:
                        pe.wait_ge(f_done, 2 * L + 2)
                        wait_emptied(pe, L, "hq1")
                    for m in range(M):
                        if j >= 1:
                            pe.wait_ge(q_done, 16 * L + 2 * (j - 1) + m + 1)
                        if j >= 2:
                            pe.wait_ge(k_done, 14 * L + 2 * (j - 2) + m + 1)
                        b = open_bank(L, f"lev{j}_{m}")
                        for a in range(HG_HEADS):
                            last = nc.tensor.matmul(b[:, a * P:(a + 1) * P], K[:, a, m * P:(m + 1) * P],
                                                    Q[:, a, m * P:(m + 1) * P], start=True, stop=True)
                        close(last)
                rows_by("hg1")
                for w, name in enumerate(("qT", "kT")):
                    for m in range(M):
                        pe.wait_ge(rot_done, 4 * L + 2 * w + m + 1)
                        rr = rot[:, (2 * w + m) * W:(2 * w + m + 1) * W]
                        transposes(L, f"{name}{m}", [rr[:, k * P:(k + 1) * P] for k in range(4)])
                pe.wait_ge(q_done, 16 * L + 16)
                pe.wait_ge(k_done, 14 * L + 14)
                b = open_bank(L, "cross")
                for a in range(HG_HEADS):
                    last = nc.tensor.matmul(b[:, a * P:(a + 1) * P], K[:, a, 0:P], Q[:, a, P:T], start=True, stop=True)
                close(last)
                wait_emptied(pe, L, "kT1")
                for k, (m, heads) in enumerate(SCORES):
                    n = (m + 1) * P
                    b = open_bank(L, f"s{k}")
                    for i, h in enumerate(heads):
                        r = 64 * (h % 2)
                        last = nc.tensor.matmul(b[:, i * n:(i + 1) * n], attT[r:r + 64, h // 2, m * P:(m + 1) * P],
                                                attT[r:r + 64, 4 + h // 2, 0:n], start=True, stop=True)
                    close(last)
                wait_emptied(pe, L, "cross")
                wait_emptied(pe, L, "hi1")
                for m in range(M):
                    b = open_bank(L, f"hp{m}")
                    for a in range(HG_HEADS):
                        o = b[:, a * P:(a + 1) * P]
                        last = nc.tensor.matmul(o, S[:, m, a, :], hi[:, m, a * P:(a + 1) * P], start=True, stop=(m == 0))
                        if m:
                            last = nc.tensor.matmul(o, S01[:, a, :], hi[:, 0, a * P:(a + 1) * P], start=False, stop=True)
                    close(last)
                for k in range(6):
                    if k == 0:
                        pe.wait_ge(e_done, 6 * L + 2)
                    if k == 2:
                        pe.wait_ge(e_done, 6 * L + 6)
                    if k < 2:
                        src = [E[:, (4 * k + i) * P:(4 * k + i + 1) * P] for i in range(4)]
                    else:
                        jb, h0 = (k - 2) // 2, 4 * (k % 2)
                        src = [E[:, D + (h0 + i) * T + jb * P:D + (h0 + i) * T + (jb + 1) * P] for i in range(4)]
                    transposes(L, f"et{k}", src)
                wait_emptied(pe, L, "av1")
                for m in range(M):
                    for g in range(2):
                        wait_emptied(pe, L, f"et{g}" if m == 0 else f"et{4 + g}")
                        b = open_bank(L, f"ap{m}{g}")
                        for i in range(4):
                            h = 4 * g + i
                            o = b[:, i * P:i * P + DH + 1]
                            last = nc.tensor.matmul(o, PT[:, 2 * m, h, :], vaug[:, m, h, :], start=True, stop=(m == 0))
                            if m:
                                last = nc.tensor.matmul(o, PT[:, 1, h, :], vaug[:, 0, h, :], start=False, stop=True)
                        close(last)
                for m in range(M):
                    pe.wait_ge(y_done, 4 * L + 2 + m + 1)
                    for c2 in range(2):
                        transposes(L, f"t2_{m}{c2}", by_columns(xs, m, c2))
                for m in range(M):
                    wait_emptied(pe, L, f"t2_{m}1")
                    for n in range(2):
                        wait_unit(L, f"o{n}")
                        project(L, f"wo{n}{m}", hT, m, unit(f"o{n}"))
                w = unit("q0")
                for m in range(M):
                    pe.wait_ge(normed, 6 * L + 2 + m + 1)
                    for c2 in range(2):
                        transposes(L, f"t3_{m}{c2}", by_columns(xs, m, c2))
                    wait_emptied(pe, L, f"t3_{m}1")
                    if m == 0:
                        wait_unit(L, "q0")
                        b = open_bank(L, "qx0")
                    for k in range(2):
                        for c in range(C):
                            last = nc.tensor.matmul(b[:, k * T + m * P:k * T + (m + 1) * P], w[:, c, k * P:(k + 1) * P],
                                                    hT[:, c, m * P:(m + 1) * P], start=(c == 0), stop=(c == C - 1))
                close(last)
                for k in range(1, 4):
                    wait_unit(L, f"q{k // 2}")
                    project_T(L, f"qx{k}", hT, unit(f"q{k // 2}"), 2 * (k % 2))
                wait_emptied(pe, L, "qx3")
                for m in range(M):
                    for g in range(2):
                        b = open_bank(L, f"sx{m}{g}")
                        for i in range(2):
                            h = 2 * g + i
                            for k in range(2):
                                last = nc.tensor.matmul(b[:, i * T:(i + 1) * T], QxT[:, 2 * h + k, m * P:(m + 1) * P],
                                                        KT[:, 2 * h + k, :], start=(k == 0), stop=(k == 1))
                        close(last)
                for m in range(M):
                    wait_emptied(pe, L, f"sx{m}1")
                    for jb in range(2):
                        transposes(L, f"pt{m}{jb}", [Px[:, m, h, jb * P:(jb + 1) * P] for h in range(X_HEADS)])
                for m in range(M):
                    wait_emptied(pe, L, f"pt{m}1")
                    for g in range(2):
                        b = open_bank(L, f"px{m}{g}")
                        for i in range(2):
                            h = 2 * g + i
                            for jb in range(2):
                                last = nc.tensor.matmul(b[:, i * T:(i + 1) * T], PTx[:, 2 * m + jb, h, :],
                                                        Vx[:, jb, h * T:(h + 1) * T], start=(jb == 0), stop=(jb == 1))
                        close(last)
                for m in range(M):
                    wait_emptied(pe, L, f"px{m}1")
                    for c2 in range(2):
                        transposes(L, f"t4_{m}{c2}", by_columns(xs, m, c2))
                for m in range(M):
                    wait_emptied(pe, L, f"t4_{m}1")
                    for n in range(2):
                        wait_unit(L, f"p{n}")
                        project(L, f"ox{n}{m}", hT, m, unit(f"p{n}"))
                NR = N_GROUPS + N_EXPERTS
                for m in range(M):
                    pe.wait_ge(normed, 6 * L + 4 + m + 1)
                    for c2 in range(2):
                        transposes(L, f"t5_{m}{c2}", by_columns(xs, m, c2))
                    wait_emptied(pe, L, f"t5_{m}1")
                    if m == 0:
                        wait_unit(L, "router")
                        b = open_bank(L, "rt")
                    for c in range(C):
                        last = nc.tensor.matmul(b[0:NR, m * P:(m + 1) * P], unit("router", NR)[:, c, :], hT[:, c, m * P:(m + 1) * P],
                                                start=(c == 0), stop=(c == C - 1))
                close(last)
                wait_emptied(pe, L, "rt")
                b = open_bank(L, "rl")
                for m in range(M):
                    last = nc.tensor.transpose(b[:, m * NR:(m + 1) * NR], early[0:NR, m * P:(m + 1) * P], ident[0:NR, 0:NR])
                close(last)
                pe.wait_ge(chosen_done, L + 1)
                b = open_bank(L, "rank")
                NE = N_EXPERTS
                nc.tensor.matmul(b[:, 0:NE], before[:, :], chosen[:, 0, :], start=True, stop=True)
                nc.tensor.matmul(b[:, NE:2 * NE], before[:, :], chosen[:, 1, :], start=True, stop=False)
                nc.tensor.matmul(b[:, NE:2 * NE], ones[:, :], chosen[:, 0, :], start=False, stop=True)
                nc.tensor.matmul(b[:, 2 * NE:3 * NE], ones[:, :], chosen[:, 0, :], start=True, stop=False)
                close(nc.tensor.matmul(b[:, 2 * NE:3 * NE], ones[:, :], chosen[:, 1, :], start=False, stop=True))

                def fill(p, s):
                    pe.wait_ge(loaded[s], 16 * ROUNDS * L + 16 * p + 16 * (MIX_ROUNDS + 1))

                def routed_job(last):
                    last.then_inc(r_jobs[L], 1)

                def gather(n):
                    pe.wait_ge(r_hot[L], n)
                    for c2 in range(2):
                        for k in range(4):
                            for m in range(M):
                                cols = xs[:, m, :].rearrange("p (k c) -> p c k", c=C)[:, 4 * c2 + k, :]
                                last = nc.tensor.matmul(banks[c2][:, k * P:(k + 1) * P], cols, hot[:, m, :], start=(m == 0), stop=(m == M - 1))
                        routed_job(last)

                def first_rows():
                    gather(1)

                def routed(p):
                    pe.wait_ge(r_rowsT[L], 2 * p + 2)
                    for g in range(2):
                        for b2 in range(2):
                            fill(p, 2 * g + b2)
                        for c in range(C):
                            for b2 in range(2):
                                w = ring[:, 2 * g + b2, c * W:(c + 1) * W]
                                last = nc.tensor.matmul(banks[2 + g][b2 * CAP:(b2 + 1) * CAP, :], rowsT[:, c, b2 * CAP:(b2 + 1) * CAP],
                                                        w, start=(c == 0), stop=(c == C - 1))
                        routed_job(last)
                    pe.wait_ge(r_added[L], 4 * p + 4)
                    pe.wait_ge(r_hot[L], 2 * p + 2)
                    for m in range(M):
                        last = nc.tensor.transpose(banks[7][:, m * P:(m + 1) * P], gated[:, m, :], ident[:, :])
                    routed_job(last)
                    pe.wait_ge(r_act[L], p + 1)
                    av = ract.rearrange("p (k c) -> p c k", c=4)
                    for k in range(4):
                        last = nc.tensor.transpose(banks[4][:, k * P:(k + 1) * P], av[:, k, :], ident[:, :])
                    routed_job(last)
                    pe.wait_ge(r_evac[L], 4 * p + 2)
                    for b2 in range(2):
                        fill(p, 4 + b2)
                    for n in range(2):
                        for c in range(4):
                            for b2 in range(2):
                                w = ring[:, 4 + b2, c * D + n * W:c * D + (n + 1) * W]
                                last = nc.tensor.matmul(banks[5 + n][b2 * CAP:(b2 + 1) * CAP, :], ractT[:, c, b2 * CAP:(b2 + 1) * CAP],
                                                        w, start=(c == 0), stop=(c == 3))
                        routed_job(last)
                    gather(2 * p + 3)
                    pe.wait_ge(r_evac[L], 4 * p + 4)
                    for n in range(2):
                        for m in range(M):
                            routed_job(nc.tensor.matmul(banks[OUT_BANK[n][m]][:, :], gatedT[:, m, :], yrows[:, n * W:(n + 1) * W],
                                                        start=True, stop=True))

                def dense(p):
                    n4 = 4 * p + 4
                    for b2 in range(2):
                        for s in (b2, 2 + b2):
                            fill(p, s)
                            w = ring[:, s, :].rearrange("p (c n) -> p c n", c=C)
                            for m in range(M):
                                if s < 2:
                                    pe.wait_ge(d_act[L], n4 + 2 * b2)
                                for c in range(C):
                                    last = nc.tensor.matmul(banks[(0 if s < 2 else 2) + m][:, :], hT[:, c, m * P:(m + 1) * P],
                                                            w[:, c, :], start=(c == 0), stop=(c == C - 1))
                                last.then_inc(d_jobs[L], 1)
                        for m in range(M):
                            pe.wait_ge(d_act[L], n4 + 2 * b2 + m + 1)
                            pe.wait_ge(d_actT[L], n4 + 2 * b2 + m)
                            av = actb[:, m, :].rearrange("p (k c) -> p c k", c=4)
                            for k in range(4):
                                last = nc.tensor.transpose(banks[4][:, k * P:(k + 1) * P], av[:, k, :], ident[:, :])
                            last.then_inc(d_jobs[L], 1)
                            pe.wait_ge(d_actT[L], n4 + 2 * b2 + m + 1)
                            if m == 0:
                                fill(p, 4 + b2)
                            w = ring[:, 4 + b2, :].rearrange("p (c n) -> p c n", c=4)
                            for n in range(2):
                                pe.wait_ge(d_added[L], 2 * n4 + 4 * b2 + 2 * m)
                                for c in range(4):
                                    last = nc.tensor.matmul(banks[5 + n][:, :], actT[:, c, :], w[:, c, n * W:(n + 1) * W],
                                                            start=(c == 0), stop=(c == 3))
                                last.then_inc(d_jobs[L], 1)

                def routed_banks():
                    pe.wait_ge(r_added[L], 4 * PAIRS + 4)

                def dense_banks():
                    pe.wait_ge(d_added[L], 8 * PAIRS + 8)

                either_way(pe, L, routed, dense, first_rows, routed_banks, None, dense_banks)

        @block.scalar
        def _(act):
            for l in range(DEPTH):
                act.sem_inc(d_actT[l], 4)
            act.wait_ge(zeroed, 1)
            nc.scalar.activation(sm[:, 108:109], sm[:, 109:110], ACT.Square)
            for m in range(M):
                act.wait_ge(mem_loaded[m], 16)
                nc.scalar.activation(sq, E[:, m * D:(m + 1) * D], ACT.Square, accum_out=mss[:, m:m + 1]).then_inc(mem_sq, 1)
                act.wait_ge(mem_sq, m + 1)
            for m in range(M):
                for c2 in range(2):
                    act.wait_ge(mem_gained, 2 * m + c2 + 1)
                    nc.scalar.activation(memT[:, 4 * c2:4 * c2 + 4, m * P:(m + 1) * P],
                                         banks[4 + 2 * m + c2][:, :].rearrange("p (c t) -> p c t", c=4), ACT.Copy).then_inc(mem_kept, 1)
            act.wait_ge(lb_max, 1)
            nc.scalar.activation(gains[:, :, 36:40], gains[:, :, 36:40], ACT.Exp).then_inc(lb_exp, 1)
            act.wait_ge(trig_arg, 1)
            nc.scalar.activation(cosT[:, :, :], cosT[:, :, :], ACT.Sin)
            nc.scalar.activation(sinT[:, :, :], sinT[:, :, :], ACT.Sin).then_inc(tables_done, 1)

            def squares(count, ready=None):
                for m in range(M):
                    if ready:
                        wait_emptied(act, L, f"{ready}{m}")
                    nc.scalar.activation(sq, x[:, m, :], ACT.Square, accum_out=ss[:, m:m + 1]).then_inc(sq_done, 1)
                    act.wait_ge(sq_done, count + m + 1)

            for L in range(DEPTH):
                act.wait_ge(y_done, 4 * L)
                with nc.allow_non_contiguous_dma(reason="one row to all partitions"):
                    act.dma_start(og[:, :], og_in[L:L + 1, :].rearrange("l n -> (l n)").partition_broadcast(P)).then_inc(og_loaded, 16)

                def empty(name, dst, func=ACT.Copy, scale=1.0, view=None):
                    wait_job(act, L, name)
                    src = bank(name)[:, :] if view is None else view
                    nc.scalar.activation(dst, src, func, scale=scale).then_inc(empt["A"], 1)

                def halves(name):
                    return bank(name)[:, :].rearrange("p (a t) -> p a t", a=2)

                def empty_kv(j):
                    if j < 4:
                        empty(f"kv{j}", KT[:, 2 * j:2 * j + 2, :], view=halves(f"kv{j}"))
                    else:
                        empty(f"kv{j}", Vx[:, j % 2, ((j - 4) // 2) * W:((j - 4) // 2 + 1) * W])

                if L == 0:
                    act.wait_ge(x_loaded, 16)
                    squares(6 * L)
                for j in range(KV_EARLY):
                    empty_kv(j)
                if L:
                    act.wait_ge(x_done, L)
                    squares(6 * L)
                for j in range(KV_EARLY, 8):
                    empty_kv(j)
                for k in range(2):
                    empty(f"hf{k}", F[:, 2 * k:2 * k + 2, :], ACT.Exp, -1.0, halves(f"hf{k}"))
                for k in range(2):
                    empty(f"hq{k}", Q[:, 2 * k:2 * k + 2, :], view=halves(f"hq{k}"))
                for m in range(M):
                    empty(f"hi{m}", hi[:, m, :])
                for m in range(M):
                    empty(f"av{m}", vaug[:, m, :, 0:DH], view=bank(f"av{m}")[:, :].rearrange("p (h d) -> p h d", d=DH))
                for m in range(M):
                    wait_job(act, L, f"hg{m}")
                    nc.scalar.activation(gg[:, m, :], bank(f"hg{m}")[:, :], ACT.Exp, scale=-1.0).then_inc(gate_exp, 1)
                for w, name in enumerate(("qT", "kT")):
                    for m in range(M):
                        empty(f"{name}{m}", attT[:, 4 * w:4 * w + 4, m * P:(m + 1) * P], scale=(DH ** -0.5 if w == 0 else 1.0),
                              view=bank(f"{name}{m}")[:, :].rearrange("p (g t) -> p g t", t=P))
                at = 0
                for k, (m, heads) in enumerate(SCORES):
                    act.wait_ge(max_done, 6 * L + k + 1)
                    n = (m + 1) * P
                    for h in heads:
                        e = E[:, m * D + h * n:m * D + (h + 1) * n]
                        last = nc.scalar.activation(e, e, ACT.Exp, bias=nmx[:, at:at + 1])
                        at += 1
                    last.then_inc(e_done, 1)
                for m in range(M):
                    wait_job(act, L, f"hp{m}")
                    nc.scalar.activation(rot[:, m * W:(m + 1) * W], bank(f"hp{m}")[:, :], ACT.Square).then_inc(hsq_done, 1)

                def rows_T(t):
                    for m in range(M):
                        for c2 in range(2):
                            empty(f"{t}_{m}{c2}", hT[:, 4 * c2:4 * c2 + 4, m * P:(m + 1) * P],
                                  view=bank(f"{t}_{m}{c2}")[:, :].rearrange("p (c t) -> p c t", c=4))

                wait_job(act, L, "kv7")
                rows_T("t2")
                squares(6 * L + 2, "wo1")
                act.wait_ge(hms_done, 2 * L + 2)
                for k in range(4):
                    empty(f"qx{k}", QxT[:, 2 * k:2 * k + 2, :], view=halves(f"qx{k}"))
                for m in range(M):
                    for g in range(2):
                        act.wait_ge(xmax_done, 4 * L + 2 * m + g + 1)
                        for i in range(2):
                            h = 2 * g + i
                            last = nc.scalar.activation(Px[:, m, h, :], bank(f"sx{m}{g}")[:, i * T:(i + 1) * T], ACT.Exp,
                                                        bias=xmx[:, m, h:h + 1], scale=X_DH ** -0.5, accum_out=xden[:, m, h:h + 1])
                        last.then_inc(empt["A"], 1)
                rows_T("t4")
                squares(6 * L + 4, "ox1")
                empty("rt", early[0:20, 0:T], view=bank("rt")[0:20, 0:T])
                act.wait_ge(lmax_done, 2 * L + 1)
                for m in range(M):
                    last = nc.scalar.activation(lexp[:, m, :], logits[:, m, 0:N_GROUPS], ACT.Exp, bias=ngmx[:, m:m + 1],
                                                accum_out=gsum[:, m:m + 1])
                last.then_inc(lexp_done, 1)
                act.wait_ge(lmax_done, 2 * L + 2)
                nc.scalar.activation(e2[:, :], e2[:, :], ACT.Exp).then_inc(lexp_done, 1)

                def routed(p):
                    jobs = 2 + ROUTED_JOBS * p
                    act.wait_ge(r_jobs[L], jobs + 1)
                    nc.scalar.activation(rexp, banks[2][:, :], ACT.Exp, scale=-1.0).then_inc(r_gexp[L], 1)
                    act.wait_ge(r_jobs[L], jobs + 3)
                    nc.scalar.activation(gatedT, banks[7][:, 0:M * P].rearrange("p (m t) -> p m t", m=M), ACT.Copy).then_inc(r_evac[L], 1)
                    act.wait_ge(r_jobs[L], jobs + 4)
                    nc.scalar.activation(ractT, banks[4][:, :].rearrange("p (c t) -> p c t", c=4), ACT.Copy).then_inc(r_evac[L], 1)
                    for n in range(2):
                        act.wait_ge(r_jobs[L], jobs + 5 + n)
                        nc.scalar.activation(yrows[:, n * W:(n + 1) * W], banks[5 + n][:, :], ACT.Copy).then_inc(r_evac[L], 1)

                def dense(p):
                    n4 = 4 * p + 4
                    for b2 in range(2):
                        for m in range(M):
                            act.wait_ge(d_jobs[L], DENSE_JOBS * p + 10 * b2 + m + 1)
                            act.wait_ge(d_act[L], n4 + 2 * b2)
                            nc.scalar.activation(gexp[:, m, :], banks[m][:, :], ACT.Exp, scale=-1.0).then_inc(d_gexp[L], 1)
                        for m in range(M):
                            act.wait_ge(d_jobs[L], DENSE_JOBS * p + 10 * b2 + 4 + 3 * m + 1)
                            nc.scalar.activation(actT[:, :, :], banks[4][:, :].rearrange("p (c t) -> p c t", c=4), ACT.Copy)\
                              .then_inc(d_actT[L], 1)

                either_way(act, L, routed, dense)

            act.wait_ge(x_done, DEPTH)
            act.wait_ge(y_done, 4 * DEPTH)
            with nc.allow_non_contiguous_dma(reason="one row to all partitions"):
                act.dma_start(Vx[:, 0, :], nf_in.partition_broadcast(P)).then_inc(nf_loaded, 16)
            squares(6 * DEPTH)
            for m in range(M):
                act.wait_ge(fin_done, m + 1)
                act.dma_start(out[m * P:(m + 1) * P, :], xs[:, m, :]).then_inc(out_done, 16)
            act.wait_ge(out_done, 16 * M)

        @block.gpsimd
        def _(pool):
            chain = Chain(pool, pool_chain)
            link = chain.link
            nc.gpsimd.memset(sm[:, :], 0.0).then_inc(zeroed, 1)
            pool.wait_ge(zeroed, 1)
            nc.gpsimd.iota(PT[:, 0, 0, :].bitcast(I32), pattern=[[1, P]], base=P, channel_multiplier=-1)
            nc.gpsimd.iota(PT[:, 1, 0, :].bitcast(I32), pattern=[[1, P]], base=0, channel_multiplier=0)
            nc.gpsimd.iota(PT[:, 1, 1, :].bitcast(I32), pattern=[[0, P]], base=0, channel_multiplier=1).then_inc(iota_done, 1)
            nc.gpsimd.iota(io16, pattern=[[1, N_EXPERTS]], base=0, channel_multiplier=0, allow_small_or_imprecise_dtypes=True)\
              .then_inc(iota_done, 1)
            nc.gpsimd.iota(columns[:, :], pattern=[[1, P]], base=0, channel_multiplier=0, allow_small_or_imprecise_dtypes=True)
            link(nc.gpsimd.memset(expo, -0.5))
            nc.gpsimd.memset(ident[:, :], 0.0).then_inc(ident_done, 1)
            pool.wait_ge(ident_done, 1)
            nc.gpsimd.affine_select(out=ident[:, :], in_=ident[:, :], compare_op=ALU.not_equal, fill=1.0, base=0,
                                    pattern=[[-1, P]], channel_multiplier=1).then_inc(ident_done, 1)
            nc.gpsimd.memset(S[:, :, :, :], 0.0)
            nc.gpsimd.memset(pad8[:, :, :], NEG)
            nc.gpsimd.memset(vaug[:, :, :, :], 1.0).then_inc(zeroed, 1)

            def root(dst, src, n, width):
                link(nc.gpsimd.tensor_scalar(dst, src, 1.0 / n, EPS, ALU.mult, ALU.add))
                return nc.gpsimd.tensor_tensor(dst, dst, expo[:, 0:width], ALU.pow)

            for m in range(M):
                pool.wait_ge(mem_sq, m + 1)
                root(mrs[:, m:m + 1], mss[:, m:m + 1], D, 1).then_inc(mem_rstd, 1)

            def memory(L):
                pool.wait_ge(small_loaded, 48)
                pool.wait_ge(mem_kept, 4)
                nc.gpsimd.tensor_tensor(hT[:, :, :], memT[:, :, :], gains[:, L, 16:24].unsqueeze(2).to_broadcast([P, C, T]), ALU.mult)\
                  .then_inc(memg_done, 1)

            for L in range(DEPTH):
                def norm(k):
                    for m in range(M):
                        pool.wait_ge(sq_done, 6 * L + 2 * k + m + 1)
                        root(rstd[:, m:m + 1], ss[:, m:m + 1], D, 1).then_inc(rstd_done, 1)

                norm(0)
                tot_n = 0
                pool.wait_ge(f_done, 2 * L + 2)
                for prev, cu in zip([F] + tots, tots):
                    pv = prev.rearrange("p a (b u) -> p a b u", u=2)
                    nc.gpsimd.tensor_tensor(cu, pv[:, :, :, 0], pv[:, :, :, 1], ALU.mult).then_inc(tot_done, 1)
                    tot_n += 1
                    pool.wait_ge(tot_done, 6 * L + tot_n)
                for j in range(7):
                    h = 1 << j
                    tj = [F] + tots
                    for m in range(M):
                        kv = K[:, :, m * P:(m + 1) * P].rearrange("p a (b u i) -> p a b u i", u=2, i=h)[:, :, :, 0, :]
                        tv = tj[j][:, :, m * (P // h):(m + 1) * (P // h)].rearrange("p a (b u) -> p a b u", u=2)[:, :, :, 1]
                        wait_job(pool, L, f"lev{j + 1}_{m}")
                        nc.gpsimd.tensor_tensor(kv, kv, tv.unsqueeze(3).to_broadcast([P, HG_HEADS, P // (2 * h), h]), ALU.mult)\
                          .then_inc(k_done, 1)
                        pool.wait_ge(k_done, 14 * L + 2 * j + m + 1)
                for m in range(M):
                    pool.wait_ge(hms_done, 2 * L + m + 1)
                    root(hrs[:, m, :], hss[:, m, :], P, HG_HEADS).then_inc(hrs_done, 1)
                norm(1)
                norm(2)

                pool.wait_ge(flag_done, L + 1)
                fullest = pool.value_load(most[0:1, 0:1], min_val=0, max_val=T)
                with pool.If(fullest <= CAP):
                    pool.wait_ge(r_rowsT[L], 2 * PAIRS + 2)
                    if L + 1 < DEPTH:
                        memory(L + 1)
                with pool.Else():
                    pool.wait_ge(d_jobs[L], DENSE_JOBS * PAIRS)
                    if L + 1 < DEPTH:
                        memory(L + 1)
            for m in range(M):
                pool.wait_ge(sq_done, 6 * DEPTH + m + 1)
                root(rstd[:, m:m + 1], ss[:, m:m + 1], D, 1).then_inc(rstd_done, 1)

        @block.vector
        def _(dve):
            chain = Chain(dve, dve_chain)
            link = chain.link
            V = nc.vector
            for l in range(DEPTH):
                dve.sem_inc(d_act[l], 4)
                dve.sem_inc(d_added[l], 8)
                dve.sem_inc(r_added[l], 4)
            dve.sem_inc(slots_read, 3)
            for m in range(M):
                dve.wait_ge(mem_loaded[m], 16)
                dve.wait_ge(mem_rstd, m + 1)
                V.tensor_scalar(E[:, m * D:(m + 1) * D], E[:, m * D:(m + 1) * D], mrs[:, m:m + 1], None, ALU.mult).then_inc(mem_scaled, 1)
            dve.wait_ge(small_loaded, 48)
            for m in range(M):
                for c2 in range(2):
                    dve.wait_ge(mem_tr, 2 * m + c2 + 1)
                    V.tensor_tensor(hT[:, 4 * c2:4 * c2 + 4, m * P:(m + 1) * P],
                                    banks[4 + 2 * m + c2][:, :].rearrange("p (c t) -> p c t", c=4),
                                    gains[:, 0, 16 + 4 * c2:20 + 4 * c2].unsqueeze(2).to_broadcast([P, 4, P]), ALU.mult)\
                     .then_inc(mem_gained, 1)
            lb = [gains[:, l, 32:36] for l in range(DEPTH)]
            ex = [gains[:, l, 36:40] for l in range(DEPTH)]
            mx, tot = early[:, 100:104], early[:, 104:108]
            link(V.tensor_tensor(mx, lb[0], lb[1], ALU.max))
            V.tensor_tensor(ex[0], lb[0], mx, ALU.subtract)
            V.tensor_tensor(ex[1], lb[1], mx, ALU.subtract).then_inc(lb_max, 1)
            link(V.tensor_copy(posf, early[:, 0:M].bitcast(I32)))
            for m in range(M):
                last = V.tensor_scalar(sinT[:, m, :], early[:, 64:96], posf[:, m:m + 1], None, ALU.mult)
            link(last)
            ang = sinT[:, :, :].rearrange("p m k -> p (m k)")
            red = cosT[:, :, :].rearrange("p m k -> p (m k)")
            turns = early[:, 128:192]
            MAGIC = 1.5 * 2.0 ** 23
            two_pi = 2.0 * np.pi
            c1 = 6.28125
            c2 = float(np.float32(np.round((two_pi - c1) * 2.0 ** 20) / 2.0 ** 20))
            c3 = float(two_pi - c1 - c2)
            for table, shift in ((red, 0.25), (ang, 0.0)):
                link(V.tensor_scalar(turns, ang, 1.0 / two_pi, shift, ALU.mult, ALU.add))
                link(V.tensor_scalar(turns, turns, MAGIC, None, ALU.add))
                link(V.tensor_scalar(turns, turns, MAGIC, None, ALU.subtract))
                link(V.scalar_tensor_tensor(table, turns, -c1, ang, ALU.mult, ALU.add))
                link(V.scalar_tensor_tensor(table, turns, -c2, table, ALU.mult, ALU.add))
                link(V.scalar_tensor_tensor(table, turns, -c3, table, ALU.mult, ALU.add))
                if shift:
                    link(V.tensor_scalar(table, table, HALF_PI, None, ALU.add))
                link(V.tensor_scalar(table, table, 3.1415925, -3.1415925, ALU.min, ALU.max))
            V.tensor_copy(sm[:, 106:107], sm[:, 107:108]).then_inc(trig_arg, 1)
            dve.wait_ge(iota_done, 2)
            dve.wait_ge(zeroed, 2)
            dif, fi, pi = (PT[:, 0, 0, :].bitcast(I32), PT[:, 1, 0, :].bitcast(I32), PT[:, 1, 1, :].bitcast(I32))
            tmp = PT[:, 2, 0, :].bitcast(I32)
            ge, le, m4, m16 = (PT[:, 2, k, :] for k in range(1, 5))
            V.tensor_scalar(ge, dif, float(P), None, ALU.is_ge)
            V.tensor_scalar(le, dif, float(P), None, ALU.is_le)
            link(V.tensor_scalar(tmp, dif, 3, None, ALU.bitwise_and))
            link(V.tensor_scalar(m4, tmp, 0.0, None, ALU.is_equal))
            link(V.tensor_scalar(tmp, dif, 15, None, ALU.bitwise_and))
            link(V.tensor_scalar(m16, tmp, 0.0, None, ALU.is_equal))
            V.tensor_scalar(before[:, :], dif, float(P), None, ALU.is_gt)
            V.memset(ones[:, :], 1.0)
            V.tensor_scalar(base16, io16, float(CAP), None, ALU.mult)
            V.tensor_scalar(bias0[:, :], le, 1.0, -NEG, ALU.subtract, ALU.mult)
            link(V.tensor_tensor(bias10[:, :], ge, m4, ALU.max))
            link(V.tensor_scalar(bias10[:, :], bias10[:, :], 1.0, -NEG, ALU.subtract, ALU.mult))
            link(V.tensor_tensor(m4, m4, m16, ALU.add))
            link(V.tensor_tensor(cnt[:, 1, :], le, m4, ALU.add))
            link(V.tensor_scalar(m4, m4, 1.0, None, ALU.add))
            link(V.tensor_tensor(cnt[:, 0, :], ge, m4, ALU.mult))
            link(V.tensor_tensor(fi, fi, pi, ALU.bitwise_xor))
            V.tensor_scalar(lev[:, 0, :], dif, float(P), None, ALU.is_equal)
            for j in range(7):
                link(V.tensor_scalar(tmp, fi, j, None, ALU.logical_shift_right))
                link(V.tensor_scalar(lev[:, j + 1, :], tmp, 1.0, None, ALU.is_equal))
                link(V.tensor_tensor(lev[:, j + 1, :], lev[:, j + 1, :], ge, ALU.mult))
            dve.wait_ge(lb_exp, 1)
            link(V.tensor_tensor(tot, ex[0], ex[1], ALU.add))
            link(V.reciprocal(tot, tot))
            V.tensor_tensor(ex[0], ex[0], tot, ALU.mult)
            link(V.tensor_tensor(ex[1], ex[1], tot, ALU.mult))
            link(V.tensor_tensor(lb[1], ex[0], ex[1], ALU.add))
            V.tensor_tensor(lb[0], ex[0], ex[0], ALU.subtract)
            link(V.tensor_tensor(lb[1], lb[1], ex[0], ALU.subtract))
            for l in range(DEPTH):
                last = V.tensor_scalar(ex[l], lb[l], -1.0, 1.0, ALU.mult, ALU.add)
            last.then_inc(gains_done, 1)
            dve.wait_ge(tables_done, 1)
            dve.wait_ge(gains_done, 1)

            def scale_tile(L, k, m):
                dve.wait_ge(rstd_done, 6 * L + 2 * k + m + 1)
                V.tensor_scalar(xs[:, m, :], x[:, m, :], rstd[:, m:m + 1], None, ALU.mult).then_inc(normed, 1)

            for L in range(DEPTH):

                def emptied(ins):
                    ins.then_inc(empt["D"], 1)

                def rows_T(t, m, g0):
                    for c2 in range(2):
                        wait_job(dve, L, f"{t}_{m}{c2}")
                        emptied(V.tensor_tensor(hT[:, 4 * c2:4 * c2 + 4, m * P:(m + 1) * P],
                                                bank(f"{t}_{m}{c2}")[:, :].rearrange("p (c t) -> p c t", c=4),
                                                gains[:, L, g0 + 4 * c2:g0 + 4 * c2 + 4].unsqueeze(2).to_broadcast([P, 4, P]), ALU.mult))

                for m in range(M):
                    scale_tile(L, 0, m)
                for m in range(M):
                    rows_T("t1", m, 0)
                Fall = F[:, :, :].rearrange("p a t -> p (a t)")
                wait_emptied(dve, L, "hf1")
                link(V.tensor_scalar(Fall, Fall, 1.0, None, ALU.add))
                link(V.reciprocal(Fall, Fall))
                for a in range(HG_HEADS):
                    last = V.tensor_scalar(F[:, a, :], F[:, a, :], gains[:, L, 36 + a:37 + a], gains[:, L, 32 + a:33 + a], ALU.mult, ALU.add)
                last.then_inc(f_done, 1)
                dve.wait_ge(f_done, 2 * L + 1)
                V.tensor_scalar(K[:, :, :].rearrange("p a t -> p (a t)"), Fall, -1.0, 1.0, ALU.mult, ALU.add).then_inc(f_done, 1)
                dve.wait_ge(og_loaded, 16 * L + 16)

                def rotate(w, m):
                    name = f"{('aq', 'ak')[w]}{m}"
                    wait_job(dve, L, name)
                    t = bank(name)[:, :].rearrange("p (h u i) -> p h u i", u=2, i=32)
                    r = rot[:, (2 * w + m) * W:(2 * w + m + 1) * W].rearrange("p (h u i) -> p h u i", u=2, i=32)
                    b = PT[:, 0, 0:4, :].rearrange("p a (h u i) -> p (a h) u i", u=2, i=32)
                    cs = cosT[:, m, :].unsqueeze(1).unsqueeze(1).to_broadcast([P, ATT_HEADS, 2, 32])
                    sn = sinT[:, m, :].unsqueeze(1).unsqueeze(1).to_broadcast([P, ATT_HEADS, 2, 32])
                    V.tensor_tensor(r, t, cs, ALU.mult)
                    emptied(V.tensor_tensor(b, t, sn, ALU.mult))
                    wait_emptied(dve, L, name)
                    V.tensor_tensor(r[:, :, 0, :], r[:, :, 0, :], b[:, :, 1, :], ALU.subtract)
                    V.tensor_tensor(r[:, :, 1, :], r[:, :, 1, :], b[:, :, 0, :], ALU.add).then_inc(rot_done, 1)

                def gate(m):
                    dve.wait_ge(gate_exp, 2 * L + m + 1)
                    g = gg[:, m, :]
                    link(V.tensor_scalar(g, g, 1.0, None, ALU.add))
                    link(V.reciprocal(g, g))
                    link(V.tensor_tensor(g, bank(f"hg{m}")[:, :], g, ALU.mult))
                    emptied(V.tensor_tensor(g, g, og[:, :], ALU.mult))

                dve.wait_ge(tot_done, 6 * L + 6)
                tj = [F] + tots
                for j, (name, _) in enumerate(BETWEEN):
                    if name[:2] in ("aq", "ak"):
                        rotate(("aq", "ak").index(name[:2]), int(name[2]))
                    elif name == "hg0":
                        gate(0)
                    for m in range(M):
                        wait_job(dve, L, f"lev{j}_{m}")
                        emptied(V.copy_predicated(S[:, m, :, :], lev[:, j, :].bitcast(I32).unsqueeze(1).to_broadcast([P, HG_HEADS, P]),
                                                  bank(f"lev{j}_{m}")[:, :].rearrange("p (a t) -> p a t", t=P)))
                        Qm = Q[:, :, m * P:(m + 1) * P]
                        if j == 0:
                            V.tensor_tensor(Qm, Qm, F[:, :, m * P:(m + 1) * P], ALU.mult).then_inc(q_done, 1)
                        else:
                            h = 1 << (j - 1)
                            qv = Qm.rearrange("p a (b u i) -> p a b u i", u=2, i=h)[:, :, :, 1, :]
                            tv = tj[j - 1][:, :, m * (P // h):(m + 1) * (P // h)].rearrange("p a (b u) -> p a b u", u=2)[:, :, :, 0]
                            V.tensor_tensor(qv, qv, tv.unsqueeze(3).to_broadcast([P, HG_HEADS, P // (2 * h), h]), ALU.mult)\
                             .then_inc(q_done, 1)
                        dve.wait_ge(q_done, 16 * L + 2 * j + m + 1)
                gate(1)
                wait_job(dve, L, "cross")
                emptied(V.tensor_copy(S01[:, :, :], bank("cross")[:, :].rearrange("p (a t) -> p a t", t=P)))
                at = 0
                dve.wait_ge(k_done, 14 * L + 14)
                for k, (m, heads) in enumerate(SCORES):
                    wait_job(dve, L, f"s{k}")
                    n, nh, h0 = (m + 1) * P, len(heads), heads[0]
                    eh = E[:, m * D:m * D + ATT_HEADS * n].rearrange("p (g u n) -> p g u n", u=2, n=n)
                    e = eh[:, h0 // 2:h0 // 2 + nh, h0 % 2, :]
                    src = bank(f"s{k}")[:, :].rearrange("p (g n) -> p g n", n=n)
                    if m:
                        V.tensor_tensor(e[:, :, 0:P], src[:, :, 0:P], bias10[:, :].unsqueeze(1).to_broadcast([P, nh, P]), ALU.add)
                    last = V.tensor_tensor(e[:, :, n - P:n], src[:, :, n - P:n], bias0[:, :].unsqueeze(1).to_broadcast([P, nh, P]), ALU.add)
                    emptied(last)
                    wait_emptied(dve, L, f"s{k}")
                    V.tensor_reduce(nmx[:, at:at + nh], e, AX, ALU.max, negate=True).then_inc(max_done, 1)
                    at += nh
                for m in range(M):
                    dve.wait_ge(hsq_done, 2 * L + m + 1)
                    V.tensor_reduce(hss[:, m, :], rot[:, m * W:(m + 1) * W].rearrange("p (h v) -> p h v", v=P), AX, ALU.add).then_inc(hms_done, 1)
                wait_job(dve, L, "s5")
                for m in range(M):
                    y = xs[:, m, 0:W]
                    emptied(V.tensor_tensor(y, bank(f"hp{m}")[:, :], gg[:, m, :], ALU.mult))
                    wait_emptied(dve, L, f"hp{m}")
                    dve.wait_ge(hrs_done, 2 * L + m + 1)
                    yh = y.rearrange("p (h v) -> p h v", v=P)
                    V.tensor_tensor(yh, yh, hrs[:, m, :].unsqueeze(2).to_broadcast([P, HG_HEADS, P]), ALU.mult).then_inc(y_done, 1)
                for k in range(6):
                    wait_job(dve, L, f"et{k}")
                    blk = 0 if k < 2 else 1 + (k - 2) // 2
                    c = cnt[:, 1 if blk == 1 else 0, :]
                    emptied(V.tensor_tensor(PT[:, blk, 4 * (k % 2):4 * (k % 2) + 4, :], bank(f"et{k}")[:, :].rearrange("p (h t) -> p h t", t=P),
                                            c.unsqueeze(1).to_broadcast([P, 4, P]), ALU.mult))
                for m in range(M):
                    for g in range(2):
                        wait_job(dve, L, f"ap{m}{g}")
                        o = bank(f"ap{m}{g}")[:, :].rearrange("p (h n) -> p h n", n=P)
                        rd = rden[:, m, 4 * g:4 * g + 4]
                        link(V.reciprocal(rd.unsqueeze(2), o[:, :, DH:DH + 1]))
                        y = xs[:, m, W + g * 256:W + (g + 1) * 256].rearrange("p (h d) -> p h d", d=DH)
                        emptied(V.tensor_tensor(y, o[:, :, 0:DH], rd.unsqueeze(2).to_broadcast([P, 4, DH]), ALU.mult))
                    wait_emptied(dve, L, f"ap{m}1")
                    V.tensor_copy(sm[:, 104:105], sm[:, 105:106]).then_inc(y_done, 1)

                def add_rows(t, k, t_next, g0):
                    for m in range(M):
                        for n in range(2):
                            wait_job(dve, L, f"{t}{n}{m}")
                            xv = x[:, m, n * W:(n + 1) * W]
                            emptied(V.tensor_tensor(xv, bank(f"{t}{n}{m}")[:, :], xv, ALU.add))
                        wait_emptied(dve, L, f"{t}1{m}")
                        if m:
                            rows_T(t_next, 0, g0)
                        scale_tile(L, k, m)
                    rows_T(t_next, 1, g0)

                add_rows("wo", 1, "t3", 8)
                for m in range(M):
                    for g in range(2):
                        wait_job(dve, L, f"sx{m}{g}")
                        mv = xmx[:, m, 2 * g:2 * g + 2]
                        link(V.tensor_reduce(mv, bank(f"sx{m}{g}")[:, :].rearrange("p (h s) -> p h s", s=T), AX, ALU.max, negate=True))
                        V.tensor_scalar(mv, mv, X_DH ** -0.5, None, ALU.mult).then_inc(xmax_done, 1)
                for m in range(M):
                    for jb in range(2):
                        wait_job(dve, L, f"pt{m}{jb}")
                        emptied(V.tensor_copy(PTx[:, 2 * m + jb, :, :], bank(f"pt{m}{jb}")[:, :].rearrange("p (h t) -> p h t", t=P)))
                wait_emptied(dve, L, "sx11")
                link(V.reciprocal(xrd[:, :, :], xden[:, :, :]))
                for m in range(M):
                    for g in range(2):
                        wait_job(dve, L, f"px{m}{g}")
                        y = xs[:, m, g * W:(g + 1) * W].rearrange("p (h d) -> p h d", d=T)
                        emptied(V.tensor_tensor(y, bank(f"px{m}{g}")[:, :].rearrange("p (h d) -> p h d", d=T),
                                                xrd[:, m, 2 * g:2 * g + 2].unsqueeze(2).to_broadcast([P, 2, T]), ALU.mult))
                add_rows("ox", 2, "t5", 24)
                wait_job(dve, L, "rl")
                emptied(V.tensor_copy(logits[:, :, :], bank("rl")[:, 0:40].rearrange("p (m n) -> p m n", m=M)))
                wait_emptied(dve, L, "rl")
                link(V.tensor_copy(pad8[:, :, 0:N_GROUPS], logits[:, :, 0:N_GROUPS]))
                for m in range(M):
                    last = V.max(top8[:, m, :], pad8[:, m, :])
                link(last)
                V.tensor_scalar(ngmx.unsqueeze(2), top8[:, :, 0:1], -1.0, None, ALU.mult).then_inc(lmax_done, 1)
                for m in range(M):
                    last = V.max_index(idx8[:, m, :].bitcast(mybir.dt.uint32), top8[:, m, :], pad8[:, m, :])
                link(last)
                link(V.tensor_copy(idxf[:, :, :], idx8[:, :, :].bitcast(mybir.dt.uint32)))
                for m in range(M):
                    last = V.tensor_scalar(oneg[:, m, :], io16[:, 0:N_GROUPS], idxf[:, m, 0:1], None, ALU.is_equal)
                link(last)
                link(V.tensor_scalar(oneg[:, :, :], oneg[:, :, :], 1.0, -NEG, ALU.subtract, ALU.mult))
                for m in range(M):
                    last = V.tensor_tensor(elog[:, m, :].rearrange("p (g e) -> p g e", e=4),
                                           logits[:, m, N_GROUPS:].rearrange("p (g e) -> p g e", e=4),
                                           oneg[:, m, :].unsqueeze(2).to_broadcast([P, N_GROUPS, 4]), ALU.add)
                link(last)
                for m in range(M):
                    last = V.max(top8[:, m, :], elog[:, m, :])
                link(last)
                dve.wait_ge(lexp_done, 2 * L + 1)
                V.tensor_tensor(e2.unsqueeze(2), top8[:, :, 1:2], top8[:, :, 0:1], ALU.subtract).then_inc(lmax_done, 1)
                for m in range(M):
                    last = V.max_index(idx8[:, m, :].bitcast(mybir.dt.uint32), top8[:, m, :], elog[:, m, :])
                link(last)
                link(V.tensor_copy(idxf[:, :, :], idx8[:, :, :].bitcast(mybir.dt.uint32)))
                for m in range(M):
                    for k in range(2):
                        last = V.tensor_scalar(one2[:, m, k, :], io16, idxf[:, m, k:k + 1], None, ALU.is_equal)
                link(last)
                V.tensor_tensor(chosen[:, :, :], one2[:, :, 0, :], one2[:, :, 1, :], ALU.add).then_inc(chosen_done, 1)
                dve.wait_ge(lexp_done, 2 * L + 2)
                link(V.tensor_scalar(sc2, e2, 1.0, None, ALU.add))
                link(V.tensor_tensor(sc2, sc2, gsum, ALU.mult))
                link(V.reciprocal(w1, sc2))
                link(V.tensor_tensor(w2, w1, e2, ALU.mult))
                wait_job(dve, L, "rank")
                bk = bank("rank")
                V.tensor_reduce(mostf, bk[:, 2 * N_EXPERTS:3 * N_EXPERTS], AX, ALU.max)
                last = V.tensor_tensor(rank[:, :, :], bk[:, 0:2 * N_EXPERTS].rearrange("p (m n) -> p m n", m=M),
                                       base16.unsqueeze(1).to_broadcast([P, M, N_EXPERTS]), ALU.add)
                emptied(last)
                wait_emptied(dve, L, "rank")
                V.tensor_copy(most, mostf)
                for k in range(2):
                    last = V.tensor_tensor(pick[:, :, k, :], one2[:, :, k, :], rank[:, :, :], ALU.mult)
                link(last)
                link(V.tensor_reduce(slotf[:, :, :], pick[:, :, :, :], AX, ALU.add))
                dve.sem_inc(flag_done, 1)

                def taken(semaphore, value):
                    dve.wait_ge(semaphore, value)
                    dve.sem_inc(slots_read, 1)

                def rows_transposed(jobs):
                    for c2 in range(2):
                        dve.wait_ge(r_jobs[L], jobs + c2 + 1)
                        V.tensor_tensor(rowsT[:, 4 * c2:4 * c2 + 4, :], banks[c2][:, :].rearrange("p (c t) -> p c t", c=4),
                                        gains[:, L, 24 + 4 * c2:28 + 4 * c2].unsqueeze(2).to_broadcast([P, 4, P]), ALU.mult).then_inc(r_rowsT[L], 1)

                def one_hot(inner):
                    for m in range(M):
                        last = V.tensor_scalar(hot1[:, m, :], columns[:, :], slotf[:, m, 0:1], None, ALU.is_equal)
                    inner.link(last)
                    for m in range(M):
                        last = V.scalar_tensor_tensor(hot[:, m, :], columns[:, :], slotf[:, m, 1:2], hot1[:, m, :], ALU.is_equal, ALU.add)
                    last.then_inc(r_hot[L], 1)

                def first_pair():
                    one_hot(Chain(dve, r_chain[L]))
                    rows_transposed(0)

                def routed(p):
                    inner = Chain(dve, r_chain[L], ROUTED_LINKS * p + 1)
                    jobs = 2 + ROUTED_JOBS * p
                    for m in range(M):
                        V.tensor_scalar(hot1[:, m, :], columns[:, :], slotf[:, m, 0:1], w1[:, m:m + 1], ALU.is_equal, ALU.mult)
                        last = V.tensor_scalar(gated[:, m, :], columns[:, :], slotf[:, m, 1:2], w2[:, m:m + 1], ALU.is_equal, ALU.mult)
                    inner.link(last)
                    V.tensor_scalar(slotf[:, :, :], slotf[:, :, :], float(P), None, ALU.subtract)
                    V.tensor_tensor(gated[:, :, :], gated[:, :, :], hot1[:, :, :], ALU.add).then_inc(r_hot[L], 1)
                    dve.wait_ge(r_hot[L], 2 * p + 2)
                    one_hot(inner)
                    taken(r_jobs[L], jobs + 1)
                    dve.wait_ge(r_gexp[L], p + 1)
                    inner.link(V.tensor_scalar(rexp, rexp, 1.0, None, ALU.add))
                    inner.link(V.reciprocal(rexp, rexp))
                    inner.link(V.tensor_tensor(rexp, banks[2][:, :], rexp, ALU.mult))
                    taken(r_jobs[L], jobs + 2)
                    V.tensor_tensor(ract, banks[3][:, :], rexp, ALU.mult).then_inc(r_act[L], 1)
                    taken(r_jobs[L], jobs + 6)
                    rows_transposed(jobs + 6)
                    for n in range(2):
                        for m in range(M):
                            dve.wait_ge(r_jobs[L], jobs + 9 + 2 * n + m)
                            xv = x[:, m, n * W:(n + 1) * W]
                            last = V.tensor_tensor(xv, banks[OUT_BANK[n][m]][:, :], xv, ALU.add)
                            last.then_inc(r_added[L], 1)
                    assert inner.n == ROUTED_LINKS

                def routed_added():
                    dve.wait_ge(r_added[L], 4 * PAIRS + 4)

                def gates_of_all():
                    start = Chain(dve, d_chain[L])
                    for m in range(M):
                        V.tensor_scalar(gates[:, m, :], one2[:, m, 0, :], w1[:, m:m + 1], None, ALU.mult)
                        last = V.tensor_scalar(one1[:, m, :], one2[:, m, 1, :], w2[:, m:m + 1], None, ALU.mult)
                    start.link(last)
                    start.link(V.tensor_tensor(gates[:, :, :], gates[:, :, :], one1[:, :, :], ALU.add))

                def dense(p):
                    inner = Chain(dve, d_chain[L], DENSE_LINKS * p + 2)
                    jobs = DENSE_JOBS * p
                    for b2 in range(2):
                        for m in range(M):
                            dve.wait_ge(d_gexp[L], 4 * p + 2 * b2 + m + 1)
                            g = gexp[:, m, :]
                            inner.link(V.tensor_scalar(g, g, 1.0, None, ALU.add))
                            inner.link(V.reciprocal(g, g))
                            inner.link(V.tensor_tensor(g, banks[m][:, :], g, ALU.mult))
                            dve.wait_ge(d_jobs[L], jobs + 10 * b2 + 2 + m + 1)
                            V.tensor_tensor(actb[:, m, :], banks[2 + m][:, :], g, ALU.mult).then_inc(d_act[L], 1)
                        for m in range(M):
                            for n in range(2):
                                dve.wait_ge(d_jobs[L], jobs + 10 * b2 + 4 + 3 * m + 1 + n + 1)
                                xv = x[:, m, n * W:(n + 1) * W]
                                gate = gates[:, m, bass.ds(2 * p + b2, 1)]
                                V.scalar_tensor_tensor(xv, banks[5 + n][:, :], gate, xv, ALU.mult, ALU.add).then_inc(d_added[L], 1)
                    for done in (12, 14, 20):
                        taken(d_jobs[L], jobs + done)
                    assert inner.n == DENSE_LINKS

                def all_added():
                    dve.wait_ge(d_added[L], 8 * PAIRS + 8)

                dve.wait_ge(flag_done, L + 1)
                either_way(dve, L, routed, dense, first_pair, routed_added, gates_of_all, all_added)
                dve.sem_inc(x_done, 1)
            dve.wait_ge(nf_loaded, 16)
            for m in range(M):
                dve.wait_ge(rstd_done, 6 * DEPTH + m + 1)
                V.scalar_tensor_tensor(xs[:, m, :], x[:, m, :], rstd[:, m:m + 1], Vx[:, 0, :], ALU.mult, ALU.mult).then_inc(fin_done, 1)


_INS = ["x", "mem", "positions", "inv", "gains", "hg_out_norm", "w_in", "w_out", "wq_x", "wkv_x", "wo_x",
        "w_router", "w_gate", "w_up", "w_down", "norm_final"]


def kernel(**inputs):
    import numpy as _np
    import concourse.bacc as _bacc
    from concourse import mybir as _mybir
    from concourse.bass_utils import run_bass_kernel_spmd as _run

    a = {k: _np.ascontiguousarray(v) for k, v in inputs.items()}
    a["x"], a["mem"], a["positions"] = a["x"].reshape(T, D), a["mem"].reshape(T, D), a["positions"].reshape(T)
    a["inv"] = _np.power(_np.float32(ROPE_THETA), -_np.arange(0, DH, 2, dtype=_np.float32) / _np.float32(DH)).astype(_np.float32)
    norms = _np.stack([a.pop("norm_mix"), a.pop("norm_cross"), a.pop("norm_mem"), a.pop("norm_ffn")])
    norms = norms.reshape(4, DEPTH, P, C).transpose(2, 1, 0, 3).reshape(P, DEPTH, 4 * C)
    bounds = a.pop("hg_lower_bounds").reshape(DEPTH, HG_HEADS, P).transpose(2, 0, 1)
    a["gains"] = _np.ascontiguousarray(_np.concatenate([norms, bounds], axis=2))
    a["w_router"] = _np.concatenate([a.pop("w_router_group"), a.pop("w_router_expert")], axis=2)
    for name in ("w_gate", "w_up", "w_down"):
        a[name] = a[name].reshape(DEPTH * N_EXPERTS, P, D * FF // P)
    nc = _bacc.Bacc("TRN2", target_bir_lowering=False, num_devices=1)
    arrays = {f"in_{n}": a[n] for n in _INS}
    args = [nc.dram_tensor(f"in_{n}", a[n].shape, _mybir.dt.from_np(a[n].dtype), kind="ExternalInput").ap() for n in _INS]
    out = nc.dram_tensor("out", (T, D), F32, kind="ExternalOutput").ap()
    trunk(nc, *args, out)
    r = _run(nc, [arrays], core_ids=[0])
    return r.results[0]["out"].reshape(1, T, D)
```
